# Optimizing a Trainium2 kernel written in Bass

```python
import jax, jax.numpy as jnp
from jax import lax
import numpy as np
import math

D_MODEL = 1024
BATCH = 1
SEQ = 256
DEPTH = 2

CHUNK = 64
N_MEM = 256
ROPE_THETA = 10000.0
LN_EPS = 1e-5

POOL_GROUPS = 4
POOL_GROUP_DIM = 128
POOL_WINDOWS = (2, 4, 8, 16)
POOL_WIDTH = POOL_GROUPS * POOL_GROUP_DIM
ATT_HEADS = 8
ATT_HEAD_DIM = 64
ATT_WIDTH = ATT_HEADS * ATT_HEAD_DIM
IDX_HEADS = 8
IDX_HEAD_DIM = 64
TOPK_MAX = 256
Q_BLOCK = 128
MEM_HEADS = 4
MEM_HEAD_DIM = 128
MEM_WIDTH = MEM_HEADS * MEM_HEAD_DIM
N_BRANCH = 3
BRANCH_WIDTH = 512
IN_WIDTHS = (POOL_WIDTH, ATT_WIDTH, ATT_WIDTH, ATT_WIDTH, IDX_HEADS * IDX_HEAD_DIM,
             IDX_HEAD_DIM, IDX_HEADS, MEM_WIDTH, N_BRANCH * D_MODEL)
D_IN = sum(IN_WIDTHS)
N_EXPERTS = 16
N_GROUPS = 4
EXPERTS_PER_GROUP = N_EXPERTS // N_GROUPS
TOP_K_EXPERTS = 2
GROUP_SCORE_TOPK = 2
D_EXPERT = 512
MOE_BLOCK = 128
DN_ALPHA = (2 * DEPTH) ** 0.25
DN_BETA = (8 * DEPTH) ** -0.25


def layer_norm(x, g, b):
    xf = x.astype(jnp.float32)
    mu = jnp.mean(xf, axis=-1, keepdims=True)
    var = jnp.mean(jnp.square(xf - mu), axis=-1, keepdims=True)
    y = (xf - mu) * lax.rsqrt(var + LN_EPS) * g.astype(jnp.float32) + b.astype(jnp.float32)
    return y.astype(x.dtype)

def rotary(x, positions):
    half = x.shape[-1] // 2
    inv_freq = ROPE_THETA ** (-jnp.arange(half, dtype=jnp.float32) / half)
    ang = positions.astype(jnp.float32)[..., None] * inv_freq
    cos = jnp.cos(ang)[:, :, None, :]
    sin = jnp.sin(ang)[:, :, None, :]
    xf = x.astype(jnp.float32)
    x1, x2 = xf[..., :half], xf[..., half:]
    out = jnp.concatenate([x1 * cos - x2 * sin, x2 * cos + x1 * sin], axis=-1)
    return out.astype(x.dtype)

def pool_branch(u, pool_w, pool_scale):
    B, S, _ = u.shape
    u = u.reshape(B, S, POOL_GROUPS, POOL_GROUP_DIM)
    t = jnp.arange(S)
    outs = []
    for g, w in enumerate(POOL_WINDOWS):
        ug = u[:, :, g].astype(jnp.float32)
        cs = jnp.cumsum(ug, axis=1)
        lagged = jnp.pad(cs, ((0, 0), (w, 0), (0, 0)))[:, :S]
        cnt = jnp.minimum(t + 1, w).astype(jnp.float32)[None, :, None]
        outs.append((cs - lagged) / cnt - ug)
    d = jnp.stack(outs, axis=2).astype(u.dtype)
    mixed = jnp.einsum('bsgc,gce->bsge', d, pool_w).reshape(B, S, POOL_WIDTH)
    return mixed * pool_scale

def dsa_branch(q, k, v, iq, ik, iw, positions):
    B, S, _ = q.shape
    q = rotary(q.reshape(B, S, ATT_HEADS, ATT_HEAD_DIM), positions)
    k = rotary(k.reshape(B, S, ATT_HEADS, ATT_HEAD_DIM), positions)
    v = v.reshape(B, S, ATT_HEADS, ATT_HEAD_DIM)
    iq = rotary(iq.reshape(B, S, IDX_HEADS, IDX_HEAD_DIM), positions)
    ik = rotary(ik[:, :, None, :], positions)[:, :, 0]
    iw = iw * (IDX_HEADS ** -0.5)
    n_sel = min(TOPK_MAX, S // 4)
    nb = S // Q_BLOCK
    key_chunk = jnp.arange(S) // CHUNK

    def to_blocks(a):
        return a.reshape(B, nb, Q_BLOCK, *a.shape[2:]).swapaxes(0, 1)

    def attend_block(args):
        blk, qb, iqb, iwb = args
        t = blk * Q_BLOCK + jnp.arange(Q_BLOCK)
        q_chunk = t // CHUNK
        admissible = key_chunk[None, :] <= q_chunk[:, None]
        rel = jax.nn.relu(jnp.einsum('bqhd,bsd->bqhs', iqb, ik) * (IDX_HEAD_DIM ** -0.5))
        score = jnp.einsum('bqhs,bqh->bqs', rel, iwb).astype(jnp.float32)
        score = jnp.where(admissible[None], score, -jnp.inf)
        _, sel = lax.top_k(score, n_sel)
        valid = (sel // CHUNK) <= q_chunk[None, :, None]
        kg = jax.vmap(lambda kk, ii: kk[ii])(k, sel)
        vg = jax.vmap(lambda vv, ii: vv[ii])(v, sel)
        s = jnp.einsum('bqhd,bqkhd->bqhk', qb, kg).astype(jnp.float32) * (ATT_HEAD_DIM ** -0.5)
        s = jnp.where(valid[:, :, None, :], s, -jnp.inf)
        p = jax.nn.softmax(s, axis=-1).astype(vg.dtype)
        return jnp.einsum('bqhk,bqkhd->bqhd', p, vg)

    out = lax.map(attend_block, (jnp.arange(nb), to_blocks(q), to_blocks(iq), to_blocks(iw)))
    return out.swapaxes(0, 1).reshape(B, S, ATT_WIDTH)

def memory_branch(mq, mem, w_mem_kv):
    B, S, _ = mq.shape
    M = mem.shape[1]
    kv = jnp.einsum('bmd,de->bme', mem, w_mem_kv)
    mk, mv = jnp.split(kv, 2, axis=-1)
    mk = mk.reshape(B, M, MEM_HEADS, MEM_HEAD_DIM)
    mv = mv.reshape(B, M, MEM_HEADS, MEM_HEAD_DIM)
    q = mq.reshape(B, S, MEM_HEADS, MEM_HEAD_DIM)
    s = jnp.einsum('bshd,bmhd->bhsm', q, mk).astype(jnp.float32) * (MEM_HEAD_DIM ** -0.5)
    p = jax.nn.softmax(s, axis=-1).astype(mv.dtype)
    return jnp.einsum('bhsm,bmhd->bshd', p, mv).reshape(B, S, MEM_WIDTH)

def token_mixing(x, mem, positions, w_in, b_in, pool_w, pool_scale, w_mem_kv, w_br, w_out):
    B, S, D = x.shape
    proj = jnp.einsum('bsd,de->bse', x, w_in) + b_in
    split_points = np.cumsum(IN_WIDTHS)[:-1].tolist()
    u_pool, q, k, v, iq, ik, iw, mq, gate_logits = jnp.split(proj, split_points, axis=-1)
    gates = jax.nn.sigmoid(gate_logits.astype(jnp.float32)).astype(x.dtype).reshape(B, S, N_BRANCH, D)
    branches = (pool_branch(u_pool, pool_w, pool_scale),
                dsa_branch(q, k, v, iq, ik, iw, positions),
                memory_branch(mq, mem, w_mem_kv))
    merged = jnp.zeros_like(x)
    for n in range(N_BRANCH):
        merged = merged + gates[:, :, n] * jnp.einsum('bsc,cd->bsd', branches[n], w_br[n])
    return jnp.einsum('bsd,de->bse', merged, w_out)

def route(x2, w_router, router_bias):
    scores = jax.nn.sigmoid(jnp.einsum('nd,de->ne', x2, w_router).astype(jnp.float32))
    biased = scores + router_bias.astype(jnp.float32)
    grouped = biased.reshape(-1, N_GROUPS, EXPERTS_PER_GROUP)
    group_score = lax.top_k(grouped, GROUP_SCORE_TOPK)[0].sum(-1)
    best = jnp.argmax(group_score, axis=-1).astype(jnp.int32)
    within = jnp.take_along_axis(grouped, best[:, None, None], axis=1)[:, 0]
    _, local = lax.top_k(within, TOP_K_EXPERTS)
    expert_idx = (best[:, None] * EXPERTS_PER_GROUP + local).astype(jnp.int32)
    w = jnp.take_along_axis(scores, expert_idx, axis=1)
    w = w / jnp.sum(w, axis=-1, keepdims=True)
    return expert_idx, w

def moe(x2, w_router, router_bias, w1, w3, w2):
    N, D = x2.shape
    expert_idx, gate_w = route(x2, w_router, router_bias)
    n_assign = N * TOP_K_EXPERTS
    n_blk = -(-n_assign // MOE_BLOCK) + N_EXPERTS
    flat_e = expert_idx.reshape(-1)
    flat_tok = jnp.repeat(jnp.arange(N, dtype=jnp.int32), TOP_K_EXPERTS)
    flat_g = gate_w.reshape(-1).astype(x2.dtype)
    order = jnp.argsort(flat_e)
    e_sorted = flat_e[order]
    counts = jax.ops.segment_sum(jnp.ones_like(flat_e), flat_e, num_segments=N_EXPERTS)
    padded = ((counts + MOE_BLOCK - 1) // MOE_BLOCK) * MOE_BLOCK
    pad_end = jnp.cumsum(padded)
    pad_start = pad_end - padded
    start = jnp.cumsum(counts) - counts
    rank = jnp.arange(n_assign, dtype=jnp.int32) - start[e_sorted]
    dest = pad_start[e_sorted] + rank
    slot_tok = jnp.full((n_blk * MOE_BLOCK,), N, jnp.int32).at[dest].set(flat_tok[order])
    slot_gate = jnp.zeros((n_blk * MOE_BLOCK,), x2.dtype).at[dest].set(flat_g[order])
    blk_e = jnp.minimum(jnp.searchsorted(pad_end, jnp.arange(n_blk) * MOE_BLOCK, side='right'),
                        N_EXPERTS - 1).astype(jnp.int32)
    x_pad = jnp.concatenate([x2, jnp.zeros((1, D), x2.dtype)], axis=0)

    def run_block(args):
        e, toks = args
        xb = x_pad[toks]
        h = jax.nn.silu(xb @ w1[e]) * (xb @ w3[e])
        return h @ w2[e]

    yb = lax.map(run_block, (blk_e, slot_tok.reshape(n_blk, MOE_BLOCK)))
    y = yb.reshape(-1, D) * slot_gate[:, None]
    return jnp.zeros((N + 1, D), x2.dtype).at[slot_tok].add(y)[:N]

def first_inputs(seed: int = 0) -> dict:
    key = jax.random.key(seed)
    ks = jax.random.split(key, 20)
    f32 = jnp.float32
    nrm = lambda k, shape, scale: jax.random.normal(k, shape, f32) * scale
    return {
        'x': nrm(ks[0], (BATCH, SEQ, D_MODEL), 1.0),
        'mem': nrm(ks[1], (BATCH, N_MEM, D_MODEL), 1.0),
        'positions': jnp.broadcast_to(jnp.arange(SEQ, dtype=jnp.int32)[None], (BATCH, SEQ)),
        'w_in': nrm(ks[2], (DEPTH, D_MODEL, D_IN), D_MODEL ** -0.5),
        'b_in': nrm(ks[3], (DEPTH, D_IN), 0.02),
        'pool_w': nrm(ks[4], (DEPTH, POOL_GROUPS, POOL_GROUP_DIM, POOL_GROUP_DIM), POOL_GROUP_DIM ** -0.5),
        'pool_scale': 1.0 + nrm(ks[5], (DEPTH, POOL_WIDTH), 0.02),
        'w_mem_kv': nrm(ks[6], (DEPTH, D_MODEL, 2 * MEM_WIDTH), D_MODEL ** -0.5),
        'w_br': nrm(ks[7], (DEPTH, N_BRANCH, BRANCH_WIDTH, D_MODEL), DN_BETA * BRANCH_WIDTH ** -0.5),
        'w_out': nrm(ks[8], (DEPTH, D_MODEL, D_MODEL), DN_BETA * D_MODEL ** -0.5),
        'ln1_g': 1.0 + nrm(ks[9], (DEPTH, D_MODEL), 0.02),
        'ln1_b': nrm(ks[10], (DEPTH, D_MODEL), 0.02),
        'w_router': nrm(ks[11], (D_MODEL, N_EXPERTS), D_MODEL ** -0.5),
        'router_bias': nrm(ks[12], (N_EXPERTS,), 0.01),
        'w1': nrm(ks[13], (DEPTH, N_EXPERTS, D_MODEL, D_EXPERT), D_MODEL ** -0.5),
        'w3': nrm(ks[14], (DEPTH, N_EXPERTS, D_MODEL, D_EXPERT), D_MODEL ** -0.5),
        'w2': nrm(ks[15], (DEPTH, N_EXPERTS, D_EXPERT, D_MODEL), DN_BETA * D_EXPERT ** -0.5),
        'ln2_g': 1.0 + nrm(ks[16], (DEPTH, D_MODEL), 0.02),
        'ln2_b': nrm(ks[17], (DEPTH, D_MODEL), 0.02),
    }

def first_block(x, mem, positions, w_in, b_in, pool_w, pool_scale, w_mem_kv, w_br, w_out,
              ln1_g, ln1_b, w_router, router_bias, w1, w3, w2, ln2_g, ln2_b):
    B, S, D = x.shape
    for l in range(DEPTH):
        mix = token_mixing(x, mem, positions, w_in[l], b_in[l], pool_w[l], pool_scale[l],
                           w_mem_kv[l], w_br[l], w_out[l])
        x = layer_norm(DN_ALPHA * x + mix, ln1_g[l], ln1_b[l])
        ffn = moe(x.reshape(B * S, D), w_router, router_bias, w1[l], w3[l], w2[l]).reshape(B, S, D)
        x = layer_norm(DN_ALPHA * x + ffn, ln2_g[l], ln2_b[l])
    return x


HEAD_DIM = 64
MIX_WIDTH = D_MODEL
N_HEADS_TOTAL = MIX_WIDTH // HEAD_DIM
SWA_HEADS = N_HEADS_TOTAL // 2
SWA_KV_HEADS = SWA_HEADS // 4
FOX_HEADS = N_HEADS_TOTAL // 4
MLSTM_HEADS = N_HEADS_TOTAL - SWA_HEADS - FOX_HEADS
SWA_Q = SWA_HEADS * HEAD_DIM
SWA_KV = SWA_KV_HEADS * HEAD_DIM
FOX_W = FOX_HEADS * HEAD_DIM
MLSTM_W = MLSTM_HEADS * HEAD_DIM
IN_WIDTH = SWA_Q + 2 * SWA_KV + 3 * FOX_W + FOX_HEADS + 4 * MLSTM_W + 2 * MLSTM_HEADS
WINDOW = 128
WIN_CHUNKS = WINDOW // CHUNK
QBLK = 128
D_FF = 4 * D_MODEL
EPS = 1e-6


def _rms(x, gain):
    xf = x.astype(jnp.float32)
    y = xf * lax.rsqrt(jnp.mean(xf * xf, axis=-1, keepdims=True) + EPS)
    return (y * gain.astype(jnp.float32)).astype(x.dtype)

def _rope(x, pos):
    half = HEAD_DIM // 2
    inv = ROPE_THETA ** (-jnp.arange(half, dtype=jnp.float32) / half)
    ang = pos.astype(jnp.float32)[:, None] * inv[None, :]
    cos = jnp.cos(ang)[None, :, None, :]
    sin = jnp.sin(ang)[None, :, None, :]
    xf = x.astype(jnp.float32)
    x1, x2 = xf[..., :half], xf[..., half:]
    return jnp.concatenate([x1 * cos - x2 * sin, x2 * cos + x1 * sin], axis=-1).astype(x.dtype)

def _split_in_proj(z):
    sizes = (SWA_Q, SWA_KV, SWA_KV, FOX_W, FOX_W, FOX_W, FOX_HEADS,
             MLSTM_W, MLSTM_W, MLSTM_W, MLSTM_HEADS, MLSTM_HEADS, MLSTM_W)
    idx = np.cumsum(sizes)[:-1].tolist()
    return jnp.split(z, idx, axis=-1)

def _swa_attention(q, k, v, sinks):
    B, S = q.shape[0], q.shape[1]
    nb = S // QBLK
    G = SWA_HEADS // SWA_KV_HEADS
    qb = q.reshape(B, nb, QBLK, SWA_KV_HEADS, G, HEAD_DIM)

    def band(t):
        tb = t.reshape(B, nb, QBLK, SWA_KV_HEADS, HEAD_DIM)
        prev = jnp.concatenate([jnp.zeros_like(tb[:, :1]), tb[:, :-1]], axis=1)
        return jnp.concatenate([prev, tb], axis=2)

    kb, vb = band(k), band(v)
    s = jnp.einsum('bnqhgd,bnkhd->bnhgqk', qb, kb).astype(jnp.float32) / math.sqrt(HEAD_DIM)
    qpos = jnp.arange(nb)[:, None] * QBLK + jnp.arange(QBLK)[None, :]
    kpos = jnp.arange(nb)[:, None] * QBLK - QBLK + jnp.arange(2 * QBLK)[None, :]
    qc = (qpos // CHUNK)[:, :, None]
    kc = (kpos // CHUNK)[:, None, :]
    allowed = (kpos[:, None, :] >= 0) & (kc <= qc) & (kc >= qc - WIN_CHUNKS)
    s = jnp.where(allowed[None, :, None, None], s, -jnp.inf)
    sink = sinks.astype(jnp.float32).reshape(SWA_KV_HEADS, G)[None, None, :, :, None, None]
    m = jnp.maximum(jnp.max(s, axis=-1, keepdims=True), sink)
    p = jnp.exp(s - m)
    p = p / (jnp.sum(p, axis=-1, keepdims=True) + jnp.exp(sink - m))
    o = jnp.einsum('bnhgqk,bnkhd->bnqhgd', p.astype(v.dtype), vb)
    return o.reshape(B, S, SWA_Q)

def _fox_attention(q, k, v, log_f):
    B, S, H, D = q.shape
    nb = S // QBLK
    FT = jnp.cumsum(log_f, axis=1).transpose(0, 2, 1)
    qb = q.reshape(B, nb, QBLK, H, D).transpose(1, 0, 2, 3, 4)
    Fb = FT.reshape(B, H, nb, QBLK).transpose(2, 0, 1, 3)
    kpos = jnp.arange(S)

    def block(args):
        qi, Fi, n = args
        s = jnp.einsum('bqhd,bkhd->bhqk', qi, k).astype(jnp.float32) / math.sqrt(D)
        s = s + Fi[..., None] - FT[:, :, None, :]
        qpos = n * QBLK + jnp.arange(QBLK)
        s = jnp.where((kpos[None, :] <= qpos[:, None])[None, None], s, -jnp.inf)
        p = jax.nn.softmax(s, axis=-1).astype(v.dtype)
        return jnp.einsum('bhqk,bkhd->bqhd', p, v)

    o = lax.map(block, (qb, Fb, jnp.arange(nb)))
    return o.transpose(1, 0, 2, 3, 4).reshape(B, S, H * D)

def _mlstm(q, k, v, i_pre, f_pre):
    B, S, H, D = q.shape
    nc, L = S // CHUNK, CHUNK

    def chunks(t):
        return t.astype(jnp.float32).reshape(B, nc, L, H, D).transpose(0, 3, 1, 2, 4)

    qc, kc, vc = chunks(q), chunks(k) / math.sqrt(D), chunks(v)
    ig = i_pre.reshape(B, nc, L, H).transpose(0, 3, 1, 2)
    lf = jax.nn.log_sigmoid(f_pre).reshape(B, nc, L, H).transpose(0, 3, 1, 2)
    b = jnp.cumsum(lf, axis=-1)
    g = b[..., -1]
    causal = jnp.tril(jnp.ones((L, L), dtype=bool))
    Dm = jnp.where(causal, b[..., :, None] - b[..., None, :] + ig[..., None, :], -jnp.inf)
    a = g[..., None] - b + ig
    a_max = jnp.max(a, axis=-1)
    wa = jnp.exp(a - a_max[..., None])
    C_loc = jnp.einsum('bhcl,bhclv,bhclk->bhcvk', wa, vc, kc)
    n_loc = jnp.einsum('bhcl,bhclk->bhck', wa, kc)

    def step(carry, inp):
        C, n, m = carry
        Cl, nl, gl, aml = inp
        m_new = jnp.maximum(gl + m, aml)
        s_old = jnp.exp(gl + m - m_new)
        s_loc = jnp.exp(aml - m_new)
        C_new = s_old[..., None, None] * C + s_loc[..., None, None] * Cl
        n_new = s_old[..., None] * n + s_loc[..., None] * nl
        return (C_new, n_new, m_new), (C, n, m)

    init = (jnp.zeros((B, H, D, D), jnp.float32), jnp.zeros((B, H, D), jnp.float32),
            jnp.zeros((B, H), jnp.float32))
    xs = (C_loc.transpose(2, 0, 1, 3, 4), n_loc.transpose(2, 0, 1, 3),
          g.transpose(2, 0, 1), a_max.transpose(2, 0, 1))
    _, (C_prev, n_prev, m_prev) = lax.scan(step, init, xs)
    C_prev = C_prev.transpose(1, 2, 0, 3, 4)
    n_prev = n_prev.transpose(1, 2, 0, 3)
    m_prev = m_prev.transpose(1, 2, 0)

    inter = b + m_prev[..., None]
    m_t = jnp.maximum(inter, jnp.max(Dm, axis=-1))
    w_inter = jnp.exp(inter - m_t)
    Sm = jnp.einsum('bhcld,bhcsd->bhcls', qc, kc) * jnp.exp(Dm - m_t[..., None])
    num = (w_inter[..., None] * jnp.einsum('bhcvk,bhclk->bhclv', C_prev, qc)
           + jnp.einsum('bhcls,bhcsv->bhclv', Sm, vc))
    den = w_inter * jnp.einsum('bhck,bhclk->bhcl', n_prev, qc) + jnp.sum(Sm, axis=-1)
    h = num / jnp.maximum(jnp.abs(den), jnp.exp(-m_t))[..., None]
    return h.transpose(0, 2, 3, 1, 4).reshape(B, S, H, D)

def _layer(x, norm1, w_in, swa_q_norm, swa_k_norm, swa_sinks, fox_q_norm, fox_k_norm,
           fox_f_bias, mlstm_i_bias, mlstm_f_bias, mlstm_out_norm, w_out, norm2, w_ff1, w_ff2):
    B, S, _ = x.shape
    h = _rms(x, norm1)
    z = h @ w_in
    (aq, ak, av, bq, bk, bv, bf, cq, ck, cv, ci, cf, co) = _split_in_proj(z)
    pos = jnp.arange(S)

    aq = _rope(_rms(aq.reshape(B, S, SWA_HEADS, HEAD_DIM), swa_q_norm), pos)
    ak = _rope(_rms(ak.reshape(B, S, SWA_KV_HEADS, HEAD_DIM), swa_k_norm), pos)
    ya = _swa_attention(aq, ak, av.reshape(B, S, SWA_KV_HEADS, HEAD_DIM), swa_sinks)

    bq = _rms(bq.reshape(B, S, FOX_HEADS, HEAD_DIM), fox_q_norm)
    bk = _rms(bk.reshape(B, S, FOX_HEADS, HEAD_DIM), fox_k_norm)
    log_f = jax.nn.log_sigmoid(bf.astype(jnp.float32) + fox_f_bias.astype(jnp.float32))
    yb = _fox_attention(bq, bk, bv.reshape(B, S, FOX_HEADS, HEAD_DIM), log_f)

    hc = _mlstm(cq.reshape(B, S, MLSTM_HEADS, HEAD_DIM), ck.reshape(B, S, MLSTM_HEADS, HEAD_DIM),
                cv.reshape(B, S, MLSTM_HEADS, HEAD_DIM),
                ci.astype(jnp.float32) + mlstm_i_bias.astype(jnp.float32),
                cf.astype(jnp.float32) + mlstm_f_bias.astype(jnp.float32))
    hc = _rms(hc, mlstm_out_norm)
    og = jax.nn.sigmoid(co.astype(jnp.float32)).reshape(B, S, MLSTM_HEADS, HEAD_DIM)
    yc = (og * hc).reshape(B, S, MLSTM_W).astype(x.dtype)

    x = x + jnp.concatenate([ya, yb, yc], axis=-1) @ w_out
    u = _rms(x, norm2) @ w_ff1
    return x + jnp.square(jax.nn.relu(u)) @ w_ff2

def second_inputs(seed: int = 0) -> dict:
    key = jax.random.key(seed)
    ks = jax.random.split(key, 17)
    f32 = jnp.float32

    def gain(k, shape):
        return 1.0 + 0.02 * jax.random.normal(k, shape, f32)

    return {
        "x": jax.random.normal(ks[0], (BATCH, SEQ, D_MODEL), f32),
        "norm1": gain(ks[1], (DEPTH, D_MODEL)),
        "w_in": jax.random.normal(ks[2], (DEPTH, D_MODEL, IN_WIDTH), f32) * D_MODEL ** -0.5,
        "swa_q_norm": gain(ks[3], (DEPTH, HEAD_DIM)),
        "swa_k_norm": gain(ks[4], (DEPTH, HEAD_DIM)),
        "swa_sinks": jax.random.normal(ks[5], (DEPTH, SWA_HEADS), f32),
        "fox_q_norm": gain(ks[6], (DEPTH, HEAD_DIM)),
        "fox_k_norm": gain(ks[7], (DEPTH, HEAD_DIM)),
        "fox_f_bias": jax.random.uniform(ks[8], (DEPTH, FOX_HEADS), f32, 2.0, 6.0),
        "mlstm_i_bias": 0.1 * jax.random.normal(ks[9], (DEPTH, MLSTM_HEADS), f32),
        "mlstm_f_bias": jax.random.uniform(ks[10], (DEPTH, MLSTM_HEADS), f32, 3.0, 6.0),
        "mlstm_out_norm": gain(ks[11], (DEPTH, MLSTM_HEADS, HEAD_DIM)),
        "w_out": jax.random.normal(ks[12], (DEPTH, MIX_WIDTH, D_MODEL), f32) * MIX_WIDTH ** -0.5,
        "norm2": gain(ks[13], (DEPTH, D_MODEL)),
        "w_ff1": jax.random.normal(ks[14], (DEPTH, D_MODEL, D_FF), f32) * D_MODEL ** -0.5,
        "w_ff2": jax.random.normal(ks[15], (DEPTH, D_FF, D_MODEL), f32) * D_FF ** -0.5,
    }

def second_block(x, norm1, w_in, swa_q_norm, swa_k_norm, swa_sinks, fox_q_norm, fox_k_norm,
              fox_f_bias, mlstm_i_bias, mlstm_f_bias, mlstm_out_norm, w_out, norm2, w_ff1, w_ff2):
    for l in range(DEPTH):
        x = _layer(x, norm1[l], w_in[l], swa_q_norm[l], swa_k_norm[l], swa_sinks[l],
                   fox_q_norm[l], fox_k_norm[l], fox_f_bias[l], mlstm_i_bias[l], mlstm_f_bias[l],
                   mlstm_out_norm[l], w_out[l], norm2[l], w_ff1[l], w_ff2[l])
    return x


def setup_inputs(seed=0):
    out = dict(first_inputs(seed))
    for name, value in second_inputs(seed + 1).items():
        if name != "x":
            out[name + "_2"] = value
    return out


def reference(
    x, mem, positions, w_in, b_in, pool_w, pool_scale, w_mem_kv, w_br, w_out, ln1_g, ln1_b,
    w_router, router_bias, w1, w3, w2, ln2_g, ln2_b, norm1_2, w_in_2, swa_q_norm_2,
    swa_k_norm_2, swa_sinks_2, fox_q_norm_2, fox_k_norm_2, fox_f_bias_2, mlstm_i_bias_2,
    mlstm_f_bias_2, mlstm_out_norm_2, w_out_2, norm2_2, w_ff1_2, w_ff2_2,
):
    x = first_block(
        x, mem, positions, w_in, b_in, pool_w, pool_scale, w_mem_kv, w_br, w_out, ln1_g, ln1_b,
        w_router, router_bias, w1, w3, w2, ln2_g, ln2_b,
    )
    return second_block(
        x, norm1_2, w_in_2, swa_q_norm_2, swa_k_norm_2, swa_sinks_2, fox_q_norm_2, fox_k_norm_2,
        fox_f_bias_2, mlstm_i_bias_2, mlstm_f_bias_2, mlstm_out_norm_2, w_out_2, norm2_2,
        w_ff1_2, w_ff2_2,
    )


_drawn_inputs = setup_inputs


def setup_inputs(seed=0):
    import zlib

    import numpy as np

    out = dict(_drawn_inputs(seed))
    spreads = {}
    factors = {'b_in': 2.811,
     'pool_scale': 5.107,
     'norm1_2': 3.345,
     'swa_q_norm_2': 8.0,
     'swa_k_norm_2': 8.0,
     'swa_sinks_2': 8.0,
     'fox_q_norm_2': 8.0,
     'fox_k_norm_2': 8.0,
     'mlstm_i_bias_2': 64.0,
     'mlstm_out_norm_2': 7.484}
    for name, (base, spread) in spreads.items():
        noise = np.random.default_rng([zlib.crc32(name.encode()), seed]).standard_normal(out[name].shape)
        drawn = base * np.exp(spread * noise) if base else spread * noise
        out[name] = __import__('jax').numpy.asarray(drawn.astype(out[name].dtype))
    for name, factor in factors.items():
        out[name] = (out[name] * factor).astype(out[name].dtype)
    return out
```

```python
import numpy as np
from contextlib import ExitStack

import concourse.bass as bass
from concourse import mybir

F32 = mybir.dt.float32
F32R = mybir.dt.float32r
I32 = mybir.dt.int32
ALU = mybir.AluOpType
ACT = mybir.ActivationFunctionType
AX = mybir.AxisListType

P = 128
S = 256
TB = S // P
D = 1024
KC = D // P
DEPTH = 2
CHUNK = 64
N_MEM = 256
BANK = 512

POOL_GROUPS = 4
POOL_WINDOWS = (2, 4, 8, 16)
HD = 64
HALF = HD // 2
DSA_HEADS = 8
DSA_TOPK = S // 4
MEM_HEADS = 4
N_BRANCH = 3
BRANCH = 512
C_POOL, C_Q, C_K, C_V, C_IQ, C_IK, C_IW, C_MQ, C_GATE = 0, 512, 1024, 1536, 2048, 2560, 2624, 2632, 3144
D_IN = C_GATE + N_BRANCH * D
N_EXPERTS, N_GROUPS, PER_GROUP, D_EXPERT = 16, 4, 4, 512
DN_ALPHA = (2 * DEPTH) ** 0.25
LN_EPS = 1e-5

SWA_HEADS, SWA_KV, FOX_HEADS, MLSTM_HEADS = 8, 2, 4, 4
C2_AQ, C2_AK, C2_AV, C2_BQ, C2_BK, C2_BV, C2_BF = 0, 512, 640, 768, 1024, 1280, 1536
C2_CQ, C2_CK, C2_CV, C2_CI, C2_CF, C2_CO = 1540, 1796, 2052, 2308, 2312, 2316
IN2 = C2_CO + MLSTM_HEADS * HD
D_FF = 4 * D
RMS_EPS = 1e-6

OUT_OF_REACH = -1e30
TAKEN = -3e38
ROPE_THETA = 10000.0

CONSTS = (
    ("ident", P), ("upto", TB * S), ("pool_band", POOL_GROUPS * TB * S), ("rope_cos", TB * HALF), ("rope_sin", TB * HALF),
    ("inv_freq", HALF), ("dsa_reach", TB * S), ("swa_reach", TB * S), ("causal", TB * S),
    ("descend", N_EXPERTS), ("ln_eps", 1), ("rms_eps", 1), ("one", 1), ("half_pi", 1),
)
CONST_AT = {}
_at = 0
for _name, _width in CONSTS:
    CONST_AT[_name] = (_at, _width)
    _at += _width
CONST_WIDTH = _at


def shape_constants():
    t = np.arange(S)
    s = (np.arange(TB)[None, :] * P + np.arange(P)[:, None])
    parts = {}
    parts["ident"] = np.eye(P)
    parts["upto"] = (s[:, :, None] <= t).astype(np.float32)
    band = np.zeros((P, POOL_GROUPS, TB, S))
    for g, w in enumerate(POOL_WINDOWS):
        inside = (s[:, :, None] <= t) & (s[:, :, None] > t - w)
        band[:, g] = inside / np.minimum(t + 1, w) - (s[:, :, None] == t)
    parts["pool_band"] = band
    inv = (np.float32(ROPE_THETA) ** (-np.arange(HALF, dtype=np.float32) / np.float32(HALF))).astype(np.float32)
    ang = (s[:, :, None].astype(np.float32) * inv).astype(np.float32).astype(np.float64)
    parts["rope_cos"], parts["rope_sin"] = np.cos(ang), np.sin(ang)
    parts["inv_freq"] = np.broadcast_to(inv, (P, HALF))
    q, k = s[:, :, None] // CHUNK, t // CHUNK
    parts["dsa_reach"] = np.where(k <= q, 0.0, OUT_OF_REACH)
    parts["swa_reach"] = np.where((k <= q) & (k >= q - 2), 0.0, OUT_OF_REACH)
    parts["causal"] = np.where(t <= s[:, :, None], 0.0, OUT_OF_REACH)
    parts["descend"] = np.broadcast_to(np.arange(N_EXPERTS, 0, -1.0), (P, N_EXPERTS))
    parts["ln_eps"] = np.full((P, 1), LN_EPS)
    parts["rms_eps"] = np.full((P, 1), RMS_EPS)
    parts["one"] = np.ones((P, 1))
    parts["half_pi"] = np.full((P, 1), np.pi / 2)
    return np.concatenate([np.asarray(parts[n], np.float32).reshape(P, w) for n, w in CONSTS], axis=1)


class Lane:

    def __init__(self, engine, sem, in_order):
        self.engine, self.sem, self.count, self.passed, self.in_order = engine, sem, 0, {}, in_order

    def after(self, *tokens):
        if self.in_order and self.count:
            tokens = (*tokens, (self.sem, self.count))
        for token in tokens:
            if token is not None and self.passed.get(token[0].name, 0) < token[1]:
                self.engine.wait_ge(token[0], token[1])
                self.passed[token[0].name] = token[1]
        return self.engine

    def done(self, instruction):
        self.count += 1
        instruction.then_inc(self.sem, 1)
        return (self.sem, self.count)


class Loads:

    def __init__(self, sem):
        self.sem, self.count = sem, 0

    def start(self, engine, dst, src):
        self.count += 16
        engine.dma_start(dst, src, allow_slow_non_contiguous=True).then_inc(self.sem, 16)
        return (self.sem, self.count)


class Banks:

    def __init__(self, banks):
        self.banks, self.free, self.at = banks, [None] * len(banks), -1

    def take(self):
        self.at = (self.at + 1) % len(self.banks)
        return self.at, self.banks[self.at], self.free[self.at]


class WeightRing:

    def __init__(self, sp, slots, sems, plan):
        self.sp, self.slots, self.plan = sp, slots, plan
        self.loads = [Loads(s) for s in sems]
        self.issued = self.taken = 0
        for _ in slots:
            self.issue(None)

    def view(self, n):
        a, b = self.plan[n].shape[1:]
        return self.slots[n % len(self.slots)][:, 0:a * b].rearrange("p (a b) -> p a b", a=a)

    def issue(self, token):
        if self.issued < len(self.plan):
            n = self.issued
            self.sp.after(token)
            self.loads[n % len(self.slots)].start(self.sp.engine, self.view(n), self.plan[n])
            self.issued += 1

    def take(self):
        n = self.taken
        self.taken += 1
        load = self.loads[n % len(self.slots)]
        return self.view(n), (load.sem, 16 * (n // len(self.slots) + 1))

    def release(self, token):
        self.issue(token)


def by_rows(ap):
    return ap.rearrange("(c p) n -> p c n", p=P)


def first_cuts():
    n = 440
    return [(a, min(a + n, C_MQ)) for a in range(0, C_MQ, n)]


def second_cuts():
    n = 432
    return [(a, min(a + n, IN2)) for a in range(0, IN2, n)]


def weight_plan(t, first_layers, second_layers):
    plan = [by_rows(t["w_mem_kv"][l, :, a:a + BANK]) for l in range(first_layers) for a in (0, BANK)]
    for l in range(first_layers):
        plan += [by_rows(t["w_in"][l, :, a:b]) for a, b in first_cuts()]
        plan.append(by_rows(t["w_in"][l, :, C_MQ:C_GATE]))
        for n in range(N_BRANCH):
            first_half, second_half = (by_rows(t["w_in"][l, :, a:a + BANK]) for a in (C_GATE + n * D, C_GATE + n * D + BANK))
            plan += [first_half, by_rows(t["w_br"][l, n]), second_half]
        plan += [by_rows(t["w_out"][l, :, a:a + BANK]) for a in (0, BANK)]
        for e in range(N_EXPERTS):
            plan += [by_rows(t["w1"][l, e]), by_rows(t["w3"][l, e]), by_rows(t["w2"][l, e])]
    for l in range(second_layers):
        plan += [by_rows(t["w_in_2"][l, :, a:b]) for a, b in second_cuts()]
        plan += [by_rows(t["w_out_2"][l, :, a:a + BANK]) for a in (0, BANK)]
        for j in range(0, D_FF, BANK):
            plan += [by_rows(t["w_ff1_2"][l, :, j:j + BANK]), by_rows(t["w_ff2_2"][l, j:j + BANK, :])]
    return plan


def build_program(nc, t, out, first_layers=DEPTH, second_layers=DEPTH):
    with ExitStack() as ctx:
        def sb(name, *shape, dt=F32):
            return ctx.enter_context(nc.sbuf_tensor(name + "_sb", [P, *shape], dt))

        def sem(name):
            return ctx.enter_context(nc.semaphore(name))

        consts = sb("consts", CONST_WIDTH)
        ring_slots = [sb(f"ring{i}", KC * BANK) for i in range(3)]
        x = sb("x", TB, D)
        xT = sb("xT", KC, S)
        z = sb("z", TB, C_MQ)
        norm_rows = sb("norm_rows", 2, D)
        mkT = sb("mkT", DEPTH, MEM_HEADS, N_MEM)
        mv = sb("mv", DEPTH, TB, BRANCH)
        mqT = sb("mqT", MEM_HEADS, S)
        turned = sb("turned", TB, 10 * HD)
        scratch = sb("scratch", TB, 10 * HD)
        qT = sb("qT", 4, S)
        kT = sb("kT", 4, S)
        iqT = sb("iqT", 4, S)
        ikT = sb("ikT", S)
        branchT = sb("branchT", N_BRANCH * 4, S)
        mergedT = sb("mergedT", KC, S)
        probs = sb("probs", 8, S)
        probsT = sb("probsT", 8, TB, P)
        hiddenT = [probs[:, 0:4, :], probs[:, 4:8, :]]
        upT = [sb(f"upT{i}", S) for i in range(2)]
        gate_row = [sb(f"gate_row{i}", S) for i in range(2)]
        small = sb("small", 512)
        bias_cols = sb("bias_cols", DEPTH, (D_IN - C_MQ) // P)
        pool_scale = sb("pool_scale", DEPTH, POOL_GROUPS)
        pool_w = sb("pool_w", DEPTH, POOL_GROUPS, P)
        router_w = sb("router_w", KC, N_EXPERTS)
        router_b = sb("router_b", N_EXPERTS)
        rms_cols = sb("rms_cols", DEPTH, 2, KC)
        head_gain = sb("head_gain", DEPTH, 4, HD)
        mlstm_gain = sb("mlstm_gain", DEPTH, MLSTM_HEADS * HD)
        sinks = sb("sinks", DEPTH, SWA_HEADS)
        gate_bias = sb("gate_bias", DEPTH, 12)
        positions = sb("positions", TB, dt=I32)
        pos_cos = sb("pos_cos", TB, HALF)
        pos_sin = sb("pos_sin", TB, HALF)

        psum = ctx.enter_context(nc.psum_tensor("psum", [P, 8, BANK], F32))

        def const(name):
            at, width = CONST_AT[name]
            return consts[:, at:at + width]

        ident = const("ident")
        upto = const("upto").rearrange("p (b t) -> p b t", b=TB)
        small_at = [0]

        def row_of(r, rows):
            return ident[0:rows, r:r + 1].to_broadcast([rows, P])

        def stat(width):
            if small_at[0] + width > 512:
                small_at[0] = 0
            small_at[0] += width
            return small[:, small_at[0] - width:small_at[0]]

        pe = Lane(nc.tensor, sem("pe_done"), False)
        vec = Lane(nc.vector, sem("vec_done"), True)
        act = Lane(nc.scalar, sem("act_done"), True)
        pool = Lane(nc.gpsimd, sem("pool_done"), True)
        sp = Lane(nc.sync, sem("sp_done"), False)
        const_loads = Loads(sem("consts_in"))
        param_loads = Loads(sem("params_in"))
        x_loads = Loads(sem("x_in"))
        mem_loads = Loads(sem("mem_in"))
        bias_loads = Loads(sem("bias_rows_in"))
        norm_loads = Loads(sem("norm_rows_in"))
        stores = Loads(sem("out_stored"))

        for b in range(TB):
            x_in = x_loads.start(nc.scalar, x[:, b, :], t["x"][0, b * P:(b + 1) * P, :])
        consts_in = const_loads.start(nc.scalar, consts[:, :], t["shape_consts"])
        memT = mergedT
        mem_rows = branchT[:, 0:8, :].rearrange("p (b c) t -> p b (c t)", b=TB)
        mem_in = mem_loads.start(nc.scalar, mem_rows, t["mem"][0].rearrange("(b p) n -> p b n", p=P))

        def param(dst, src):
            return param_loads.start(nc.gpsimd, dst, src)

        param(positions[:, :], t["positions"][0].rearrange("(b p) -> p b", p=P))
        param(router_w[:, :, :], by_rows(t["w_router"]))
        param(router_b[:, :], t["router_bias"].partition_broadcast(P))
        for l in range(DEPTH):
            param(bias_cols[:, l, :], t["b_in"][l, C_MQ:D_IN].rearrange("(c p) -> p c", p=P))
            param(pool_scale[:, l, :], t["pool_scale"][l].rearrange("(c p) -> p c", p=P))
            param(pool_w[:, l, :, :], t["pool_w"][l].rearrange("g c e -> c g e"))
            for i, name in enumerate(("norm1_2", "norm2_2")):
                param(rms_cols[:, l, i, :], t[name][l].rearrange("(c p) -> p c", p=P))
            for i, name in enumerate(("swa_q_norm_2", "swa_k_norm_2", "fox_q_norm_2", "fox_k_norm_2")):
                param(head_gain[:, l, i, :], t[name][l].partition_broadcast(P))
            param(mlstm_gain[:, l, :], t["mlstm_out_norm_2"][l].rearrange("h d -> (h d)").partition_broadcast(P))
            param(sinks[:, l, :], t["swa_sinks_2"][l].partition_broadcast(P))
            for i, name in enumerate(("fox_f_bias_2", "mlstm_f_bias_2", "mlstm_i_bias_2")):
                params_in = param(gate_bias[:, l, 4 * i:4 * i + 4], t[name][l].partition_broadcast(P))

        def load_bias_rows(l, free):
            pool.after(free)
            for b in range(TB):
                tok = bias_loads.start(nc.gpsimd, z[:, b, :], t["b_in"][l, 0:C_MQ].partition_broadcast(P))
            return tok

        def load_norm_rows(gain, shift, free):
            pool.after(free)
            norm_loads.start(nc.gpsimd, norm_rows[:, 0, :], gain.partition_broadcast(P))
            return norm_loads.start(nc.gpsimd, norm_rows[:, 1, :], shift.partition_broadcast(P))

        weights = WeightRing(sp, ring_slots, [sem(f"ring_in{i}") for i in range(len(ring_slots))],
                             weight_plan(t, first_layers, second_layers))
        banks = Banks([psum[:, 4 + i, :] for i in range(4)])
        held = psum[:, 0:4, :].rearrange("p (b h) n -> p b (h n)", b=TB)
        held_free = [None]

        def matmul(dst, lhsT, rhs, first, last):
            return pe.engine.matmul(dst, lhsT, rhs, start=first, stop=last, skip_group_check=True)

        def turn(src, width, dst, ready, copy_by, scale_col=None):
            tok = None
            for c in range(0, width // P, 2):
                n = min(2, width // P - c)
                i, bank, free = banks.take()
                pe.after(ready, free)
                for j in range(n):
                    for b in range(TB):
                        last = pe.engine.transpose(bank[:, j * S + b * P:j * S + (b + 1) * P],
                                                   src[:, b, (c + j) * P:(c + j + 1) * P], ident)
                turned_in = pe.done(last)
                if scale_col is None:
                    tok = copy_by(dst[:, c:c + n, :], bank[:, 0:n * S].rearrange("p (c t) -> p c t", c=n), turned_in)
                else:
                    for j in range(n):
                        tok = act.done(act.after(turned_in).activation(
                            dst[:, c + j, :], bank[:, j * S:(j + 1) * S], ACT.Copy, scale=scale_col[:, c + j:c + j + 1]))
                banks.free[i] = tok
            return tok

        def act_copy(dst, src, *tokens):
            return act.done(act.after(*tokens).activation(dst, src, ACT.Copy))

        def vec_copy(dst, src, *tokens):
            return vec.done(vec.after(*tokens).tensor_copy(dst, src))

        def rows_product(lhs, w, n, emit, ready, w_in):
            tok = None
            for b in range(TB):
                i, bank, free = banks.take()
                pe.after(ready, w_in, free)
                chunks = w.shape[1]
                for c in range(chunks):
                    last = matmul(bank[:, 0:n], lhs[:, c, b * P:(b + 1) * P], w[:, c, 0:n], c == 0, c == chunks - 1)
                product = pe.done(last)
                banks.free[i] = tok = emit(b, bank[:, 0:n], product)
            weights.release(product)
            return tok

        def cols_product(w, cols, rhs, rhs_width, ready, w_in):
            i, bank, free = banks.take()
            pe.after(ready, w_in, free)
            chunks = w.shape[1]
            for c in range(chunks):
                last = matmul(bank[:, 0:rhs_width], w[:, c, cols:cols + P], rhs[:, c, :], c == 0, c == chunks - 1)
            return i, bank[:, 0:rhs_width], pe.done(last)

        def softmax(scores, tops, heads, keys, sink, exp_scale):
            if sink is not None:
                vec.done(vec.after().tensor_tensor(tops, tops, sink, ALU.max))
            minus = stat(heads)
            sums = stat(heads)
            lowered = vec.done(vec.after().tensor_scalar(minus, tops, -exp_scale, None, ALU.mult))
            for h in range(heads):
                summed = act.done(act.after(lowered).activation(
                    scores[:, h, 0:keys], scores[:, h, 0:keys], ACT.Exp, bias=minus[:, h:h + 1], scale=exp_scale,
                    accum_out=sums[:, h:h + 1]))
            if sink is not None:
                extra = stat(heads)
                vec.done(vec.after().tensor_tensor(extra, sink, minus, ALU.add))
                grown = act.done(act.after((vec.sem, vec.count)).activation(extra, extra, ACT.Exp))
                vec.done(vec.after(summed, grown).tensor_tensor(sums, sums, extra, ALU.add))
            share = stat(heads)
            vec.done(vec.after(summed).reciprocal(share, sums))
            for h in range(heads):
                tok = vec.done(vec.after().tensor_scalar(
                    scores[:, h, 0:keys], scores[:, h, 0:keys], share[:, h:h + 1], None, ALU.mult))
            return tok

        def turn_probs(heads, key_blocks, ready):
            pairs = [(h, kb) for h in range(heads) for kb in range(key_blocks)]
            for n in range(0, len(pairs), 4):
                i, bank, free = banks.take()
                pe.after(ready, free)
                for j, (h, kb) in enumerate(pairs[n:n + 4]):
                    last = pe.engine.transpose(bank[:, j * P:(j + 1) * P], probs[:, h, kb * P:(kb + 1) * P], ident)
                turned_in = pe.done(last)
                hs = pairs[n][0], pairs[min(n + 4, len(pairs)) - 1][0] + 1
                tok = act_copy(probsT[:, hs[0]:hs[1], 0:key_blocks, :],
                               bank[:, 0:(hs[1] - hs[0]) * key_blocks * P].rearrange(
                                   "p (h k q) -> p h k q", k=key_blocks, q=P), turned_in)
                banks.free[i] = tok
            return tok

        def layer_norm(add_bank, ready, norm_in):
            stats = stat(TB * 2 * 6).rearrange("p (b k s) -> p b k s", b=TB, k=2)
            moments = stat(TB * 2).rearrange("p (b s) -> p b s", b=TB)
            root = stat(TB)
            for b in range(TB):
                tok = vec.done(vec.after(ready).scalar_tensor_tensor(
                    x[:, b, :], x[:, b, :], DN_ALPHA, add_bank[:, b, :], ALU.mult, ALU.add))
                held_free[0] = tok
                for k in range(2):
                    vec.done(vec.after().bn_stats(stats[:, b, k, :], x[:, b, k * BANK:(k + 1) * BANK]))
                tok = vec.done(vec.after().bn_aggr(moments[:, b, :], stats[:, b, :, :].rearrange("p k s -> p (k s)")))
            rooted = act.done(act.after(tok).activation(root, moments[:, :, 1], ACT.Sqrt, bias=const("ln_eps")))
            vec.done(vec.after(rooted).reciprocal(root, root))
            for b in range(TB):
                vec.done(vec.after().tensor_scalar(x[:, b, :], x[:, b, :], moments[:, b, 0:1], root[:, b:b + 1],
                                                   ALU.subtract, ALU.mult))
                vec.done(vec.after(norm_in).tensor_tensor(x[:, b, :], x[:, b, :], norm_rows[:, 0, :], ALU.mult))
                tok = vec.done(vec.after().tensor_tensor(x[:, b, :], x[:, b, :], norm_rows[:, 1, :], ALU.add))
            return tok

        def rope(src, dst, cos, sin, heads, tmp):
            s, d = (a.rearrange("p (h d) -> p h d", d=HD) for a in (src, dst))
            m = tmp.rearrange("p (h d) -> p h d", d=HD)
            c = cos.unsqueeze(1).to_broadcast([P, heads, HALF])
            n = sin.unsqueeze(1).to_broadcast([P, heads, HALF])
            lo, hi = slice(0, HALF), slice(HALF, HD)
            vec.done(vec.after().tensor_tensor(d[:, :, lo], s[:, :, lo], c, ALU.mult))
            vec.done(vec.after().tensor_tensor(m[:, :, lo], s[:, :, hi], n, ALU.mult))
            vec.done(vec.after().tensor_tensor(d[:, :, hi], s[:, :, hi], c, ALU.mult))
            vec.done(vec.after().tensor_tensor(m[:, :, hi], s[:, :, lo], n, ALU.mult))
            vec.done(vec.after().tensor_tensor(d[:, :, lo], d[:, :, lo], m[:, :, lo], ALU.subtract))
            return vec.done(vec.after().tensor_tensor(d[:, :, hi], d[:, :, hi], m[:, :, hi], ALU.add))

        def position_angles():
            pos, inv = stat(TB), const("inv_freq")
            work = scratch[:, 0, :]
            vec.done(vec.after(params_in, consts_in).tensor_copy(pos, positions[:, :]))
            two_pi = 2 * np.pi
            c1 = float(np.float32(6.28125))
            c2 = float(np.float32(np.float64(two_pi - c1) // 2.0 ** -21 * 2.0 ** -21))
            c3 = float(np.float32(two_pi - c1 - c2))
            for b in range(TB):
                ang, turns, k, r = (work[:, i * HALF:(i + 1) * HALF] for i in range(4))
                vec.done(vec.after().tensor_scalar(ang, inv, pos[:, b:b + 1], None, ALU.mult))
                for dst, quarter, shift in ((pos_sin, 0.0, 0.0), (pos_cos, 0.25, np.pi / 2)):
                    magic = 1.5 * 2.0 ** 23
                    vec.done(vec.after().tensor_scalar(turns, ang, 1.0 / two_pi, quarter, ALU.mult, ALU.add))
                    vec.done(vec.after().tensor_scalar(k, turns, magic, None, ALU.add))
                    vec.done(vec.after().tensor_scalar(k, k, magic, None, ALU.subtract))
                    vec.done(vec.after().scalar_tensor_tensor(r, k, -c1, ang, ALU.mult, ALU.add))
                    vec.done(vec.after().scalar_tensor_tensor(r, k, -c2, r, ALU.mult, ALU.add))
                    vec.done(vec.after().scalar_tensor_tensor(r, k, -c3, r, ALU.mult, ALU.add))
                    if shift:
                        vec.done(vec.after().tensor_scalar(r, r, float(shift), None, ALU.add))
                    vec.done(vec.after().tensor_scalar(r, r, 3.1415925, -3.1415925, ALU.min, ALU.max))
                    tok = act.done(act.after((vec.sem, vec.count)).activation(dst[:, b, :], r, ACT.Sin))
                    vec.after(tok)
            return tok

        def dsa_branch(pos_ready, z_ready):
            vec.after(pos_ready, z_ready)
            for src, dst in ((C_Q, qT), (C_K, kT), (C_IQ, iqT)):
                for b in range(TB):
                    tok = rope(z[:, b, src:src + 512], turned[:, b, 0:512], pos_cos[:, b, :], pos_sin[:, b, :], 8,
                               scratch[:, b, 0:512])
                tok = turn(turned, 512, dst, tok, act_copy)
                vec.after(tok)
            for b in range(TB):
                rope(z[:, b, C_IK:C_IK + HD], turned[:, b, 0:HD], pos_cos[:, b, :], pos_sin[:, b, :], 1,
                     scratch[:, b, 0:HD])
                tok = vec.done(vec.after().tensor_copy(turned[:, b, HD:2 * HD], turned[:, b, 0:HD]))
            heads_ready = turn(turned, 2 * HD, ikT[:, :].unsqueeze(1), tok, act_copy)
            iw = stat(TB * DSA_HEADS).rearrange("p (b h) -> p b h", b=TB)
            vec.done(vec.after().tensor_scalar(iw, z[:, :, C_IW:C_IW + DSA_HEADS], DSA_HEADS ** -0.5, None, ALU.mult))
            branch_done = None
            for b in range(TB):
                keys = (b + 1) * P
                score, left = scratch[:, 0, 0:keys], scratch[:, 1, 0:keys]
                reach = const("dsa_reach").rearrange("p (b t) -> p b t", b=TB)[:, b, 0:keys]
                for h in range(DSA_HEADS):
                    i, bank, free = banks.take()
                    at = HD * (h % 2)
                    pe.after(heads_ready, free)
                    product = pe.done(matmul(bank[:, 0:keys], iqT[at:at + HD, h // 2, b * P:(b + 1) * P],
                                             ikT[at:at + HD, 0:keys], True, True))
                    slot = turned[:, h % 4 // 2, h % 2 * keys:(h % 2 + 1) * keys]
                    used = (vec.sem, vec.count) if h >= 4 or h == 0 else None
                    related = act.done(act.after(product, used).activation(slot, bank[:, 0:keys], ACT.Relu,
                                                                           scale=HD ** -0.5))
                    banks.free[i] = related
                    vec.done(vec.after(related).scalar_tensor_tensor(
                        score, slot, iw[:, b, h:h + 1], reach if h == 0 else score, ALU.mult, ALU.add))
                top8 = stat(8)
                now, other = score, left
                for _ in range(DSA_TOPK // 8):
                    vec.done(vec.after().max(top8, now))
                    vec.done(vec.after().match_replace(other, top8, now, TAKEN))
                    now, other = other, now
                penalty = other
                vec.done(vec.after().tensor_scalar(penalty, now, TAKEN / 2, OUT_OF_REACH, ALU.is_gt, ALU.mult))
                tops = stat(DSA_HEADS)
                vec.after(branch_done)
                for h in range(DSA_HEADS):
                    i, bank, free = banks.take()
                    at = HD * (h % 2)
                    pe.after(heads_ready, free)
                    product = pe.done(matmul(bank[:, 0:keys], qT[at:at + HD, h // 2, b * P:(b + 1) * P],
                                             kT[at:at + HD, h // 2, 0:keys], True, True))
                    tok = vec.done(vec.after(product).tensor_tensor_reduce(
                        out=probs[:, h, 0:keys], in0=bank[:, 0:keys], in1=penalty, scale=1.0, scalar=TAKEN,
                        op0=ALU.add, op1=ALU.max, accum_out=tops[:, h:h + 1]))
                    banks.free[i] = tok
                ready = softmax(probs, tops, DSA_HEADS, keys, None, HD ** -0.5)
                ready = turn_probs(DSA_HEADS, b + 1, ready)
                for pair in range(DSA_HEADS // 2):
                    branch_done = head_values(pair, b + 1, lambda h, kb: z[:, kb, C_V + h * HD:C_V + (h + 1) * HD],
                                              branchT[:, 4 + pair, b * P:(b + 1) * P], ready)
            return branch_done

        def head_values(pair, key_blocks, values, dst, ready):
            i, bank, free = banks.take()
            pe.after(ready, free)
            for j in range(2):
                h = 2 * pair + j
                for kb in range(key_blocks):
                    last = matmul(bank[j * HD:(j + 1) * HD, 0:P], values(h, kb), probsT[:, h, kb, :],
                                  kb == 0, kb == key_blocks - 1)
            tok = act_copy(dst, bank[:, 0:P], pe.done(last))
            banks.free[i] = tok
            return tok

        def pool_branch(l, ready):
            band = const("pool_band").rearrange("p (g b t) -> p g b t", g=POOL_GROUPS, b=TB)
            for g in range(POOL_GROUPS):
                i, bank, free = banks.take()
                pe.after(ready, free)
                for b in range(TB):
                    last = matmul(bank[:, 0:S], z[:, b, g * P:(g + 1) * P], band[:, g, b, :], b == 0, b == TB - 1)
                differ = scratch[:, g % 2, 0:S]
                tok = vec_copy(differ, bank[:, 0:S], pe.done(last), mixed if g >= 2 else None)
                banks.free[i] = tok
                i, bank, free = banks.take()
                pe.after(tok, free)
                mixed = pe.done(matmul(bank[:, 0:S], pool_w[:, l, g, :], differ, True, True))
                banks.free[i] = tok = act.done(act.after(mixed).activation(
                    branchT[:, g, :], bank[:, 0:S], ACT.Copy, scale=pool_scale[:, l, g:g + 1]))
            vec.after(mixed)
            return tok

        def memory_kv(l, ready):
            w, w_in = weights.take()
            for h in range(MEM_HEADS):
                i, bank, product = cols_product(w, h * P, memT, N_MEM, ready, w_in)
                banks.free[i] = act_copy(mkT[:, l, h, :], bank, product)
            weights.release(product)
            w, w_in = weights.take()
            return rows_product(memT, w, BRANCH, lambda b, bank, product: act_copy(mv[:, l, b, :], bank, product),
                                ready, w_in)

        def memory_branch(l, ready):
            done = None
            for b in range(TB):
                tops = stat(MEM_HEADS)
                vec.after(done)
                for h in range(MEM_HEADS):
                    i, bank, free = banks.take()
                    pe.after(ready, free)
                    product = pe.done(matmul(bank[:, 0:N_MEM], mqT[:, h, b * P:(b + 1) * P], mkT[:, l, h, :], True, True))
                    vec.done(vec.after(product).reduce_max(tops[:, h:h + 1], bank[:, 0:N_MEM], AX.X))
                    banks.free[i] = vec_copy(probs[:, h, :], bank[:, 0:N_MEM])
                tok = softmax(probs, tops, MEM_HEADS, N_MEM, None, P ** -0.5)
                tok = turn_probs(MEM_HEADS, TB, tok)
                for h in range(MEM_HEADS):
                    i, bank, free = banks.take()
                    pe.after(tok, free)
                    for kb in range(TB):
                        last = matmul(bank[:, 0:P], mv[:, l, kb, h * P:(h + 1) * P], probsT[:, h, kb, :], kb == 0, kb == 1)
                    done = act_copy(branchT[:, 8 + h, b * P:(b + 1) * P], bank[:, 0:P], pe.done(last))
                    banks.free[i] = done
            return done

        def route(gates_w, gatesT, ready):
            E = N_EXPERTS
            scores, biased, mask, ordered, first = (stat(TB * E).rearrange("p (b e) -> p b e", b=TB) for _ in range(5))
            i, bank, free = banks.take()
            pe.after(ready, free, params_in)
            for b in range(TB):
                for c in range(KC):
                    last = matmul(bank[:, b * E:(b + 1) * E], xT[:, c, b * P:(b + 1) * P], router_w[:, c, :],
                                  c == 0, c == KC - 1)
            logits = pe.done(last)
            tok = act.done(act.after(logits).activation(scores.rearrange("p b e -> p (b e)"), bank[:, 0:TB * E], ACT.Sigmoid))
            banks.free[i] = tok
            bc = [P, TB, E]
            vec.done(vec.after(tok).tensor_tensor(biased, scores, router_b[:, :].unsqueeze(1).to_broadcast(bc), ALU.add))
            pairs = stat(TB * N_GROUPS * 6).rearrange("p (g k) -> p g k", k=6)
            grouped = biased.rearrange("p b (g k) -> p (b g) k", k=PER_GROUP)
            vec.done(vec.after().tensor_tensor(pairs[:, :, 0:3], grouped[:, :, 0:3], grouped[:, :, 1:4], ALU.add))
            vec.done(vec.after().tensor_tensor(pairs[:, :, 3:5], grouped[:, :, 0:2], grouped[:, :, 2:4], ALU.add))
            vec.done(vec.after().tensor_tensor(pairs[:, :, 5:6], grouped[:, :, 0:1], grouped[:, :, 3:4], ALU.add))
            best = stat(TB * N_GROUPS).rearrange("p (b g) -> p b g", b=TB)
            top, top_g = stat(TB), stat(TB)
            vec.done(vec.after().reduce_max(best.rearrange("p b g -> p (b g)"), pairs, AX.X))

            def first_of(values, width, hot):
                row = [P, TB, width]
                steps = const("descend")[:, E - width:E].unsqueeze(1).to_broadcast(row)
                vec.done(vec.after().reduce_max(top, values, AX.X))
                vec.done(vec.after().tensor_tensor(hot, values, top.unsqueeze(2).to_broadcast(row), ALU.is_equal))
                vec.done(vec.after().tensor_tensor(hot, hot, steps, ALU.mult))
                vec.done(vec.after().reduce_max(top_g, hot, AX.X))
                vec.done(vec.after().tensor_tensor(hot, steps, top_g.unsqueeze(2).to_broadcast(row), ALU.is_equal))

            chosen = stat(TB * N_GROUPS).rearrange("p (b g) -> p b g", b=TB)
            first_of(best, N_GROUPS, chosen)
            vec.done(vec.after().tensor_scalar(chosen, chosen, 1.0, -OUT_OF_REACH, ALU.subtract, ALU.mult))
            vec.done(vec.after().tensor_tensor(
                biased.rearrange("p b (g k) -> p (b g) k", k=PER_GROUP), grouped,
                chosen.rearrange("p b g -> p (b g)").unsqueeze(2).to_broadcast([P, TB * N_GROUPS, PER_GROUP]), ALU.add))
            first_of(biased, E, first)
            vec.done(vec.after().scalar_tensor_tensor(biased, first, TAKEN, biased, ALU.mult, ALU.add))
            first_of(biased, E, mask)
            vec.done(vec.after().tensor_tensor(mask, mask, first, ALU.add))
            vec.done(vec.after().tensor_tensor(ordered, scores, mask, ALU.mult))
            vec.done(vec.after().reduce_sum(top, ordered, AX.X))
            vec.done(vec.after().reciprocal(top, top))
            tok = vec.done(vec.after().tensor_tensor(gates_w, ordered, top.unsqueeze(2).to_broadcast(bc), ALU.mult))
            i, bank, free = banks.take()
            pe.after(tok, free)
            for b in range(TB):
                last = pe.engine.transpose(bank[0:E, b * P:(b + 1) * P], gates_w[:, b, :], ident)
            banks.free[i] = tok = vec_copy(gatesT, bank[0:E, 0:S], pe.done(last))
            return tok

        def expert_layer(l, ready):
            gates_w = stat(TB * N_EXPERTS).rearrange("p (b e) -> p b e", b=TB)
            gatesT = scratch[0:N_EXPERTS, 0, 0:S]
            routed = route(gates_w, gatesT, ready)
            read_hidden = [None, None]
            for e in range(N_EXPERTS):
                hidden, weight = hiddenT[e % 2], gate_row[e % 2]
                i, bank, free = banks.take()
                pe.after(routed, free)
                spread = pe.done(matmul(bank[:, 0:S], row_of(e, N_EXPERTS), gatesT, True, True))
                banks.free[i] = vec_copy(weight[:, :], bank[:, 0:S], spread)
                w1, w1_in = weights.take()
                w3, w3_in = weights.take()
                w2, w2_in = weights.take()
                for f in range(4):
                    ia, a, product_a = cols_product(w1, f * P, xT, S, ready, w1_in)
                    ib, g, product_b = cols_product(w3, f * P, xT, S, ready, w3_in)
                    up = upT[f % 2]
                    sig = act.done(act.after(product_a, (vec.sem, vec.count)).activation(up[:, :], a, ACT.Sigmoid))
                    banks.free[ia] = vec.done(vec.after(sig).tensor_tensor(up[:, :], up[:, :], a, ALU.mult))
                    banks.free[ib] = vec.done(vec.after(product_b).tensor_tensor(up[:, :], up[:, :], g, ALU.mult))
                    made = vec.done(vec.after(read_hidden[e % 2]).tensor_tensor(hidden[:, f, :], up[:, :], weight[:, :], ALU.mult))
                weights.release(product_a)
                weights.release(product_b)
                pe.after(made, w2_in, held_free[0] if e == 0 else None)
                for b in range(TB):
                    for half in range(2):
                        for f in range(4):
                            last = matmul(held[:, b, half * BANK:(half + 1) * BANK], hidden[:, f, b * P:(b + 1) * P],
                                          w2[:, f, half * BANK:(half + 1) * BANK], e == 0 and f == 0,
                                          e == N_EXPERTS - 1 and f == 3)
                read_hidden[e % 2] = down = pe.done(last)
                weights.release(down)
            return down

        def first_block(l, ready, pos_ready, bias_in, norm_in):
            for a, b_ in first_cuts():
                w, w_in = weights.take()
                z_ready = rows_product(xT, w, b_ - a, lambda b, bank, product: vec.done(
                    vec.after(product, bias_in).tensor_tensor(z[:, b, a:b_], bank, z[:, b, a:b_], ALU.add)),
                    ready, w_in)
            w, w_in = weights.take()
            for h in range(MEM_HEADS):
                i, bank, product = cols_product(w, h * P, xT, S, ready, w_in)
                mq_ready = act.done(act.after(product).activation(mqT[:, h, :], bank, ACT.Identity,
                                                                 bias=bias_cols[:, l, h:h + 1]))
                banks.free[i] = mq_ready
            weights.release(product)
            pool_branch(l, z_ready)
            dsa_branch(pos_ready, z_ready)
            branches = memory_branch(l, mq_ready)
            for n in range(N_BRANCH):
                for half in range(2):
                    wg, wg_in = weights.take()
                    if half == 0:
                        wb, wb_in = weights.take()
                    for c in range(4):
                        dc = half * 4 + c
                        ig, gate_bank, gate_product = cols_product(wg, c * P, xT, S, ready, wg_in)
                        ib, bank, product = cols_product(wb, dc * P, branchT[:, 4 * n:4 * n + 4, :], S, branches, wb_in)
                        gate = upT[dc % 2]
                        opened = act.done(act.after(gate_product, (vec.sem, vec.count)).activation(
                            gate[:, :], gate_bank, ACT.Sigmoid, bias=bias_cols[:, l, 4 + n * KC + dc:5 + n * KC + dc]))
                        banks.free[ig] = opened
                        target = mergedT[:, dc, :] if n == 0 else gate[:, :]
                        banks.free[ib] = merged = vec.done(vec.after(opened, product).tensor_tensor(
                            target, gate[:, :], bank, ALU.mult))
                        if n:
                            merged = vec.done(vec.after().tensor_tensor(mergedT[:, dc, :], mergedT[:, dc, :], target, ALU.add))
                    if half == 0:
                        weights.release(gate_product)
                weights.release(product)
                weights.release(product)
            for half in range(2):
                w, w_in = weights.take()
                pe.after(merged, w_in, held_free[0])
                for b in range(TB):
                    for c in range(KC):
                        last = matmul(held[:, b, half * BANK:(half + 1) * BANK], mergedT[:, c, b * P:(b + 1) * P],
                                      w[:, c, :], c == 0, c == KC - 1)
                mixed = pe.done(last)
                weights.release(mixed)
            next_bias = load_bias_rows(l + 1, mixed) if l + 1 < first_layers else None
            normed = layer_norm(held, mixed, norm_in)
            norm_in = load_norm_rows(t["ln2_g"][l], t["ln2_b"][l], normed)
            ready = turn(x, D, xT, normed, act_copy)
            down = expert_layer(l, ready)
            normed = layer_norm(held, down, norm_in)
            if l + 1 < first_layers:
                norm_in = load_norm_rows(t["ln1_g"][l + 1], t["ln1_b"][l + 1], normed)
            return normed, next_bias, norm_in

        def rms_turned(gain, ready):
            sums, root = stat(TB), stat(TB)
            normed = z[:, :, 0:D]
            for b in range(TB):
                tok = act.done(act.after(ready).activation(normed[:, b, :], x[:, b, :], ACT.Square,
                                                           accum_out=sums[:, b:b + 1]))
            tok = act.done(act.after().activation(root, sums, ACT.Sqrt, bias=const("rms_eps"), scale=1.0 / D))
            vec.done(vec.after(tok).reciprocal(root, root))
            for b in range(TB):
                tok = vec.done(vec.after().tensor_scalar(normed[:, b, :], x[:, b, :], root[:, b:b + 1], None, ALU.mult))
            tok = turn(normed, D, xT, tok, act_copy, scale_col=gain)
            vec.after(tok)
            return tok

        def head_norm(src, dst, heads, gain, scale, sq):
            s, d, m = (a.rearrange("p (h d) -> p h d", d=HD) for a in (src, dst, sq))
            sums, root = stat(heads), stat(heads)
            vec.done(vec.after().tensor_tensor(m, s, s, ALU.mult))
            tok = vec.done(vec.after().reduce_sum(sums, m, AX.X))
            tok = act.done(act.after(tok).activation(root, sums, ACT.Sqrt, bias=const("rms_eps"), scale=1.0 / HD))
            vec.done(vec.after(tok).reciprocal(root, root))
            vec.done(vec.after().tensor_tensor(d, s, root.unsqueeze(2).to_broadcast([P, heads, HD]), ALU.mult))
            g = gain if len(gain.shape) == 3 else gain.unsqueeze(1).to_broadcast([P, heads, HD])
            return vec.done(vec.after().scalar_tensor_tensor(d, d, scale, g, ALU.mult, ALU.mult))

        def swa_branch(l, z_ready):
            vec.after(z_ready)
            cos = const("rope_cos").rearrange("p (b d) -> p b d", b=TB)
            sin = const("rope_sin").rearrange("p (b d) -> p b d", b=TB)
            for b in range(TB):
                zb = z[:, b, :]
                head_norm(zb[:, C2_AQ:C2_AK], zb[:, C2_AQ:C2_AK], SWA_HEADS, head_gain[:, l, 0, :], HD ** -0.5, scratch[:, b, 0:512])
                head_norm(zb[:, C2_AK:C2_AV], zb[:, C2_AK:C2_AV], SWA_KV, head_gain[:, l, 1, :], 1.0, scratch[:, b, 512:640])
                rope(zb[:, 0:C2_AV], turned[:, b, :], cos[:, b, :], sin[:, b, :], SWA_HEADS + SWA_KV, scratch[:, b, :])
                for kv in range(SWA_KV):
                    for j in range(2):
                        at = kv * P + j * HD
                        tok = vec.done(vec.after().tensor_copy(zb[:, C2_AQ + at:C2_AQ + at + HD],
                                                               turned[:, b, 512 + kv * HD:512 + (kv + 1) * HD]))
            turn(turned, 512, qT, tok, act_copy)
            heads_ready = turn(z[:, :, C2_AQ:C2_AQ + 2 * P], 2 * P, kT[:, 0:2, :], tok, act_copy)
            reach = const("swa_reach").rearrange("p (b t) -> p b t", b=TB)
            done = None
            for b in range(TB):
                keys = (b + 1) * P
                tops = stat(SWA_HEADS)
                vec.after(done)
                for h in range(SWA_HEADS):
                    i, bank, free = banks.take()
                    at = HD * (h % 2)
                    pe.after(heads_ready, free)
                    product = pe.done(matmul(bank[:, 0:keys], qT[at:at + HD, h // 2, b * P:(b + 1) * P],
                                             kT[at:at + HD, h // 4, 0:keys], True, True))
                    banks.free[i] = vec.done(vec.after(product).tensor_tensor_reduce(
                        out=probs[:, h, 0:keys], in0=bank[:, 0:keys], in1=reach[:, b, 0:keys], scale=1.0, scalar=TAKEN,
                        op0=ALU.add, op1=ALU.max, accum_out=tops[:, h:h + 1]))
                ready = softmax(probs, tops, SWA_HEADS, keys, sinks[:, l, :], 1.0)
                ready = turn_probs(SWA_HEADS, b + 1, ready)
                for pair in range(SWA_HEADS // 2):
                    done = head_values(pair, b + 1,
                                       lambda h, kb: z[:, kb, C2_AV + (h // 4) * HD:C2_AV + (h // 4 + 1) * HD],
                                       branchT[:, pair, b * P:(b + 1) * P], ready)
            vec.after(done)
            return done

        def decays(l):
            pre, low, logs, sums, keys_add = (stat(TB * 8).rearrange("p (b h) -> p b h", b=TB) for _ in range(5))
            inp = stat(TB * 4).rearrange("p (b h) -> p b h", b=TB)

            def biased(dst, at, i):
                return vec.done(vec.after().tensor_tensor(
                    dst, z[:, :, at:at + 4], gate_bias[:, l, 4 * i:4 * i + 4].unsqueeze(1).to_broadcast([P, TB, 4]), ALU.add))

            biased(pre[:, :, 0:4], C2_BF, 0)
            biased(pre[:, :, 4:8], C2_CF, 1)
            biased(inp, C2_CI, 2)
            tok = vec.done(vec.after().scalar_tensor_tensor(low, pre, -1.0, pre, ALU.mult, ALU.max))
            act.done(act.after(tok).activation(low, low, ACT.Exp, scale=-1.0))
            tok = act.done(act.after().activation(low, low, ACT.Ln, bias=const("one")))
            tok = vec.done(vec.after(tok).scalar_tensor_tensor(logs, pre, 0.0, low, ALU.min, ALU.subtract))
            i, bank, free = banks.take()
            pe.after(tok, free)
            for b in range(TB):
                for sb_ in range(b + 1):
                    last = matmul(bank[:, b * 8:b * 8 + 8], upto[:, sb_, b * P:(b + 1) * P], logs[:, sb_, :], sb_ == 0, sb_ == b)
            banks.free[i] = vec_copy(sums.rearrange("p b h -> p (b h)"), bank[:, 0:TB * 8], pe.done(last))
            vec.done(vec.after().tensor_scalar(keys_add[:, :, 0:4], sums[:, :, 0:4], -1.0, None, ALU.mult))
            tok = vec.done(vec.after().tensor_tensor(keys_add[:, :, 4:8], inp, sums[:, :, 4:8], ALU.subtract))
            key_rows = upT[0][0:8, :]
            i, bank, free = banks.take()
            pe.after(tok, free)
            for b in range(TB):
                last = pe.engine.transpose(bank[0:8, b * P:(b + 1) * P], keys_add[:, b, :], ident)
            banks.free[i] = tok = vec_copy(key_rows, bank[0:8, 0:S], pe.done(last))
            return sums, key_rows, tok

        def fox_branch(l, sums, key_rows, rows_ready):
            for b in range(TB):
                zb = z[:, b, :]
                head_norm(zb[:, C2_BQ:C2_BK], turned[:, b, 0:256], FOX_HEADS, head_gain[:, l, 2, :], HD ** -0.5, scratch[:, b, 0:256])
                tok = head_norm(zb[:, C2_BK:C2_BV], turned[:, b, 256:512], FOX_HEADS, head_gain[:, l, 3, :], 1.0, scratch[:, b, 0:256])
            turn(turned, 256, qT[:, 0:2, :], tok, act_copy)
            heads_ready = turn(turned[:, :, 256:512], 256, kT[:, 0:2, :], tok, act_copy)
            causal = const("causal").rearrange("p (b t) -> p b t", b=TB)
            done = None
            for b in range(TB):
                keys = (b + 1) * P
                tops = stat(FOX_HEADS)
                vec.after(done)
                for h in range(FOX_HEADS):
                    i, bank, free = banks.take()
                    at = HD * (h % 2)
                    pe.after(heads_ready, rows_ready, free)
                    matmul(bank[:, 0:keys], qT[at:at + HD, h // 2, b * P:(b + 1) * P], kT[at:at + HD, h // 2, 0:keys],
                           True, False)
                    product = pe.done(matmul(bank[:, 0:keys], row_of(h, 8), key_rows[:, 0:keys], False, True))
                    banks.free[i] = vec.done(vec.after(product).scalar_tensor_tensor(
                        probs[:, h, 0:keys], bank[:, 0:keys], sums[:, b, h:h + 1], causal[:, b, 0:keys], ALU.add, ALU.add))
                vec.done(vec.after().reduce_max(tops, probs[:, 0:FOX_HEADS, 0:keys], AX.X))
                ready = softmax(probs, tops, FOX_HEADS, keys, None, 1.0)
                ready = turn_probs(FOX_HEADS, b + 1, ready)
                for pair in range(FOX_HEADS // 2):
                    done = head_values(pair, b + 1, lambda h, kb: z[:, kb, C2_BV + h * HD:C2_BV + (h + 1) * HD],
                                       branchT[:, 4 + pair, b * P:(b + 1) * P], ready)
            vec.after(done)
            return done

        def mlstm_branch(l, sums, key_rows, rows_ready, z_ready):
            turn(z[:, :, C2_CQ:C2_CK], 256, qT[:, 2:4, :], z_ready, act_copy)
            heads_ready = turn(z[:, :, C2_CK:C2_CV], 256, kT[:, 2:4, :], z_ready, act_copy)
            causal = const("causal").rearrange("p (b t) -> p b t", b=TB)
            H = MLSTM_HEADS
            for b in range(TB):
                keys = (b + 1) * P
                tops, minus, dens, floor = stat(H), stat(H), stat(H), stat(H)
                own = sums[:, b, 4:8]
                for h in range(H):
                    i, bank, free = banks.take()
                    pe.after(rows_ready, free)
                    product = pe.done(matmul(bank[:, 0:keys], row_of(4 + h, 8), key_rows[:, 0:keys], True, True))
                    banks.free[i] = vec.done(vec.after(product).scalar_tensor_tensor(
                        probs[:, h, 0:keys], bank[:, 0:keys], own[:, h:h + 1], causal[:, b, 0:keys], ALU.add, ALU.add))
                vec.done(vec.after().reduce_max(tops, probs[:, 0:H, 0:keys], AX.X))
                vec.done(vec.after().tensor_tensor(tops, tops, own, ALU.max))
                lowered = vec.done(vec.after().tensor_scalar(minus, tops, -1.0, None, ALU.mult))
                for h in range(H):
                    weighed = act.done(act.after(lowered).activation(probs[:, h, 0:keys], probs[:, h, 0:keys], ACT.Exp,
                                                                     bias=minus[:, h:h + 1]))
                floored = act.done(act.after().activation(floor, minus, ACT.Exp))
                for h in range(H):
                    i, bank, free = banks.take()
                    at = HD * (h % 2)
                    pe.after(heads_ready, free)
                    product = pe.done(matmul(bank[:, 0:keys], qT[at:at + HD, 2 + h // 2, b * P:(b + 1) * P],
                                             kT[at:at + HD, 2 + h // 2, 0:keys], True, True))
                    banks.free[i] = tok = vec.done(vec.after(product, weighed).tensor_tensor_reduce(
                        out=probs[:, h, 0:keys], in0=bank[:, 0:keys], in1=probs[:, h, 0:keys], scale=HD ** -0.5, scalar=0.0,
                        op0=ALU.mult, op1=ALU.add, accum_out=dens[:, h:h + 1]))
                ready = turn_probs(H, b + 1, tok)
                vec.done(vec.after().scalar_tensor_tensor(dens, dens, -1.0, dens, ALU.mult, ALU.max))
                vec.done(vec.after(floored).tensor_tensor(dens, dens, floor, ALU.max))
                vec.done(vec.after().reciprocal(dens, dens))
                i, bank, free = banks.take()
                pe.after(ready, free)
                for h in range(H):
                    for kb in range(b + 1):
                        last = matmul(bank[:, h * HD:(h + 1) * HD], probsT[:, h, kb, :],
                                      z[:, kb, C2_CV + h * HD:C2_CV + (h + 1) * HD], kb == 0, kb == b)
                hc = turned[:, b, 0:256]
                banks.free[i] = vec.done(vec.after(pe.done(last)).tensor_tensor(
                    hc.rearrange("p (h d) -> p h d", d=HD), bank[:, 0:256].rearrange("p (h d) -> p h d", d=HD),
                    dens.unsqueeze(2).to_broadcast([P, H, HD]), ALU.mult))
                head_norm(hc, hc, H, mlstm_gain[:, l, :].rearrange("p (h d) -> p h d", d=HD), 1.0, scratch[:, b, 0:256])
                opened = act.done(act.after(z_ready, (vec.sem, vec.count)).activation(
                    scratch[:, b, 256:512], z[:, b, C2_CO:C2_CO + 256], ACT.Sigmoid))
                tok = vec.done(vec.after(opened).tensor_tensor(hc, hc, scratch[:, b, 256:512], ALU.mult))
            return turn(turned, 256, branchT[:, 6:8, :], tok, act_copy)

        def second_block(l, x_ready):
            ready = rms_turned(rms_cols[:, l, 0, :], x_ready)
            for a, b_ in second_cuts():
                w, w_in = weights.take()
                z_ready = rows_product(xT, w, b_ - a, lambda b, bank, product: act_copy(z[:, b, a:b_], bank, product),
                                       ready, w_in)
            vec.after(z_ready)
            sums, key_rows, rows_ready = decays(l)
            swa_branch(l, z_ready)
            fox_branch(l, sums, key_rows, rows_ready)
            branches = mlstm_branch(l, sums, key_rows, rows_ready, z_ready)
            for half in range(2):
                w, w_in = weights.take()
                pe.after(branches, w_in, held_free[0])
                for b in range(TB):
                    for c in range(KC):
                        last = matmul(held[:, b, half * BANK:(half + 1) * BANK], branchT[:, c, b * P:(b + 1) * P],
                                      w[:, c, :], c == 0, c == KC - 1)
                mixed = pe.done(last)
                weights.release(mixed)
            for b in range(TB):
                tok = vec.done(vec.after(mixed).tensor_tensor(x[:, b, :], x[:, b, :], held[:, b, :], ALU.add))
            held_free[0] = tok
            ready = rms_turned(rms_cols[:, l, 1, :], tok)
            read_hidden = [None, None]
            steps = D_FF // BANK
            for j in range(steps):
                w1, w1_in = weights.take()
                hidden = hiddenT[j % 2]
                for f in range(4):
                    i, bank, product = cols_product(w1, f * P, xT, S, ready, w1_in)
                    up = upT[f % 2]
                    kept = act.done(act.after(product, (vec.sem, vec.count)).activation(up[:, :], bank, ACT.Relu))
                    banks.free[i] = kept
                    made = vec.done(vec.after(kept, read_hidden[j % 2]).tensor_tensor(hidden[:, f, :], up[:, :], up[:, :], ALU.mult))
                weights.release(product)
                w2, w2_in = weights.take()
                pe.after(made, w2_in, held_free[0] if j == 0 else None)
                for b in range(TB):
                    for half in range(2):
                        for f in range(4):
                            last = matmul(held[:, b, half * BANK:(half + 1) * BANK], hidden[:, f, b * P:(b + 1) * P],
                                          w2[:, f, half * BANK:(half + 1) * BANK], j == 0 and f == 0,
                                          j == steps - 1 and f == 3)
                read_hidden[j % 2] = down = pe.done(last)
                weights.release(down)
            for b in range(TB):
                tok = vec.done(vec.after(down).tensor_tensor(x[:, b, :], x[:, b, :], held[:, b, :], ALU.add))
            held_free[0] = tok
            return tok

        bias_in = load_bias_rows(0, None) if first_layers else None
        norm_in = load_norm_rows(t["ln1_g"][0], t["ln1_b"][0], None) if first_layers else None
        pos_ready = position_angles()
        pe.after(consts_in)
        mem_ready = turn(mem_rows, D, memT, mem_in, act_copy)
        for l in range(first_layers):
            mem_kv = memory_kv(l, mem_ready)
        x_ready = x_in
        for l in range(first_layers):
            ready = turn(x, D, xT, x_ready, act_copy)
            if l == 0:
                vec.after(mem_kv)
            x_ready, bias_in, norm_in = first_block(l, ready, pos_ready, bias_in, norm_in)
        for l in range(second_layers):
            x_ready = second_block(l, x_ready)
        sp.after(x_ready)
        for b in range(TB):
            stored = stores.start(nc.sync, out[0, b * P:(b + 1) * P, :], x[:, b, :])
        sp.after(stored)


_INPUTS = ("x", "mem", "positions", "w_in", "b_in", "pool_w", "pool_scale", "w_mem_kv", "w_br", "w_out", "ln1_g", "ln1_b",
           "w_router", "router_bias", "w1", "w3", "w2", "ln2_g", "ln2_b", "norm1_2", "w_in_2", "swa_q_norm_2",
           "swa_k_norm_2", "swa_sinks_2", "fox_q_norm_2", "fox_k_norm_2", "fox_f_bias_2", "mlstm_i_bias_2",
           "mlstm_f_bias_2", "mlstm_out_norm_2", "w_out_2", "norm2_2", "w_ff1_2", "w_ff2_2")


def kernel(**inputs):
    import concourse.bacc as bacc
    from concourse.bass_utils import run_bass_kernel_spmd

    nc = bacc.Bacc("TRN2", target_bir_lowering=False, num_devices=1)
    arrays = {f"in_{n}": np.ascontiguousarray(inputs[n]) for n in _INPUTS}
    arrays["in_shape_consts"] = shape_constants()
    t = {n[3:]: nc.dram_tensor(n, a.shape, mybir.dt.from_np(a.dtype), kind="ExternalInput").ap() for n, a in arrays.items()}
    out = nc.dram_tensor("out_0", (1, S, D), F32, kind="ExternalOutput").ap()
    build_program(nc, t, out)
    return run_bass_kernel_spmd(nc, [arrays], core_ids=[0]).results[0]["out_0"]
```

```python
import numpy as np
from contextlib import ExitStack

import concourse.bass as bass
from concourse import mybir

F32 = mybir.dt.float32
F32R = mybir.dt.float32r
I32 = mybir.dt.int32
ALU = mybir.AluOpType
ACT = mybir.ActivationFunctionType
AX = mybir.AxisListType

P = 128
S = 256
TB = S // P
D = 1024
KC = D // P
DEPTH = 2
CHUNK = 64
N_MEM = 256
BANK = 512

POOL_GROUPS = 4
POOL_WINDOWS = (2, 4, 8, 16)
HD = 64
HALF = HD // 2
DSA_HEADS = 8
DSA_TOPK = S // 4
MEM_HEADS = 4
N_BRANCH = 3
BRANCH = 512
C_POOL, C_Q, C_K, C_V, C_IQ, C_IK, C_IW, C_MQ, C_GATE = 0, 512, 1024, 1536, 2048, 2560, 2624, 2632, 3144
D_IN = C_GATE + N_BRANCH * D
N_EXPERTS, N_GROUPS, PER_GROUP, D_EXPERT = 16, 4, 4, 512
SLOTS = 64
PAIRS = N_EXPERTS // 2
DN_ALPHA = (2 * DEPTH) ** 0.25
LN_EPS = 1e-5

SWA_HEADS, SWA_KV, FOX_HEADS, MLSTM_HEADS = 8, 2, 4, 4
C2_AQ, C2_AK, C2_AV, C2_BQ, C2_BK, C2_BV, C2_BF = 0, 512, 640, 768, 1024, 1280, 1536
C2_CQ, C2_CK, C2_CV, C2_CI, C2_CF, C2_CO = 1540, 1796, 2052, 2308, 2312, 2316
IN2 = C2_CO + MLSTM_HEADS * HD
D_FF = 4 * D
RMS_EPS = 1e-6

RING = 8
REGION = TB * C_MQ + 2 * TB * 10 * HD + (N_BRANCH * 4 + 8 + 4 + 4 + 4 * 4 + 1 + KC) * S
SMALL = 1024

OUT_OF_REACH = -1e30
TAKEN = -3e38
ROPE_THETA = 10000.0

CONSTS = (
    ("ident", P), ("upto", TB * S), ("rope_cos", TB * HALF), ("rope_sin", TB * HALF),
    ("inv_freq", HALF), ("dsa_reach", TB * S), ("swa_reach", TB * S), ("causal", TB * S),
    ("descend", N_EXPERTS), ("slot", SLOTS), ("ln_eps", 1), ("rms_eps", 1), ("one", 1), ("half_pi", 1),
)
CONST_AT = {}
_at = 0
for _name, _width in CONSTS:
    CONST_AT[_name] = (_at, _width)
    _at += _width
CONST_WIDTH = _at


def token_of():
    return np.arange(TB)[None, :] * P + np.arange(P)[:, None], np.arange(S)


def pool_band():
    s, t = token_of()
    band = np.zeros((P, POOL_GROUPS, TB, S), np.float32)
    for g, w in enumerate(POOL_WINDOWS):
        inside = (s[:, :, None] <= t) & (s[:, :, None] > t - w)
        band[:, g] = inside / np.minimum(t + 1, w) - (s[:, :, None] == t)
    return band


def shape_constants():
    s, t = token_of()
    parts = {}
    parts["ident"] = np.eye(P)
    parts["upto"] = (s[:, :, None] <= t).astype(np.float32)
    inv = (np.float32(ROPE_THETA) ** (-np.arange(HALF, dtype=np.float32) / np.float32(HALF))).astype(np.float32)
    ang = (s[:, :, None].astype(np.float32) * inv).astype(np.float32).astype(np.float64)
    parts["rope_cos"], parts["rope_sin"] = np.cos(ang), np.sin(ang)
    parts["inv_freq"] = np.broadcast_to(inv, (P, HALF))
    q, k = s[:, :, None] // CHUNK, t // CHUNK
    parts["dsa_reach"] = np.where(k <= q, 0.0, OUT_OF_REACH)
    parts["swa_reach"] = np.where((k <= q) & (k >= q - 2), 0.0, OUT_OF_REACH)
    parts["causal"] = np.where(t <= s[:, :, None], 0.0, OUT_OF_REACH)
    parts["descend"] = np.broadcast_to(np.arange(N_EXPERTS, 0, -1.0), (P, N_EXPERTS))
    parts["slot"] = np.broadcast_to(np.arange(SLOTS, dtype=np.float32), (P, SLOTS))
    parts["ln_eps"] = np.full((P, 1), LN_EPS)
    parts["rms_eps"] = np.full((P, 1), RMS_EPS)
    parts["one"] = np.ones((P, 1))
    parts["half_pi"] = np.full((P, 1), np.pi / 2)
    return np.concatenate([np.asarray(parts[n], np.float32).reshape(P, w) for n, w in CONSTS], axis=1)


class Lane:

    def __init__(self, engine, sem, in_order):
        self.engine, self.sem, self.count, self.passed, self.in_order = engine, sem, 0, {}, in_order

    def after(self, *tokens):
        if self.in_order and self.count:
            tokens = (*tokens, (self.sem, self.count))
        for token in tokens:
            if token is not None and self.passed.get(token[0].name, 0) < token[1]:
                self.engine.wait_ge(token[0], token[1])
                self.passed[token[0].name] = token[1]
        return self.engine

    def done(self, instruction):
        self.count += 1
        instruction.then_inc(self.sem, 1)
        return (self.sem, self.count)


class Loads:

    def __init__(self, sem):
        self.sem, self.count = sem, 0

    def start(self, engine, dst, src):
        self.count += 16
        engine.dma_start(dst, src, allow_slow_non_contiguous=True).then_inc(self.sem, 16)
        return (self.sem, self.count)


class Banks:

    def __init__(self, banks):
        self.banks, self.free, self.at = banks, [None] * len(banks), -1

    def take(self):
        self.at = (self.at + 1) % len(self.banks)
        return self.at, self.banks[self.at], self.free[self.at]


class Piece:

    def __init__(self, raw, positions, loaded):
        self.raw, self.positions, self.loaded = raw, positions, loaded
        self.parts, self.ready = None, None


class WeightRing:

    AHEAD = 3

    def __init__(self, sp, act, vec, slots, sems, plan, rounded):
        self.sp, self.act, self.vec, self.slots, self.plan = sp, act, vec, slots, plan
        self.rounded = rounded
        self.loads = [Loads(s) for s in sems]
        self.freed, self.pieces = {}, []
        self.position = self.taken = self.prepared = 0
        self.load_ahead()

    def free(self, position):
        return position < len(self.slots) or position - len(self.slots) in self.freed

    def last_reader(self, position):
        return self.freed.get(position - len(self.slots))

    def view(self, position, shape):
        a, b = shape[1:]
        return self.slots[position % len(self.slots)][:, 0:a * b].rearrange("p (a b) -> p a b", a=a)

    def load_ahead(self):
        while len(self.pieces) < len(self.plan) and self.free(self.position):
            source, split = self.plan[len(self.pieces)]
            at = self.position
            self.sp.after(self.last_reader(at))
            raw = self.view(at, source.shape)
            loaded = self.loads[at % len(self.slots)].start(self.sp.engine, raw, source)
            self.pieces.append(Piece(raw, (at, at + 1) if split else (at,), loaded))
            self.position += 1 + split

    def prepare(self, upto):
        while self.prepared < min(upto, len(self.pieces)) and self.free(self.pieces[self.prepared].positions[-1]):
            piece = self.pieces[self.prepared]
            self.prepared += 1
            if len(piece.positions) == 1:
                piece.parts, piece.ready = [piece.raw], [piece.loaded]
                continue
            hi = self.view(piece.positions[1], piece.raw.shape)
            lo = piece.raw
            hi_in = self.act.done(self.act.after(piece.loaded, self.last_reader(piece.positions[1])).activation(
                self.rounded(hi), piece.raw, ACT.Copy))
            left = self.vec.done(self.vec.after(hi_in).tensor_tensor(self.rounded(lo), piece.raw, self.rounded(hi).bitcast(F32), ALU.subtract))
            piece.parts, piece.ready = [hi, lo], [hi_in, left]

    def take(self):
        self.prepare(self.taken + self.AHEAD)
        self.taken += 1
        assert self.prepared >= self.taken
        return self.pieces[self.taken - 1]

    def release(self, piece, token):
        for position in piece.positions:
            self.freed[position] = token
        self.load_ahead()


def by_rows(ap):
    return ap.rearrange("(c p) n -> p c n", p=P)


def first_cuts():
    n = 440
    return [(a, min(a + n, C_MQ)) for a in range(0, C_MQ, n)]


def second_cuts():
    n = 432
    return [(a, min(a + n, IN2)) for a in range(0, IN2, n)]


def halves(ap, how):
    n = ap.shape[0 if how == "rows" else 1] // 2
    return [by_rows(ap[i * n:(i + 1) * n, :] if how == "rows" else ap[:, i * n:(i + 1) * n]) for i in range(2)]


def merge_plan(t, l, n):
    plan = []
    for half in range(2):
        a = C_GATE + n * D + half * BANK
        plan += [(w, True) for w in halves(t["w_in"][l, :, a:a + BANK], "cols")]
        plan.append((by_rows(t["w_br"][l, n, :, half * BANK:(half + 1) * BANK]), False))
    return plan


def weight_plan(t, first_layers, second_layers):
    plan = []
    for l in range(first_layers):
        for a, b in first_cuts():
            plan += [(w, True) for w in halves(t["w_in"][l, :, a:b], "rows")]
        plan += [(w, False) for w in halves(t["w_mem_kv"][l, :, 0:BANK], "cols")]
        plan += [(w, False) for w in halves(t["w_mem_kv"][l, :, BANK:2 * BANK], "rows")]
        plan += merge_plan(t, l, 0)
        plan += [(w, True) for w in halves(t["w_in"][l, :, C_MQ:C_GATE], "cols")]
        plan += merge_plan(t, l, 2) + merge_plan(t, l, 1)
        for a in (0, BANK):
            plan += [(w, False) for w in halves(t["w_out"][l, :, a:a + BANK], "rows")]
        for pair in range(PAIRS + 1):
            if pair < PAIRS:
                for w in ("w1", "w3"):
                    both = [halves(t[w][l, 2 * pair + j], "rows") for j in range(2)]
                    plan += [(both[j][half], False) for half in range(2) for j in range(2)]
            if pair:
                both = [halves(t["w2"][l, 2 * pair - 2 + j], "cols") for j in range(2)]
                plan += [(both[j][half], False) for half in range(2) for j in range(2)]
    for l in range(second_layers):
        for a, b in second_cuts():
            plan += [(w, True) for w in halves(t["w_in_2"][l, :, a:b], "rows")]
        for a in (0, BANK):
            plan += [(w, False) for w in halves(t["w_out_2"][l, :, a:a + BANK], "rows")]
        for j in range(0, D_FF, BANK):
            plan += [(w, True) for w in halves(t["w_ff1_2"][l, :, j:j + BANK], "cols")]
            plan += [(w, True) for w in halves(t["w_ff2_2"][l, j:j + BANK, :], "cols")]
    return plan


def together(*works):
    works = list(works)
    while works:
        for work in list(works):
            try:
                next(work)
            except StopIteration:
                works.remove(work)


def build_program(nc, t, out, first_layers=DEPTH, second_layers=DEPTH):
    with ExitStack() as ctx:
        def sb(name, *shape, dt=F32):
            return ctx.enter_context(nc.sbuf_tensor(name + "_sb", [P, *shape], dt))

        def sem(name):
            return ctx.enter_context(nc.semaphore(name))

        rounded_face = {}

        def two_faced(name, *shape):
            width = int(np.prod(shape))
            tile = sb(name, *shape)
            rounded_face[tile.name] = nc.alloc_sbuf_tensor_at(name + "_rounded", [P, *shape], F32R,
                                                              offset=nc.sbuf_base - 4 * width)
            return tile

        def rounded(ap):
            return bass.AP(tensor=rounded_face[ap.tensor.name], offset=ap.offset, ap=ap.ap)

        def reread(ap):
            return rounded(ap).bitcast(F32)

        consts = sb("consts", CONST_WIDTH)
        slots_of_ring = [two_faced(f"ring{i}", KC * BANK // 2) for i in range(RING)]
        x = sb("x", TB, D)
        xT = [two_faced("xT_hi", KC, S), two_faced("xT_lo", KC, S)]
        mkT = sb("mkT", MEM_HEADS, N_MEM)
        mv = sb("mv", TB, BRANCH)
        upT = [sb(f"upT{i}", S) for i in range(2)]
        region = two_faced("region", REGION)
        cut = [0]

        def part(*shape, rows=P):
            width = int(np.prod(shape))
            cut[0] += width
            assert cut[0] <= REGION
            return shaped(region[0:rows, cut[0] - width:cut[0]], *shape)

        def shaped(flat, *shape):
            return flat if len(shape) == 1 else flat.rearrange(
                "p (a b) -> p a b" if len(shape) == 2 else "p (a b c) -> p a b c", **dict(zip("abc", shape)))

        z = part(TB, C_MQ)
        turned = part(TB, 10 * HD)
        scratch = part(TB, 10 * HD)
        branchT = part(N_BRANCH * 4, S)
        bias_row = region[0:1, cut[0]:cut[0] + C_MQ]
        probs = part(8, S)
        mem_probs = part(MEM_HEADS, S)
        mem_probsT = part(MEM_HEADS, S)
        band_at = cut[0]
        qT = part(4, S)
        kT = part(4, S)
        iqT = part(4, S)
        mqT = part(MEM_HEADS, S)
        ikT = part(S)
        mergedT = part(KC, S)
        mem_rows = shaped(region[:, TB * C_MQ + 4 * TB * 5 * HD:TB * C_MQ + 4 * TB * 5 * HD + TB * D], TB, D)
        memT = mergedT
        band = shaped(region[:, band_at:band_at + POOL_GROUPS * TB * S], POOL_GROUPS, TB, S)
        pool_w = shaped(region[:, band_at + POOL_GROUPS * TB * S:band_at + POOL_GROUPS * TB * S + BANK], POOL_GROUPS, P)
        norm_at = band_at + 4 * S
        norm_rows = shaped(region[:, norm_at:norm_at + 2 * D], 2, D)

        def z_probsT(h, n):
            return shaped(z[:, h // 4, C_Q + h % 4 * S:C_Q + (h % 4 + n) * S], n, S)

        cut[0] = 0
        sel = part(TB, N_EXPERTS, SLOTS)
        selT = [part(TB, P) for _ in range(2)]
        tokensT = [part(KC, 4 * SLOTS) for _ in range(2)]
        opened = [part(D_EXPERT) for _ in range(2)]
        hidden_rows = [part(D_EXPERT) for _ in range(2)]
        expertT = [part(4, P) for _ in range(2)]
        expert_out = [part(D) for _ in range(2)]
        late_w = [part(KC, P), part(KC, P), part(D)]
        late_gate = part(S)
        late_up = [part(S), part(S)]
        late_gatesT = part(S, rows=N_EXPERTS)
        late_rest = part(TB, N_EXPERTS)
        assert cut[0] <= norm_at

        cut[0] = 0
        z2 = part(TB, IN2)
        yT = part(KC, S)
        swa = dict(turned=part(TB, 10 * HD), scratch=part(TB, 10 * HD), probs=part(8, S), probsT=part(8, S),
                   qT=part(4, S), kT=part(2, S))
        fox = dict(turned=part(TB, 8 * HD), scratch=part(TB, 4 * HD), qT=part(2, S), kT=part(2, S),
                   probs=xT[0][:, 0:4, :], probsT=xT[0][:, 4:8, :])
        mls = dict(turned=part(TB, 4 * HD), scratch=part(TB, 8 * HD), qT=part(2, S), kT=part(2, S),
                   probs=xT[1][:, 0:4, :], probsT=xT[1][:, 4:8, :])
        normed_rows = shaped(region[:, 0:TB * D], TB, D)
        hiddenT = [[shaped(region[:, (2 * i + k) * 4 * S + TB * D:(2 * i + k + 1) * 4 * S + TB * D], 4, S) for k in range(2)]
                   for i in range(2)]

        small = sb("small", SMALL)
        over = sb("over", 1, dt=I32)[0:1, :]
        bias_cols = sb("bias_cols", DEPTH, (D_IN - C_MQ) // P)
        pool_scale = sb("pool_scale", DEPTH, POOL_GROUPS)
        router_w = sb("router_w", KC, N_EXPERTS)
        router_b = sb("router_b", N_EXPERTS)
        rms_cols = sb("rms_cols", DEPTH, 2, KC)
        head_gain = sb("head_gain", DEPTH, 4, HD)
        mlstm_gain = sb("mlstm_gain", DEPTH, MLSTM_HEADS * HD)
        sinks = sb("sinks", DEPTH, SWA_HEADS)
        gate_bias = sb("gate_bias", DEPTH, 12)
        positions = sb("positions", TB, dt=I32)
        pos_cos = sb("pos_cos", TB, HALF)
        pos_sin = sb("pos_sin", TB, HALF)

        psum = ctx.enter_context(nc.psum_tensor("psum", [P, 8, BANK], F32))

        def const(name):
            at, width = CONST_AT[name]
            return consts[:, at:at + width]

        ident = const("ident")
        upto = const("upto").rearrange("p (b t) -> p b t", b=TB)
        reach_of = {n: const(n).rearrange("p (b t) -> p b t", b=TB) for n in ("dsa_reach", "swa_reach", "causal")}
        small_at = [0]

        def row_of(r, rows):
            return ident[0:rows, r:r + 1].to_broadcast([rows, P])

        def stat(*shape):
            width = int(np.prod(shape))
            if small_at[0] + width > SMALL:
                small_at[0] = 0
            small_at[0] += width
            return shaped(small[:, small_at[0] - width:small_at[0]], *shape)

        pe = Lane(nc.tensor, sem("pe_done"), False)
        vec = Lane(nc.vector, sem("vec_done"), True)
        act = Lane(nc.scalar, sem("act_done"), True)
        pool = Lane(nc.gpsimd, sem("pool_done"), True)
        sp = Lane(nc.sync, sem("sp_done"), False)
        const_loads = Loads(sem("consts_in"))
        param_loads = Loads(sem("params_in"))
        x_loads = Loads(sem("x_in"))
        mem_loads = Loads(sem("mem_in"))
        bias_loads = Loads(sem("bias_row_in"))
        band_loads = Loads(sem("band_in"))
        norm_loads = Loads(sem("norm_rows_in"))
        stores = Loads(sem("out_stored"))

        for b in range(TB):
            x_in = x_loads.start(nc.sync, x[:, b, :], t["x"][0, b * P:(b + 1) * P, :])
        consts_in = const_loads.start(nc.scalar, consts[:, :], t["shape_consts"])
        banks = Banks([psum[:, 4 + i, :] for i in range(4)])
        held = psum[:, 0:4, :].rearrange("p (b h) n -> p b (h n)", b=TB)
        held_free = [None]
        weights = WeightRing(sp, act, vec, slots_of_ring, [sem(f"ring_in{i}") for i in range(RING)],
                             weight_plan(t, first_layers, second_layers), rounded)

        def param(dst, src):
            return param_loads.start(nc.gpsimd, dst, src)

        def load_layer_inputs(l, experts_done, norm_done):
            pool.after(experts_done)
            bias = bias_loads.start(nc.gpsimd, bias_row, t["b_in"][l:l + 1, 0:C_MQ])
            if l == 0:
                load_params()
            mem = mem_loads.start(nc.gpsimd, mem_rows, t["mem"][0].rearrange("(b p) n -> p b n", p=P))
            pool.after(norm_done)
            band_loads.start(nc.gpsimd, band, t["pool_band"])
            band_in = band_loads.start(nc.gpsimd, pool_w, t["pool_w"][l].rearrange("g c e -> c g e"))
            return bias, band_in, mem

        def load_params():
            param(positions[:, :], t["positions"][0].rearrange("(b p) -> p b", p=P))
            param(router_w[:, :, :], by_rows(t["w_router"]))
            param(router_b[:, :], t["router_bias"].partition_broadcast(P))
            for l in range(DEPTH):
                param(bias_cols[:, l, :], t["b_in"][l, C_MQ:D_IN].rearrange("(c p) -> p c", p=P))
                param(pool_scale[:, l, :], t["pool_scale"][l].rearrange("(c p) -> p c", p=P))
                for i, name in enumerate(("norm1_2", "norm2_2")):
                    param(rms_cols[:, l, i, :], t[name][l].rearrange("(c p) -> p c", p=P))
                for i, name in enumerate(("swa_q_norm_2", "swa_k_norm_2", "fox_q_norm_2", "fox_k_norm_2")):
                    param(head_gain[:, l, i, :], t[name][l].partition_broadcast(P))
                param(mlstm_gain[:, l, :], t["mlstm_out_norm_2"][l].rearrange("h d -> (h d)").partition_broadcast(P))
                param(sinks[:, l, :], t["swa_sinks_2"][l].partition_broadcast(P))
                for i, name in enumerate(("fox_f_bias_2", "mlstm_f_bias_2", "mlstm_i_bias_2")):
                    param(gate_bias[:, l, 4 * i:4 * i + 4], t[name][l].partition_broadcast(P))

        def load_norm_rows(gain, shift, free):
            pool.after(free)
            norm_loads.start(nc.gpsimd, norm_rows[:, 0, :], gain.partition_broadcast(P))
            return norm_loads.start(nc.gpsimd, norm_rows[:, 1, :], shift.partition_broadcast(P))

        def matmul(dst, lhsT, rhs, first, last):
            return pe.engine.matmul(dst, lhsT, rhs, start=first, stop=last, skip_group_check=True)

        def product3(dst, lhsT, rhs, first, last):
            if len(lhsT) == 2 and len(rhs) == 2:
                (a, da), (b, db) = ([rounded(p) for p in o] for o in (lhsT, rhs))
                matmul(dst, a, db, first, False)
                matmul(dst, da, b, False, False)
                return matmul(dst, a, b, False, last)
            lhsT, rhs = ([reread(p) for p in o] if len(o) == 2 else o for o in (lhsT, rhs))
            pairs = [(a, b) for a in lhsT for b in rhs]
            for n, (a, b) in enumerate(pairs):
                ins = matmul(dst, a, b, first and n == 0, last and n == len(pairs) - 1)
            return ins

        def act_copy(dst, src, *tokens):
            return act.done(act.after(*tokens).activation(dst, src, ACT.Copy))

        def vec_copy(dst, src, *tokens):
            return vec.done(vec.after(*tokens).tensor_copy(dst, src))

        def split(dst, c, src, ready):
            hi, lo = (p[:, c, :] for p in dst)
            hi_in = act.done(act.after(ready).activation(rounded(hi), src, ACT.Copy))
            return vec.done(vec.after(hi_in).tensor_tensor(rounded(lo), src, reread(hi), ALU.subtract))

        def turn(src, width, dst, ready, scale_col=None):
            for c in range(0, width // P, 2):
                n = min(2, width // P - c)
                i, bank, free = banks.take()
                pe.after(ready, free)
                for j in range(n):
                    for b in range(TB):
                        last = pe.engine.transpose(bank[:, j * S + b * P:j * S + (b + 1) * P],
                                                   src[:, b, (c + j) * P:(c + j + 1) * P], ident)
                turned_in = pe.done(last)
                if not isinstance(dst, list):
                    tok = act_copy(dst[:, c:c + n, :], bank[:, 0:n * S].rearrange("p (c t) -> p c t", c=n), turned_in)
                elif scale_col is None:
                    tok = split(dst, slice(c, c + n), bank[:, 0:n * S].rearrange("p (c t) -> p c t", c=n), turned_in)
                else:
                    for j in range(n):
                        hi_in = act.done(act.after(turned_in).activation(
                            rounded(dst[0][:, c + j, :]), bank[:, j * S:(j + 1) * S], ACT.Copy,
                            scale=scale_col[:, c + j:c + j + 1]))
                    for j in range(n):
                        tok = vec.done(vec.after(hi_in).scalar_tensor_tensor(
                            rounded(dst[1][:, c + j, :]), bank[:, j * S:(j + 1) * S], scale_col[:, c + j:c + j + 1],
                            reread(dst[0][:, c + j, :]), ALU.mult, ALU.subtract))
                banks.free[i] = tok
            return tok

        def rows_product(lhs, n, emit, ready, bias=None):
            taken = [banks.take() for _ in range(TB)]
            for half in range(2):
                piece = weights.take()
                for b, (i, bank, free) in enumerate(taken):
                    pe.after(ready, free, *piece.ready)
                    for c in range(KC // 2):
                        k = half * KC // 2 + c
                        last = product3(bank[:, 0:n], [a[:, k, b * P:(b + 1) * P] for a in lhs],
                                        [w[:, c, :] for w in piece.parts], k == 0, k == KC - 1 and bias is None)
                    if half and bias is not None:
                        last = matmul(bank[:, 0:n], upto[0:1, 0, P:S], bias, False, True)
                    if b == TB - 1:
                        done = pe.done(last)
                        weights.release(piece, done)
                    elif half:
                        first_done = pe.done(last)
                if half:
                    tok = []
                    for b, (i, bank, free) in enumerate(taken):
                        banks.free[i] = emit(b, bank[:, 0:n], (first_done, done)[b])
                        tok.append(banks.free[i])
            return tok[-1]

        def cols_product(piece, cols, rhs, ready):
            i, bank, free = banks.take()
            pe.after(ready, free, *piece.ready)
            chunks = piece.raw.shape[1]
            for c in range(chunks):
                last = product3(bank[:, 0:S], [w[:, c, cols:cols + P] for w in piece.parts], [r[:, c, :] for r in rhs],
                                c == 0, c == chunks - 1)
            return i, bank[:, 0:S], pe.done(last)

        def held_product(lhs, width, ready):
            for half in range(2):
                for part_ in range(2):
                    piece = weights.take()
                    pe.after(ready, held_free[0], *piece.ready)
                    for b in range(TB):
                        for c in range(KC // 2):
                            k = part_ * KC // 2 + c
                            last = product3(held[:, b, half * BANK:(half + 1) * BANK],
                                            [a[:, k, b * P:(b + 1) * P] for a in lhs], [w[:, c, :] for w in piece.parts],
                                            k == 0, k == KC - 1)
                    done = pe.done(last)
                    weights.release(piece, done)
            return done

        def softmax(scores, tops, heads, keys, sink, exp_scale):
            if sink is not None:
                vec.done(vec.after().tensor_tensor(tops, tops, sink, ALU.max))
            minus = stat(heads)
            sums = stat(heads)
            lowered = vec.done(vec.after().tensor_scalar(minus, tops, -exp_scale, None, ALU.mult))
            for h in range(heads):
                summed = act.done(act.after(lowered).activation(
                    scores[:, h, 0:keys], scores[:, h, 0:keys], ACT.Exp, bias=minus[:, h:h + 1], scale=exp_scale,
                    accum_out=sums[:, h:h + 1]))
            if sink is not None:
                extra = stat(heads)
                more = vec.done(vec.after().tensor_tensor(extra, sink, minus, ALU.add))
                summed = act.done(act.after(more).activation(extra, extra, ACT.Exp))
            yield
            if sink is not None:
                vec.done(vec.after(summed).tensor_tensor(sums, sums, extra, ALU.add))
            share = stat(heads)
            vec.done(vec.after(summed).reciprocal(share, sums))
            for h in range(heads):
                tok = vec.done(vec.after().tensor_scalar(
                    scores[:, h, 0:keys], scores[:, h, 0:keys], share[:, h:h + 1], None, ALU.mult))
            return tok

        def turn_probs(scores, dst, heads, key_blocks, ready):
            pairs = [(h, kb) for h in range(heads) for kb in range(key_blocks)]
            for n in range(0, len(pairs), 4):
                i, bank, free = banks.take()
                pe.after(ready, free)
                for j, (h, kb) in enumerate(pairs[n:n + 4]):
                    last = pe.engine.transpose(bank[:, j * P:(j + 1) * P], scores[:, h, kb * P:(kb + 1) * P], ident)
                turned_in = pe.done(last)
                h0, count = pairs[n][0], 4 // key_blocks
                tok = act_copy(dst(h0, count)[:, :, 0:key_blocks * P],
                               bank[:, :].rearrange("p (h k) -> p h k", h=count), turned_in)
                banks.free[i] = tok
            return tok

        def head_values(pair, key_blocks, values, turned_probs, dst, ready):
            i, bank, free = banks.take()
            pe.after(ready, free)
            for j in range(2):
                h = 2 * pair + j
                for kb in range(key_blocks):
                    last = matmul(bank[j * HD:(j + 1) * HD, 0:P], values(h, kb), turned_probs(h, 1)[:, 0, kb * P:(kb + 1) * P],
                                  kb == 0, kb == key_blocks - 1)
            tok = act_copy(dst, bank[:, 0:P], pe.done(last))
            banks.free[i] = tok
            return tok

        def layer_norm(ready, norm_in):
            stats, moments, root = stat(TB, 2, 6), stat(TB, 2), stat(TB)
            for b in range(TB):
                tok = vec.done(vec.after(ready).scalar_tensor_tensor(
                    x[:, b, :], x[:, b, :], DN_ALPHA, held[:, b, :], ALU.mult, ALU.add))
                held_free[0] = tok
                for k in range(2):
                    vec.done(vec.after().bn_stats(stats[:, b, k, :], x[:, b, k * BANK:(k + 1) * BANK]))
                tok = vec.done(vec.after().bn_aggr(moments[:, b, :], stats[:, b, :, :].rearrange("p k s -> p (k s)")))
            rooted = act.done(act.after(tok).activation(root, moments[:, :, 1], ACT.Sqrt, bias=const("ln_eps")))
            vec.done(vec.after(rooted).reciprocal(root, root))
            for b in range(TB):
                vec.done(vec.after().tensor_scalar(x[:, b, :], x[:, b, :], moments[:, b, 0:1], root[:, b:b + 1],
                                                   ALU.subtract, ALU.mult))
                vec.done(vec.after(norm_in).tensor_tensor(x[:, b, :], x[:, b, :], norm_rows[:, 0, :], ALU.mult))
                tok = vec.done(vec.after().tensor_tensor(x[:, b, :], x[:, b, :], norm_rows[:, 1, :], ALU.add))
            return tok

        def rope(src, dst, cos, sin, heads, tmp):
            s, d = (a.rearrange("p (h d) -> p h d", d=HD) for a in (src, dst))
            m = tmp.rearrange("p (h d) -> p h d", d=HD)
            c = cos.unsqueeze(1).to_broadcast([P, heads, HALF])
            n = sin.unsqueeze(1).to_broadcast([P, heads, HALF])
            lo, hi = slice(0, HALF), slice(HALF, HD)
            vec.done(vec.after().tensor_tensor(d[:, :, lo], s[:, :, lo], c, ALU.mult))
            vec.done(vec.after().tensor_tensor(m[:, :, lo], s[:, :, hi], n, ALU.mult))
            vec.done(vec.after().tensor_tensor(d[:, :, hi], s[:, :, hi], c, ALU.mult))
            vec.done(vec.after().tensor_tensor(m[:, :, hi], s[:, :, lo], n, ALU.mult))
            vec.done(vec.after().tensor_tensor(d[:, :, lo], d[:, :, lo], m[:, :, lo], ALU.subtract))
            return vec.done(vec.after().tensor_tensor(d[:, :, hi], d[:, :, hi], m[:, :, hi], ALU.add))

        def position_angles(params_in):
            pos, inv = stat(TB), const("inv_freq")
            work = scratch[:, 0, :]
            vec.done(vec.after(params_in, consts_in).tensor_copy(pos, positions[:, :]))
            two_pi = 2 * np.pi
            c1 = float(np.float32(6.28125))
            c2 = float(np.float32(np.float64(two_pi - c1) // 2.0 ** -21 * 2.0 ** -21))
            c3 = float(np.float32(two_pi - c1 - c2))
            magic = 1.5 * 2.0 ** 23
            for b in range(TB):
                ang, turns, k, r = (work[:, i * HALF:(i + 1) * HALF] for i in range(4))
                vec.done(vec.after().tensor_scalar(ang, inv, pos[:, b:b + 1], None, ALU.mult))
                for dst, quarter in ((pos_sin, 0.0), (pos_cos, 0.25)):
                    vec.done(vec.after().tensor_scalar(turns, ang, 1.0 / two_pi, quarter, ALU.mult, ALU.add))
                    vec.done(vec.after().tensor_scalar(k, turns, magic, None, ALU.add))
                    vec.done(vec.after().tensor_scalar(k, k, magic, None, ALU.subtract))
                    vec.done(vec.after().scalar_tensor_tensor(r, k, -c1, ang, ALU.mult, ALU.add))
                    vec.done(vec.after().scalar_tensor_tensor(r, k, -c2, r, ALU.mult, ALU.add))
                    vec.done(vec.after().scalar_tensor_tensor(r, k, -c3, r, ALU.mult, ALU.add))
                    if quarter:
                        vec.done(vec.after().tensor_scalar(r, r, float(np.pi / 2), None, ALU.add))
                    tok = vec.done(vec.after().tensor_scalar(r, r, 3.1415925, -3.1415925, ALU.min, ALU.max))
                    tok = act.done(act.after(tok).activation(dst[:, b, :], r, ACT.Sin))
                    vec.after(tok)
            return tok

        def dsa_branch(pos_ready, z_ready, result):
            vec.after(pos_ready, z_ready)
            for src, dst in ((C_IQ, iqT), (C_Q, qT), (C_K, kT)):
                if src == C_Q:
                    for b in range(TB):
                        rope(z[:, b, C_IK:C_IK + HD], turned[:, b, 0:HD], pos_cos[:, b, :], pos_sin[:, b, :], 1,
                             scratch[:, b, 0:HD])
                        tok = vec.done(vec.after().tensor_copy(turned[:, b, HD:2 * HD], turned[:, b, 0:HD]))
                    yield
                    tok = turn(turned, 2 * HD, ikT.unsqueeze(1), tok)
                    vec.after(tok)
                for b in range(TB):
                    tok = rope(z[:, b, src:src + 512], turned[:, b, 0:512], pos_cos[:, b, :], pos_sin[:, b, :], 8,
                               scratch[:, b, 0:512])
                yield
                heads_ready = turn(turned, 512, dst, tok)
                vec.after(heads_ready)
            iw = stat(TB, DSA_HEADS)
            vec.done(vec.after().tensor_scalar(iw, z[:, :, C_IW:C_IW + DSA_HEADS], DSA_HEADS ** -0.5, None, ALU.mult))
            done = None
            for b in range(TB):
                keys = (b + 1) * P
                now, other = scratch[:, 0, 0:keys], scratch[:, 1, 0:keys]
                reach = reach_of["dsa_reach"][:, b, 0:keys]
                related = []
                for h in range(DSA_HEADS):
                    i, bank, free = banks.take()
                    at = HD * (h % 2)
                    pe.after(heads_ready, free)
                    product = pe.done(matmul(bank[:, 0:keys], iqT[at:at + HD, h // 2, b * P:(b + 1) * P],
                                             ikT[at:at + HD, 0:keys], True, True))
                    slot = turned[:, h % 4 // 2, h % 2 * keys:(h % 2 + 1) * keys]
                    read = related[h - 4] if h >= 4 else (vec.sem, vec.count)
                    banks.free[i] = tok = act.done(act.after(product, read).activation(slot, bank[:, 0:keys], ACT.Relu,
                                                                                       scale=HD ** -0.5))
                    related.append(vec.done(vec.after(tok).scalar_tensor_tensor(
                        now, slot, iw[:, b, h:h + 1], reach if h == 0 else now, ALU.mult, ALU.add)))
                    if h % 4 == 3:
                        yield
                top8 = stat(8)
                for _ in range(DSA_TOPK // 8):
                    vec.done(vec.after().max(top8, now))
                    vec.done(vec.after().match_replace(other, top8, now, TAKEN))
                    now, other = other, now
                penalty = other
                vec.done(vec.after().tensor_scalar(penalty, now, TAKEN / 2, OUT_OF_REACH, ALU.is_gt, ALU.mult))
                yield
                tops = stat(DSA_HEADS)
                vec.after(done)
                for h in range(DSA_HEADS):
                    i, bank, free = banks.take()
                    at = HD * (h % 2)
                    pe.after(heads_ready, free)
                    product = pe.done(matmul(bank[:, 0:keys], qT[at:at + HD, h // 2, b * P:(b + 1) * P],
                                             kT[at:at + HD, h // 2, 0:keys], True, True))
                    banks.free[i] = vec.done(vec.after(product).tensor_tensor_reduce(
                        out=probs[:, h, 0:keys], in0=bank[:, 0:keys], in1=penalty, scale=1.0, scalar=TAKEN,
                        op0=ALU.add, op1=ALU.max, accum_out=tops[:, h:h + 1]))
                    if h % 4 == 3:
                        yield
                ready = yield from softmax(probs, tops, DSA_HEADS, keys, None, HD ** -0.5)
                yield
                ready = turn_probs(probs, z_probsT, DSA_HEADS, b + 1, ready)
                yield
                for pair in range(DSA_HEADS // 2):
                    done = head_values(pair, b + 1, lambda h, kb: z[:, kb, C_V + h * HD:C_V + (h + 1) * HD], z_probsT,
                                       branchT[:, 4 + pair, b * P:(b + 1) * P], ready)
                result["dsa"] = done

        def pool_branch(l, ready, band_in):
            mixed = None
            for g in range(POOL_GROUPS):
                i, bank, free = banks.take()
                pe.after(ready, band_in, free)
                for b in range(TB):
                    last = matmul(bank[:, 0:S], z[:, b, g * P:(g + 1) * P], band[:, g, b, :], b == 0, b == TB - 1)
                differ = scratch[:, g % 2, 0:S]
                banks.free[i] = tok = vec_copy(differ, bank[:, 0:S], pe.done(last))
                i, bank, free = banks.take()
                pe.after(tok, free)
                mixed = pe.done(matmul(bank[:, 0:S], pool_w[:, g, :], differ, True, True))
                banks.free[i] = tok = act.done(act.after(mixed).activation(
                    branchT[:, g, :], bank[:, 0:S], ACT.Copy, scale=pool_scale[:, l, g:g + 1]))
            vec.after(mixed)
            return tok

        def memory_branch(l, mem_ready, x_ready, result):
            for n in range(2):
                piece = weights.take()
                for j in range(2):
                    h = 2 * n + j
                    i, bank, product = cols_product(piece, j * P, [memT], mem_ready)
                    banks.free[i] = act_copy(mkT[:, h, :], bank, product)
                weights.release(piece, product)
                yield
            kv_ready = rows_product([memT], BRANCH, lambda b, bank, product: act_copy(mv[:, b, :], bank, product), mem_ready)
            vec.after(kv_ready)
            yield
            yield from merge(l, 0, result["pool"], True, result)
            for n in range(2):
                piece = weights.take()
                for j in range(2):
                    h = 2 * n + j
                    i, bank, product = cols_product(piece, j * P, xT, x_ready)
                    mq_ready = act.done(act.after(product).activation(mqT[:, h, :], bank, ACT.Identity,
                                                                     bias=bias_cols[:, l, h:h + 1]))
                    banks.free[i] = mq_ready
                weights.release(piece, product)
                yield
            done = None
            for b in range(TB):
                tops = stat(MEM_HEADS)
                vec.after(done)
                for h in range(MEM_HEADS):
                    i, bank, free = banks.take()
                    pe.after(mq_ready, kv_ready, free)
                    product = pe.done(matmul(bank[:, 0:N_MEM], mqT[:, h, b * P:(b + 1) * P], mkT[:, h, :], True, True))
                    vec.done(vec.after(product).reduce_max(tops[:, h:h + 1], bank[:, 0:N_MEM], AX.X))
                    banks.free[i] = vec_copy(mem_probs[:, h, :], bank[:, 0:N_MEM])
                yield
                tok = yield from softmax(mem_probs, tops, MEM_HEADS, N_MEM, None, P ** -0.5)
                yield
                tok = turn_probs(mem_probs, lambda h, n: mem_probsT[:, h:h + n, :], MEM_HEADS, TB, tok)
                yield
                for h in range(MEM_HEADS):
                    i, bank, free = banks.take()
                    pe.after(tok, free)
                    for kb in range(TB):
                        last = matmul(bank[:, 0:P], mv[:, kb, h * P:(h + 1) * P], mem_probsT[:, h, kb * P:(kb + 1) * P],
                                      kb == 0, kb == 1)
                    done = act_copy(branchT[:, 8 + h, b * P:(b + 1) * P], bank[:, 0:P], pe.done(last))
                    banks.free[i] = done
                yield
            yield from merge(l, 2, done, False, result)

        def merge(l, n, branch_ready, first, result):
            for half in range(2):
                gates = [weights.take() for _ in range(2)]
                projection = weights.take()
                for c in range(4):
                    dc = half * 4 + c
                    ig, gate_bank, gate_product = cols_product(gates[c // 2], c % 2 * P, xT, result["xT"])
                    if c % 2:
                        weights.release(gates[c // 2], gate_product)
                    ib, bank, product = cols_product(projection, c * P, [branchT[:, 4 * n:4 * n + 4, :]], branch_ready)
                    gate = upT[dc % 2]
                    opened_in = act.done(act.after(gate_product, result["upT"][dc % 2]).activation(
                        gate[:, :], gate_bank, ACT.Sigmoid, bias=bias_cols[:, l, 4 + n * KC + dc:5 + n * KC + dc]))
                    banks.free[ig] = opened_in
                    target = mergedT[:, dc, :] if first else gate[:, :]
                    banks.free[ib] = merged = vec.done(vec.after(opened_in, product).tensor_tensor(
                        target, gate[:, :], bank, ALU.mult))
                    if not first:
                        merged = vec.done(vec.after().tensor_tensor(mergedT[:, dc, :], mergedT[:, dc, :], target, ALU.add))
                    result["upT"][dc % 2] = merged
                    if c < 3:
                        yield
                weights.release(projection, product)
                yield
            result["merged"] = merged

        def route(gates_w, slots, ready):
            E = N_EXPERTS
            scores, biased, mask, ordered, first = (stat(TB, E) for _ in range(5))
            i, bank, free = banks.take()
            pe.after(ready, free, result_params[0])
            for b in range(TB):
                for c in range(KC):
                    last = product3(bank[:, b * E:(b + 1) * E], [a[:, c, b * P:(b + 1) * P] for a in xT],
                                    [router_w[:, c, :]], c == 0, c == KC - 1)
            logits = pe.done(last)
            tok = act.done(act.after(logits).activation(scores.rearrange("p b e -> p (b e)"), bank[:, 0:TB * E], ACT.Sigmoid))
            banks.free[i] = tok
            bc = [P, TB, E]
            vec.done(vec.after(tok).tensor_tensor(biased, scores, router_b[:, :].unsqueeze(1).to_broadcast(bc), ALU.add))
            pairs = stat(TB * N_GROUPS, 6)
            grouped = biased.rearrange("p b (g k) -> p (b g) k", k=PER_GROUP)
            vec.done(vec.after().tensor_tensor(pairs[:, :, 0:3], grouped[:, :, 0:3], grouped[:, :, 1:4], ALU.add))
            vec.done(vec.after().tensor_tensor(pairs[:, :, 3:5], grouped[:, :, 0:2], grouped[:, :, 2:4], ALU.add))
            vec.done(vec.after().tensor_tensor(pairs[:, :, 5:6], grouped[:, :, 0:1], grouped[:, :, 3:4], ALU.add))
            best = stat(TB, N_GROUPS)
            top, top_g = stat(TB), stat(TB)
            vec.done(vec.after().reduce_max(best.rearrange("p b g -> p (b g)"), pairs, AX.X))

            def first_of(values, width, hot):
                row = [P, TB, width]
                steps = const("descend")[:, E - width:E].unsqueeze(1).to_broadcast(row)
                vec.done(vec.after().reduce_max(top, values, AX.X))
                vec.done(vec.after().tensor_tensor(hot, values, top.unsqueeze(2).to_broadcast(row), ALU.is_equal))
                vec.done(vec.after().tensor_tensor(hot, hot, steps, ALU.mult))
                vec.done(vec.after().reduce_max(top_g, hot, AX.X))
                vec.done(vec.after().tensor_tensor(hot, steps, top_g.unsqueeze(2).to_broadcast(row), ALU.is_equal))

            chosen = stat(TB, N_GROUPS)
            first_of(best, N_GROUPS, chosen)
            vec.done(vec.after().tensor_scalar(chosen, chosen, 1.0, -OUT_OF_REACH, ALU.subtract, ALU.mult))
            vec.done(vec.after().tensor_tensor(
                grouped, grouped, chosen.rearrange("p b g -> p (b g)").unsqueeze(2).to_broadcast([P, TB * N_GROUPS, PER_GROUP]),
                ALU.add))
            first_of(biased, E, first)
            vec.done(vec.after().scalar_tensor_tensor(biased, first, TAKEN, biased, ALU.mult, ALU.add))
            first_of(biased, E, mask)
            tok = vec.done(vec.after().tensor_tensor(mask, mask, first, ALU.add))
            i, bank, free = banks.take()
            pe.after(tok, free)
            for b in range(TB):
                for sb_ in range(b + 1):
                    last = matmul(bank[:, b * E:(b + 1) * E], upto[:, sb_, b * P:(b + 1) * P], mask[:, sb_, :], sb_ == 0, sb_ == b)
            counted = pe.done(last)
            vec.done(vec.after().tensor_tensor(ordered, scores, mask, ALU.mult))
            vec.done(vec.after().reduce_sum(top, ordered, AX.X))
            vec.done(vec.after().reciprocal(top, top))
            vec.done(vec.after().tensor_tensor(gates_w, ordered, top.unsqueeze(2).to_broadcast(bc), ALU.mult))
            banks.free[i] = vec.done(vec.after(counted).tensor_tensor(
                slots, bank[:, 0:TB * E].rearrange("p (b e) -> p b e", b=TB), mask, ALU.mult))
            return vec.done(vec.after().tensor_scalar(slots, slots, -1.0, None, ALU.add))

        def expert_layer(l, ready):
            E = N_EXPERTS
            gates_w, slots = routed[:, 0, :, :], routed[:, 1, :, :]
            tok = route(gates_w, slots, ready)
            for b in range(TB):
                tok = vec.done(vec.after(tok).tensor_tensor(
                    sel[:, b, :, :], const("slot").unsqueeze(1).to_broadcast([P, E, SLOTS]),
                    slots[:, b, :].unsqueeze(2).to_broadcast([P, E, SLOTS]), ALU.is_equal))
            selected = tok
            flat = sel.rearrange("p b e s -> p b (e s)")

            def dispatch(quarter):
                dst = tokensT[quarter % 2]
                for c in range(0, KC, 2):
                    i, bank, free = banks.take()
                    pe.after(ready, selected, free)
                    for j in range(2):
                        for b in range(TB):
                            last = matmul(bank[:, j * S:(j + 1) * S], x[:, b, (c + j) * P:(c + j + 1) * P],
                                          flat[:, b, quarter * S:(quarter + 1) * S], b == 0, b == TB - 1)
                    banks.free[i] = tok = act_copy(dst[:, c:c + 2, :], bank[:, :].rearrange("p (c t) -> p c t", c=2),
                                                   pe.done(last))
                return tok

            def up(pair, src, src_in):
                projected = []
                for _ in ("w1", "w3"):
                    i, bank, free = banks.take()
                    for half in range(2):
                        taken = [weights.take() for _ in range(2)]
                        pe.after(free, src_in, *taken[0].ready, *taken[1].ready)
                        for c in range(KC // 2):
                            for j in range(2):
                                at, k = (2 * (pair % 2) + j) * SLOTS, half * KC // 2 + c
                                last = matmul(bank[j * SLOTS:(j + 1) * SLOTS, :], src[:, k, at:at + SLOTS],
                                              taken[j].raw[:, c, :], k == 0, k == KC - 1)
                        product = pe.done(last)
                        for piece in taken:
                            weights.release(piece, product)
                    projected.append((i, bank, product))
                (ia, a, a_in), (ib, g, g_in) = projected
                sig, rows = opened[pair % 2], hidden_rows[pair % 2]
                tok = act.done(act.after(a_in, read_sig[pair % 2]).activation(sig, a, ACT.Sigmoid))
                banks.free[ia] = read_sig[pair % 2] = vec.done(vec.after(tok).tensor_tensor(rows, sig, a, ALU.mult))
                banks.free[ib] = tok = vec.done(vec.after(g_in).tensor_tensor(rows, rows, g, ALU.mult))
                return tok

            def down(pair, rows_in):
                rows, rowsT, sT, y = hidden_rows[pair % 2], expertT[pair % 2], selT[pair % 2], expert_out[pair % 2]
                i, bank, free = banks.take()
                pe.after(selected, free)
                for b in range(TB):
                    last = pe.engine.transpose(bank[:, b * P:(b + 1) * P], flat[:, b, pair * P:(pair + 1) * P], ident)
                banks.free[i] = spread = act_copy(sT.rearrange("p b t -> p (b t)"), bank[:, 0:S], pe.done(last))
                i, bank, free = banks.take()
                pe.after(rows_in, free)
                for f in range(4):
                    last = pe.engine.transpose(bank[:, f * P:(f + 1) * P], rows[:, f * P:(f + 1) * P], ident)
                banks.free[i] = tok = act_copy(rowsT.rearrange("p f s -> p (f s)"), bank, pe.done(last))
                for half in range(2):
                    taken = [weights.take() for _ in range(2)]
                    i, bank, free = banks.take()
                    pe.after(tok, free, *taken[0].ready, *taken[1].ready)
                    for f in range(4):
                        for j in range(2):
                            last = matmul(bank[j * SLOTS:(j + 1) * SLOTS, :], rowsT[:, f, j * SLOTS:(j + 1) * SLOTS],
                                          taken[j].raw[:, f, :], f == 0, f == 3)
                    product = pe.done(last)
                    for piece in taken:
                        weights.release(piece, product)
                    banks.free[i] = gated = vec.done(vec.after(product).tensor_scalar(
                        y[:, half * BANK:(half + 1) * BANK], bank, slot_gate[:, pair:pair + 1], None, ALU.mult))
                return spread, gated

            def gather(pair, spread, gated):
                sT, y = selT[pair % 2], expert_out[pair % 2]
                pe.after(gated, spread, held_free[0])
                for b in range(TB):
                    for half in range(2):
                        last = matmul(held[:, b, half * BANK:(half + 1) * BANK], sT[:, b, :],
                                      y[:, half * BANK:(half + 1) * BANK], pair == 0, pair == PAIRS - 1)
                return pe.done(last)

            read_sig = [None, None]
            rows_in = {}
            src_in = dispatch(0)
            i, bank, free = banks.take()
            pe.after(selected, free)
            for pair in range(PAIRS):
                for b in range(TB):
                    last = matmul(bank[:, pair * E:(pair + 1) * E], flat[:, b, pair * P:(pair + 1) * P], gates_w[:, b, :],
                                  b == 0, b == TB - 1)
            gate = pe.done(last)
            for j in range(2):
                tok = vec_copy(slot_gate[j * SLOTS:(j + 1) * SLOTS, :], bank[j * SLOTS:(j + 1) * SLOTS, j:PAIRS * E:E + 2], gate)
            banks.free[i] = tok
            flag = most_slots(slots, selected)
            for pair in range(PAIRS + 1):
                if pair < PAIRS:
                    rows_in[pair] = up(pair, tokensT[pair // 2 % 2], src_in)
                if pair:
                    made = down(pair - 1, rows_in[pair - 1])
                    if pair % 2 == 1 and pair < PAIRS - 1:
                        src_in = dispatch((pair + 1) // 2)
                    summed = gather(pair - 1, *made)
            late_tokens(l, gates_w, slots, flag)
            return summed

        def most_slots(slots, ready):
            most = stat(1)
            tok = vec.done(vec.after().reduce_max(most, slots.rearrange("p b e -> p (b e)"), AX.X))
            i, bank, free = banks.take()
            pe.after(tok, free)
            tok = pe.done(pe.engine.transpose(bank[0:1, 0:P], most, ident))
            top = stat(1)[0:1, :]
            banks.free[i] = vec.done(vec.after(tok).reduce_max(top, bank[0:1, 0:P], AX.X))
            return vec.done(vec.after().tensor_scalar(over, top, SLOTS - 0.5, None, ALU.is_gt))

        def late_tokens(l, gates_w, slots, flag):
            entered = [(lane.sem, lane.count) for lane in (pe, vec, act)]
            for lane in (pe, vec, act, pool, sp):
                lane.after(flag)
            more = nc.values_load(over, min_val=0, max_val=1)
            with nc.If(more > 0):
                names = ("pe", "vec", "act", "sp")
                lanes = [Lane(lane.engine, sem(f"late_{name}{l}"), name in ("vec", "act"))
                         for name, lane in zip(names, (pe, vec, act, sp))]
                lpe, lvec, lact, lsp = lanes
                loads = [Loads(sem(f"late_in{l}_{i}")) for i in range(3)]
                for lane in lanes:
                    lane.after(*entered)
                rest = late_rest
                lvec.done(lvec.after().tensor_scalar(rest, slots, SLOTS - 0.5, None, ALU.is_gt))
                tok = lvec.done(lvec.after().tensor_tensor(rest, rest, gates_w, ALU.mult))
                bank = [psum[:, 4 + i, :] for i in range(4)]
                lpe.after(tok)
                for b in range(TB):
                    last = lpe.engine.transpose(bank[0][0:N_EXPERTS, b * P:(b + 1) * P], rest[:, b, :], ident)
                gates_in = lvec.done(lvec.after(lpe.done(last)).tensor_copy(late_gatesT, bank[0][0:N_EXPERTS, 0:S]))
                used = gates_in
                for e in range(N_EXPERTS):
                    lpe.after(gates_in)
                    tok = lpe.done(lpe.engine.matmul(bank[0][:, 0:S], row_of(e, N_EXPERTS), late_gatesT, start=True, stop=True))
                    weight_in = lvec.done(lvec.after(tok).tensor_copy(late_gate, bank[0][:, 0:S]))
                    for f in range(4):
                        cols = slice(f * P, (f + 1) * P)
                        lsp.after(used)
                        w_in = [loads[0].start(nc.sync, late_w[0], by_rows(t["w1"][l, e])[:, :, cols]),
                                loads[1].start(nc.sync, late_w[1], by_rows(t["w3"][l, e])[:, :, cols]),
                                loads[2].start(nc.sync, late_w[2], t["w2"][l, e, cols, :])]
                        for i in range(2):
                            lpe.after(w_in[i], weight_in)
                            for c in range(KC):
                                for k in range(2):
                                    last = lpe.engine.matmul(bank[1 + i][:, 0:S], late_w[i][:, c, :], reread(xT[k][:, c, :]),
                                                             start=(c + k == 0), stop=(c + k == KC))
                            tok = lpe.done(last)
                        tok = lact.done(lact.after(tok, used).activation(late_up[0], bank[1][:, 0:S], ACT.Sigmoid))
                        lvec.done(lvec.after(tok).tensor_tensor(late_up[1], late_up[0], bank[1][:, 0:S], ALU.mult))
                        lvec.done(lvec.after().tensor_tensor(late_up[1], late_up[1], bank[2][:, 0:S], ALU.mult))
                        tok = lvec.done(lvec.after().tensor_tensor(late_up[1], late_up[1], late_gate, ALU.mult))
                        lpe.after(tok, w_in[2])
                        for b in range(TB):
                            for half in range(2):
                                last = lpe.engine.matmul(held[:, b, half * BANK:(half + 1) * BANK],
                                                         late_up[1][:, b * P:(b + 1) * P],
                                                         late_w[2][:, half * BANK:(half + 1) * BANK],
                                                         start=False, stop=False, skip_group_check=True)
                        used = lpe.done(last)
                for engine in (nc.tensor, nc.vector, nc.scalar, nc.gpsimd, nc.sync):
                    engine.wait_ge(used[0], used[1])

        def first_block(l, x_ready, pos_ready, bias_in, band_in, mem_in):
            ready = turn(x, D, xT, x_ready)
            for a, b_ in first_cuts():
                pe.after(bias_in)
                z_ready = rows_product(xT, b_ - a, lambda b, bank, product: act_copy(z[:, b, a:b_], bank, product),
                                       ready, bias_row[:, a:b_])
            mem_ready = turn(mem_rows, D, memT, mem_in)
            result = {"xT": ready, "upT": [None, None]}
            result["pool"] = pool_branch(l, z_ready, band_in)
            together(dsa_branch(pos_ready if l == 0 else None, z_ready, result), memory_branch(l, mem_ready, ready, result))
            norm_in = load_norm_rows(t["ln1_g"][l], t["ln1_b"][l], result["dsa"])
            together(merge(l, 1, result["dsa"], False, result))
            mixed = held_product([mergedT], D, result["merged"])
            normed = layer_norm(mixed, norm_in)
            norm_in = load_norm_rows(t["ln2_g"][l], t["ln2_b"][l], normed)
            ready = turn(x, D, xT, normed)
            summed = expert_layer(l, ready)
            normed = layer_norm(summed, norm_in)
            return normed, load_layer_inputs(l + 1, summed, normed) if l + 1 < first_layers else ()

        def rms_turned(gain, ready):
            sums, root = stat(TB), stat(TB)
            for b in range(TB):
                tok = act.done(act.after(ready).activation(normed_rows[:, b, :], x[:, b, :], ACT.Square,
                                                           accum_out=sums[:, b:b + 1]))
            tok = act.done(act.after().activation(root, sums, ACT.Sqrt, bias=const("rms_eps"), scale=1.0 / D))
            vec.done(vec.after(tok).reciprocal(root, root))
            for b in range(TB):
                tok = vec.done(vec.after().tensor_scalar(normed_rows[:, b, :], x[:, b, :], root[:, b:b + 1], None, ALU.mult))
            return turn(normed_rows, D, xT, tok, scale_col=gain)

        def head_norm(src, dst, heads, gain, scale, sq):
            s, d, m = (a.rearrange("p (h d) -> p h d", d=HD) for a in (src, dst, sq))
            sums, root = stat(heads), stat(heads)
            vec.done(vec.after().tensor_tensor(m, s, s, ALU.mult))
            tok = vec.done(vec.after().reduce_sum(sums, m, AX.X))
            tok = act.done(act.after(tok).activation(root, sums, ACT.Sqrt, bias=const("rms_eps"), scale=1.0 / HD))
            yield
            vec.done(vec.after(tok).reciprocal(root, root))
            vec.done(vec.after().tensor_tensor(d, s, root.unsqueeze(2).to_broadcast([P, heads, HD]), ALU.mult))
            g = gain if len(gain.shape) == 3 else gain.unsqueeze(1).to_broadcast([P, heads, HD])
            return vec.done(vec.after().scalar_tensor_tensor(d, d, scale, g, ALU.mult, ALU.mult))

        def swa_branch(l, z_ready):
            probs, qT, kT, scratch, turned = (swa[n] for n in ("probs", "qT", "kT", "scratch", "turned"))
            vec.after(z_ready)
            cos = const("rope_cos").rearrange("p (b d) -> p b d", b=TB)
            sin = const("rope_sin").rearrange("p (b d) -> p b d", b=TB)
            for b in range(TB):
                zb = z2[:, b, :]
                yield from head_norm(zb[:, C2_AQ:C2_AK], zb[:, C2_AQ:C2_AK], SWA_HEADS, head_gain[:, l, 0, :], HD ** -0.5,
                                     scratch[:, b, 0:512])
                yield from head_norm(zb[:, C2_AK:C2_AV], zb[:, C2_AK:C2_AV], SWA_KV, head_gain[:, l, 1, :], 1.0,
                                     scratch[:, b, 512:640])
                rope(zb[:, 0:C2_AV], turned[:, b, :], cos[:, b, :], sin[:, b, :], SWA_HEADS + SWA_KV, scratch[:, b, :])
                for kv in range(SWA_KV):
                    for j in range(2):
                        at = kv * P + j * HD
                        tok = vec.done(vec.after().tensor_copy(zb[:, C2_AQ + at:C2_AQ + at + HD],
                                                               turned[:, b, 512 + kv * HD:512 + (kv + 1) * HD]))
            yield
            turn(turned, 512, qT, tok)
            heads_ready = turn(z2[:, :, C2_AQ:C2_AQ + 2 * P], 2 * P, kT, tok)
            yield
            done = None
            for b in range(TB):
                keys = (b + 1) * P
                tops = stat(SWA_HEADS)
                vec.after(done)
                for h in range(SWA_HEADS):
                    i, bank, free = banks.take()
                    at = HD * (h % 2)
                    pe.after(heads_ready, free)
                    product = pe.done(matmul(bank[:, 0:keys], qT[at:at + HD, h // 2, b * P:(b + 1) * P],
                                             kT[at:at + HD, h // 4, 0:keys], True, True))
                    banks.free[i] = vec.done(vec.after(product).tensor_tensor_reduce(
                        out=probs[:, h, 0:keys], in0=bank[:, 0:keys], in1=reach_of["swa_reach"][:, b, 0:keys], scale=1.0,
                        scalar=TAKEN, op0=ALU.add, op1=ALU.max, accum_out=tops[:, h:h + 1]))
                    if h % 4 == 3:
                        yield
                ready = yield from softmax(probs, tops, SWA_HEADS, keys, sinks[:, l, :], 1.0)
                yield
                room = lambda h, n: swa["probsT"][:, h:h + n, :]
                ready = turn_probs(probs, room, SWA_HEADS, b + 1, ready)
                yield
                for pair in range(SWA_HEADS // 2):
                    done = head_values(pair, b + 1,
                                       lambda h, kb: z2[:, kb, C2_AV + (h // 4) * HD:C2_AV + (h // 4 + 1) * HD], room,
                                       yT[:, pair, b * P:(b + 1) * P], ready)
                yield

        def decays(l, z_ready):
            pre, low, logs, keys_add = (stat(TB, 8) for _ in range(4))
            sums = decay_sums
            inp = stat(TB, 4)
            vec.after(z_ready)

            def biased(dst, at, i):
                return vec.done(vec.after().tensor_tensor(
                    dst, z2[:, :, at:at + 4], gate_bias[:, l, 4 * i:4 * i + 4].unsqueeze(1).to_broadcast([P, TB, 4]), ALU.add))

            biased(pre[:, :, 0:4], C2_BF, 0)
            biased(pre[:, :, 4:8], C2_CF, 1)
            biased(inp, C2_CI, 2)
            tok = vec.done(vec.after().scalar_tensor_tensor(low, pre, -1.0, pre, ALU.mult, ALU.max))
            act.done(act.after(tok).activation(low, low, ACT.Exp, scale=-1.0))
            tok = act.done(act.after().activation(low, low, ACT.Ln, bias=const("one")))
            tok = vec.done(vec.after(tok).scalar_tensor_tensor(logs, pre, 0.0, low, ALU.min, ALU.subtract))
            i, bank, free = banks.take()
            pe.after(tok, free)
            for b in range(TB):
                for sb_ in range(b + 1):
                    last = matmul(bank[:, b * 8:b * 8 + 8], upto[:, sb_, b * P:(b + 1) * P], logs[:, sb_, :], sb_ == 0, sb_ == b)
            banks.free[i] = vec_copy(sums.rearrange("p b h -> p (b h)"), bank[:, 0:TB * 8], pe.done(last))
            vec.done(vec.after().tensor_scalar(keys_add[:, :, 0:4], sums[:, :, 0:4], -1.0, None, ALU.mult))
            tok = vec.done(vec.after().tensor_tensor(keys_add[:, :, 4:8], inp, sums[:, :, 4:8], ALU.subtract))
            key_rows = upT[0][0:8, :]
            i, bank, free = banks.take()
            pe.after(tok, free)
            for b in range(TB):
                last = pe.engine.transpose(bank[0:8, b * P:(b + 1) * P], keys_add[:, b, :], ident)
            banks.free[i] = tok = vec_copy(key_rows, bank[0:8, 0:S], pe.done(last))
            return sums, key_rows, tok

        def fox_branch(l, sums, key_rows, rows_ready):
            probs, qT, kT, scratch, turned = (fox[n] for n in ("probs", "qT", "kT", "scratch", "turned"))
            for b in range(TB):
                zb = z2[:, b, :]
                yield from head_norm(zb[:, C2_BQ:C2_BK], turned[:, b, 0:256], FOX_HEADS, head_gain[:, l, 2, :], HD ** -0.5,
                                     scratch[:, b, 0:256])
                tok = yield from head_norm(zb[:, C2_BK:C2_BV], turned[:, b, 256:512], FOX_HEADS, head_gain[:, l, 3, :], 1.0,
                                           scratch[:, b, 0:256])
            yield
            turn(turned, 256, qT, tok)
            heads_ready = turn(turned[:, :, 256:512], 256, kT, tok)
            yield
            done = None
            for b in range(TB):
                keys = (b + 1) * P
                tops = stat(FOX_HEADS)
                vec.after(done)
                for h in range(FOX_HEADS):
                    i, bank, free = banks.take()
                    at = HD * (h % 2)
                    pe.after(heads_ready, rows_ready, free)
                    matmul(bank[:, 0:keys], qT[at:at + HD, h // 2, b * P:(b + 1) * P], kT[at:at + HD, h // 2, 0:keys],
                           True, False)
                    product = pe.done(matmul(bank[:, 0:keys], row_of(h, 8), key_rows[:, 0:keys], False, True))
                    banks.free[i] = vec.done(vec.after(product).scalar_tensor_tensor(
                        probs[:, h, 0:keys], bank[:, 0:keys], sums[:, b, h:h + 1], reach_of["causal"][:, b, 0:keys],
                        ALU.add, ALU.add))
                yield
                vec.done(vec.after().reduce_max(tops, probs[:, 0:FOX_HEADS, 0:keys], AX.X))
                ready = yield from softmax(probs, tops, FOX_HEADS, keys, None, 1.0)
                yield
                room = lambda h, n: fox["probsT"][:, h:h + n, :]
                ready = turn_probs(probs, room, FOX_HEADS, b + 1, ready)
                yield
                for pair in range(FOX_HEADS // 2):
                    done = head_values(pair, b + 1, lambda h, kb: z2[:, kb, C2_BV + h * HD:C2_BV + (h + 1) * HD], room,
                                       yT[:, 4 + pair, b * P:(b + 1) * P], ready)
                yield

        def mlstm_branch(l, sums, key_rows, rows_ready, z_ready, result):
            probs, qT, kT, scratch, turned = (mls[n] for n in ("probs", "qT", "kT", "scratch", "turned"))
            turn(z2[:, :, C2_CQ:C2_CK], 256, qT, z_ready)
            heads_ready = turn(z2[:, :, C2_CK:C2_CV], 256, kT, z_ready)
            H = MLSTM_HEADS
            for b in range(TB):
                open_in = act.done(act.after(z_ready).activation(scratch[:, b, 256:512], z2[:, b, C2_CO:C2_CO + 256], ACT.Sigmoid))
            yield
            for b in range(TB):
                keys = (b + 1) * P
                tops, minus, dens, floor = stat(H), stat(H), stat(H), stat(H)
                own = sums[:, b, 4:8]
                for h in range(H):
                    i, bank, free = banks.take()
                    pe.after(rows_ready, free)
                    product = pe.done(matmul(bank[:, 0:keys], row_of(4 + h, 8), key_rows[:, 0:keys], True, True))
                    banks.free[i] = vec.done(vec.after(product).scalar_tensor_tensor(
                        probs[:, h, 0:keys], bank[:, 0:keys], own[:, h:h + 1], reach_of["causal"][:, b, 0:keys],
                        ALU.add, ALU.add))
                yield
                vec.done(vec.after().reduce_max(tops, probs[:, 0:H, 0:keys], AX.X))
                vec.done(vec.after().tensor_tensor(tops, tops, own, ALU.max))
                lowered = vec.done(vec.after().tensor_scalar(minus, tops, -1.0, None, ALU.mult))
                for h in range(H):
                    weighed = act.done(act.after(lowered).activation(probs[:, h, 0:keys], probs[:, h, 0:keys], ACT.Exp,
                                                                     bias=minus[:, h:h + 1]))
                floored = act.done(act.after().activation(floor, minus, ACT.Exp))
                yield
                for h in range(H):
                    i, bank, free = banks.take()
                    at = HD * (h % 2)
                    pe.after(heads_ready, free)
                    product = pe.done(matmul(bank[:, 0:keys], qT[at:at + HD, h // 2, b * P:(b + 1) * P],
                                             kT[at:at + HD, h // 2, 0:keys], True, True))
                    banks.free[i] = tok = vec.done(vec.after(product, weighed).tensor_tensor_reduce(
                        out=probs[:, h, 0:keys], in0=bank[:, 0:keys], in1=probs[:, h, 0:keys], scale=HD ** -0.5, scalar=0.0,
                        op0=ALU.mult, op1=ALU.add, accum_out=dens[:, h:h + 1]))
                yield
                ready = turn_probs(probs, lambda h, n: mls["probsT"][:, h:h + n, :], H, b + 1, tok)
                vec.done(vec.after().scalar_tensor_tensor(dens, dens, -1.0, dens, ALU.mult, ALU.max))
                vec.done(vec.after(floored).tensor_tensor(dens, dens, floor, ALU.max))
                vec.done(vec.after().reciprocal(dens, dens))
                yield
                i, bank, free = banks.take()
                pe.after(ready, free)
                for h in range(H):
                    for kb in range(b + 1):
                        last = matmul(bank[:, h * HD:(h + 1) * HD], mls["probsT"][:, h, kb * P:(kb + 1) * P],
                                      z2[:, kb, C2_CV + h * HD:C2_CV + (h + 1) * HD], kb == 0, kb == b)
                hc = turned[:, b, 0:256]
                banks.free[i] = vec.done(vec.after(pe.done(last)).tensor_tensor(
                    hc.rearrange("p (h d) -> p h d", d=HD), bank[:, 0:256].rearrange("p (h d) -> p h d", d=HD),
                    dens.unsqueeze(2).to_broadcast([P, H, HD]), ALU.mult))
                yield from head_norm(hc, hc, H, mlstm_gain[:, l, :].rearrange("p (h d) -> p h d", d=HD), 1.0,
                                     scratch[:, b, 0:256])
                tok = vec.done(vec.after(open_in).tensor_tensor(hc, hc, scratch[:, b, 256:512], ALU.mult))
            yield
            turn(turned, 256, yT[:, 6:8, :], tok)

        def second_block(l, x_ready):
            ready = rms_turned(rms_cols[:, l, 0, :], x_ready)
            for a, b_ in second_cuts():
                z_ready = rows_product(xT, b_ - a, lambda b, bank, product: act_copy(z2[:, b, a:b_], bank, product), ready)
            sums, key_rows, rows_ready = decays(l, z_ready)
            together(swa_branch(l, z_ready), fox_branch(l, sums, key_rows, rows_ready),
                     mlstm_branch(l, sums, key_rows, rows_ready, z_ready, {}))
            mixed = held_product([yT], D, (act.sem, act.count))
            for b in range(TB):
                tok = vec.done(vec.after(mixed).tensor_tensor(x[:, b, :], x[:, b, :], held[:, b, :], ALU.add))
            held_free[0] = tok
            ready = rms_turned(rms_cols[:, l, 1, :], tok)
            steps = D_FF // BANK

            def up(j):
                hidden = hiddenT[j % 2]
                for half in range(2):
                    piece = weights.take()
                    for f in (2 * half, 2 * half + 1):
                        i, bank, product = cols_product(piece, f % 2 * P, xT, ready)
                        kept = upT[f % 2]
                        banks.free[i] = tok = act.done(act.after(product, (vec.sem, vec.count)).activation(kept[:, :], bank, ACT.Relu))
                        squared = vec.done(vec.after(tok, down_done[j % 2]).tensor_tensor(kept[:, :], kept[:, :], kept[:, :], ALU.mult))
                        made = split(hidden, f, kept[:, :], squared)
                    weights.release(piece, product)
                return made

            def down(j, made):
                hidden = hiddenT[j % 2]
                for half in range(2):
                    piece = weights.take()
                    pe.after(made, held_free[0], *piece.ready)
                    for b in range(TB):
                        for f in range(4):
                            last = product3(held[:, b, half * BANK:(half + 1) * BANK],
                                            [h[:, f, b * P:(b + 1) * P] for h in hidden], [w[:, f, :] for w in piece.parts],
                                            j == 0 and f == 0, j == steps - 1 and f == 3)
                    done = pe.done(last)
                    weights.release(piece, done)
                return done

            down_done = [None, None]
            for j in range(steps):
                made = up(j)
                down_done[j % 2] = down(j, made)
            for b in range(TB):
                tok = vec.done(vec.after(down_done[(steps - 1) % 2]).tensor_tensor(x[:, b, :], x[:, b, :], held[:, b, :], ALU.add))
            held_free[0] = tok
            return tok

        routed = sb("routed", 2, TB, N_EXPERTS)
        slot_gate = sb("slot_gate", PAIRS)
        decay_sums = sb("decay_sums", TB, 8)
        inputs_in = load_layer_inputs(0, None, None)
        params_in = (param_loads.sem, param_loads.count)
        result_params = [params_in]
        pos_ready = position_angles(params_in)
        pe.after(consts_in)
        x_ready = x_in
        for l in range(first_layers):
            x_ready, inputs_in = first_block(l, x_ready, pos_ready, *inputs_in)
        for l in range(second_layers):
            x_ready = second_block(l, x_ready)
        sp.after(x_ready)
        for b in range(TB):
            stored = stores.start(nc.sync, out[0, b * P:(b + 1) * P, :], x[:, b, :])
        sp.after(stored)


_INPUTS = ("x", "mem", "positions", "w_in", "b_in", "pool_w", "pool_scale", "w_mem_kv", "w_br", "w_out", "ln1_g", "ln1_b",
           "w_router", "router_bias", "w1", "w3", "w2", "ln2_g", "ln2_b", "norm1_2", "w_in_2", "swa_q_norm_2",
           "swa_k_norm_2", "swa_sinks_2", "fox_q_norm_2", "fox_k_norm_2", "fox_f_bias_2", "mlstm_i_bias_2",
           "mlstm_f_bias_2", "mlstm_out_norm_2", "w_out_2", "norm2_2", "w_ff1_2", "w_ff2_2")


def kernel(**inputs):
    import concourse.bacc as bacc
    from concourse.bass_utils import run_bass_kernel_spmd

    nc = bacc.Bacc("TRN2", target_bir_lowering=False, num_devices=1)
    arrays = {f"in_{n}": np.ascontiguousarray(inputs[n]) for n in _INPUTS}
    arrays["in_shape_consts"] = shape_constants()
    arrays["in_pool_band"] = pool_band()
    t = {n[3:]: nc.dram_tensor(n, a.shape, mybir.dt.from_np(a.dtype), kind="ExternalInput").ap() for n, a in arrays.items()}
    out = nc.dram_tensor("out_0", (1, S, D), F32, kind="ExternalOutput").ap()
    build_program(nc, t, out)
    return run_bass_kernel_spmd(nc, [arrays], core_ids=[0]).results[0]["out_0"]
```

```python
import numpy as np
from contextlib import ExitStack

import concourse.bass as bass
from concourse import mybir

F32 = mybir.dt.float32
F32R = mybir.dt.float32r
I32 = mybir.dt.int32
ALU = mybir.AluOpType
ACT = mybir.ActivationFunctionType
AX = mybir.AxisListType

P = 128
S = 256
TB = S // P
D = 1024
KC = D // P
DEPTH = 2
CHUNK = 64
N_MEM = 256
BANK = 512

POOL_GROUPS = 4
POOL_WINDOWS = (2, 4, 8, 16)
HD = 64
HALF = HD // 2
DSA_HEADS = 8
DSA_TOPK = S // 4
MEM_HEADS = 4
N_BRANCH = 3
BRANCH = 512
C_POOL, C_Q, C_K, C_V, C_IQ, C_IK, C_IW, C_MQ, C_GATE = 0, 512, 1024, 1536, 2048, 2560, 2624, 2632, 3144
D_IN = C_GATE + N_BRANCH * D
N_EXPERTS, N_GROUPS, PER_GROUP, D_EXPERT = 16, 4, 4, 512
SLOTS = 64
PAIRS = N_EXPERTS // 2
DN_ALPHA = (2 * DEPTH) ** 0.25
LN_EPS = 1e-5

SWA_HEADS, SWA_KV, FOX_HEADS, MLSTM_HEADS = 8, 2, 4, 4
C2_AQ, C2_AK, C2_AV, C2_BQ, C2_BK, C2_BV, C2_BF = 0, 512, 640, 768, 1024, 1280, 1536
C2_CQ, C2_CK, C2_CV, C2_CI, C2_CF, C2_CO = 1540, 1796, 2052, 2308, 2312, 2316
IN2 = C2_CO + MLSTM_HEADS * HD
D_FF = 4 * D
RMS_EPS = 1e-6

RING = 9
REGION = TB * C_MQ + 2 * TB * 10 * HD + (N_BRANCH * 4 + 8 + 4 + 4 * 4 + 1 + KC) * S
SMALL = 1024

OUT_OF_REACH = -1e30
TAKEN = -3e38
ROPE_THETA = 10000.0

CONSTS = (
    ("ident", P), ("upto", TB * S), ("rope_cos", TB * HALF), ("rope_sin", TB * HALF),
    ("inv_freq", HALF), ("dsa_reach", TB * S), ("swa_reach", TB * S), ("causal", TB * S),
    ("descend", N_EXPERTS), ("slot", SLOTS), ("ln_eps", 1), ("rms_eps", 1), ("one", 1), ("half_pi", 1),
)
CONST_AT = {}
_at = 0
for _name, _width in CONSTS:
    CONST_AT[_name] = (_at, _width)
    _at += _width
CONST_WIDTH = _at


def token_of():
    return np.arange(TB)[None, :] * P + np.arange(P)[:, None], np.arange(S)


def pool_band():
    s, t = token_of()
    band = np.zeros((P, POOL_GROUPS, TB, S), np.float32)
    for g, w in enumerate(POOL_WINDOWS):
        inside = (s[:, :, None] <= t) & (s[:, :, None] > t - w)
        band[:, g] = inside / np.minimum(t + 1, w) - (s[:, :, None] == t)
    return band


def shape_constants():
    s, t = token_of()
    parts = {}
    parts["ident"] = np.eye(P)
    parts["upto"] = (s[:, :, None] <= t).astype(np.float32)
    inv = (np.float32(ROPE_THETA) ** (-np.arange(HALF, dtype=np.float32) / np.float32(HALF))).astype(np.float32)
    ang = (s[:, :, None].astype(np.float32) * inv).astype(np.float32).astype(np.float64)
    parts["rope_cos"], parts["rope_sin"] = np.cos(ang), np.sin(ang)
    parts["inv_freq"] = np.broadcast_to(inv, (P, HALF))
    q, k = s[:, :, None] // CHUNK, t // CHUNK
    parts["dsa_reach"] = np.where(k <= q, 0.0, OUT_OF_REACH)
    parts["swa_reach"] = np.where((k <= q) & (k >= q - 2), 0.0, OUT_OF_REACH)
    parts["causal"] = np.where(t <= s[:, :, None], 0.0, OUT_OF_REACH)
    parts["descend"] = np.broadcast_to(np.arange(N_EXPERTS, 0, -1.0), (P, N_EXPERTS))
    parts["slot"] = np.broadcast_to(np.arange(SLOTS, dtype=np.float32), (P, SLOTS))
    parts["ln_eps"] = np.full((P, 1), LN_EPS)
    parts["rms_eps"] = np.full((P, 1), RMS_EPS)
    parts["one"] = np.ones((P, 1))
    parts["half_pi"] = np.full((P, 1), np.pi / 2)
    return np.concatenate([np.asarray(parts[n], np.float32).reshape(P, w) for n, w in CONSTS], axis=1)


class Lane:

    def __init__(self, engine, sem, in_order):
        self.engine, self.sem, self.count, self.passed, self.in_order = engine, sem, 0, {}, in_order

    def after(self, *tokens):
        if self.in_order and self.count:
            tokens = (*tokens, (self.sem, self.count))
        return self.beside(*tokens)

    def beside(self, *tokens):
        for token in tokens:
            if token is not None and self.passed.get(token[0].name, 0) < token[1]:
                self.engine.wait_ge(token[0], token[1])
                self.passed[token[0].name] = token[1]
        return self.engine

    def done(self, instruction):
        self.count += 1
        instruction.then_inc(self.sem, 1)
        return (self.sem, self.count)


class Loads:

    def __init__(self, sem):
        self.sem, self.count = sem, 0

    def start(self, engine, dst, src):
        self.count += 16
        engine.dma_start(dst, src, allow_slow_non_contiguous=True).then_inc(self.sem, 16)
        return (self.sem, self.count)


class Banks:

    def __init__(self, banks):
        self.banks, self.free, self.at = banks, [None] * len(banks), -1

    def take(self):
        self.at = (self.at + 1) % len(self.banks)
        return self.at, self.banks[self.at], self.free[self.at]


class Piece:

    def __init__(self, raw, positions, loaded):
        self.raw, self.positions, self.loaded = raw, positions, loaded
        self.parts, self.ready = None, None


class WeightRing:

    AHEAD = 3

    def __init__(self, sp, act, vec, slots, sems, plan, rounded):
        self.sp, self.act, self.vec, self.slots, self.plan = sp, act, vec, slots, plan
        self.rounded = rounded
        self.loads = [Loads(s) for s in sems]
        self.freed, self.pieces = {}, []
        self.position = self.taken = self.prepared = 0
        self.load_ahead()

    def free(self, position):
        return position < len(self.slots) or position - len(self.slots) in self.freed

    def last_reader(self, position):
        return self.freed.get(position - len(self.slots))

    def view(self, position, shape):
        a, b = shape[1:]
        return self.slots[position % len(self.slots)][:, 0:a * b].rearrange("p (a b) -> p a b", a=a)

    def load_ahead(self):
        while len(self.pieces) < len(self.plan) and self.free(self.position):
            source, split = self.plan[len(self.pieces)]
            at = self.position
            self.sp.after(self.last_reader(at))
            raw = self.view(at, source.shape)
            loaded = self.loads[at % len(self.slots)].start(self.sp.engine, raw, source)
            self.pieces.append(Piece(raw, (at, at + 1) if split else (at,), loaded))
            self.position += 1 + split

    def prepare(self, upto):
        while self.prepared < min(upto, len(self.pieces)) and self.free(self.pieces[self.prepared].positions[-1]):
            piece = self.pieces[self.prepared]
            self.prepared += 1
            if len(piece.positions) == 1:
                piece.parts, piece.ready = [piece.raw], [piece.loaded]
                continue
            hi = self.view(piece.positions[1], piece.raw.shape)
            lo = piece.raw
            hi_in = self.act.done(self.act.beside(piece.loaded, self.last_reader(piece.positions[1])).activation(
                self.rounded(hi), piece.raw, ACT.Copy))
            left = self.vec.done(self.vec.beside(hi_in).tensor_tensor(self.rounded(lo), piece.raw, self.rounded(hi).bitcast(F32), ALU.subtract))
            piece.parts, piece.ready = [hi, lo], [hi_in, left]

    def take(self):
        self.prepare(self.taken + self.AHEAD)
        self.taken += 1
        assert self.prepared >= self.taken
        return self.pieces[self.taken - 1]

    def release(self, piece, token):
        for position in piece.positions:
            self.freed[position] = token
        self.load_ahead()


def by_rows(ap):
    return ap.rearrange("(c p) n -> p c n", p=P)


def even_cuts(a, b, pieces):
    ends = [a + (b - a) * i // pieces // 2 * 2 for i in range(pieces + 1)]
    return list(zip(ends, ends[1:]))


FIRST_CUTS = (("index", even_cuts(C_IQ, C_MQ, 2)), ("pool", even_cuts(C_POOL, C_Q, 1)), ("heads", even_cuts(C_Q, C_IQ, 4)))
SECOND_CUTS = (("swa", even_cuts(C2_AQ, C2_BQ, 2)), ("rest", even_cuts(C2_BQ, IN2, 4)))


def halves(ap, how):
    n = ap.shape[0 if how == "rows" else 1] // 2
    return [by_rows(ap[i * n:(i + 1) * n, :] if how == "rows" else ap[:, i * n:(i + 1) * n]) for i in range(2)]


def merge_plan(t, l, n):
    plan = []
    for half in range(2):
        a = C_GATE + n * D + half * BANK
        plan += [(w, True) for w in halves(t["w_in"][l, :, a:a + BANK], "cols")]
        plan.append((by_rows(t["w_br"][l, n, :, half * BANK:(half + 1) * BANK]), False))
    return plan


def weight_plan(t, first_layers, second_layers):
    plan = []
    for l in range(first_layers):
        for _, cuts in FIRST_CUTS:
            for a, b in cuts:
                plan += [(w, True) for w in halves(t["w_in"][l, :, a:b], "rows")]
        plan += [(w, False) for w in halves(t["w_mem_kv"][l, :, 0:BANK], "cols")]
        plan += [(w, False) for w in halves(t["w_mem_kv"][l, :, BANK:2 * BANK], "rows")]
        plan += merge_plan(t, l, 0)
        plan += [(w, True) for w in halves(t["w_in"][l, :, C_MQ:C_GATE], "cols")]
        plan += merge_plan(t, l, 2) + merge_plan(t, l, 1)
        for a in (0, BANK):
            plan += [(w, True) for w in halves(t["w_out"][l, :, a:a + BANK], "rows")]
        for pair in range(PAIRS + 1):
            if pair < PAIRS:
                for w in ("w1", "w3"):
                    both = [halves(t[w][l, 2 * pair + j], "rows") for j in range(2)]
                    plan += [(both[j][half], False) for half in range(2) for j in range(2)]
            if pair:
                both = [halves(t["w2"][l, 2 * pair - 2 + j], "cols") for j in range(2)]
                plan += [(both[j][half], False) for half in range(2) for j in range(2)]
    for l in range(second_layers):
        for _, cuts in SECOND_CUTS:
            for a, b in cuts:
                plan += [(w, True) for w in halves(t["w_in_2"][l, :, a:b], "rows")]
        for a in (0, BANK):
            plan += [(w, False) for w in halves(t["w_out_2"][l, :, a:a + BANK], "rows")]
        for j in range(0, D_FF + BANK, BANK):
            if j < D_FF:
                plan += [(w, True) for w in halves(t["w_ff1_2"][l, :, j:j + BANK], "cols")]
            if j:
                plan += [(w, True) for w in halves(t["w_ff2_2"][l, j - BANK:j, :], "cols")]
    return plan


def until(name, tokens):
    while name not in tokens:
        yield
    return tokens[name]


def together(*works):
    works = list(works)
    while works:
        for work in list(works):
            try:
                next(work)
            except StopIteration:
                works.remove(work)


def build_program(nc, t, out, first_layers=DEPTH, second_layers=DEPTH):
    with ExitStack() as ctx:
        def sb(name, *shape, dt=F32):
            return ctx.enter_context(nc.sbuf_tensor(name + "_sb", [P, *shape], dt))

        def sem(name):
            return ctx.enter_context(nc.semaphore(name))

        rounded_face = {}

        def two_faced(name, *shape):
            width = int(np.prod(shape))
            tile = sb(name, *shape)
            rounded_face[tile.name] = nc.alloc_sbuf_tensor_at(name + "_rounded", [P, *shape], F32R,
                                                              offset=nc.sbuf_base - 4 * width)
            return tile

        def rounded(ap):
            return bass.AP(tensor=rounded_face[ap.tensor.name], offset=ap.offset, ap=ap.ap)

        def reread(ap):
            return rounded(ap).bitcast(F32)

        consts = sb("consts", CONST_WIDTH)
        slots_of_ring = [two_faced(f"ring{i}", KC * BANK // 2) for i in range(RING)]
        x = sb("x", TB, D)
        xT = [two_faced("xT_hi", KC, S), two_faced("xT_lo", KC, S)]
        mkT = sb("mkT", MEM_HEADS, N_MEM)
        mv = sb("mv", TB, BRANCH)
        upT = [sb(f"upT{i}", S) for i in range(2)]
        region = two_faced("region", REGION)
        cut = [0]

        def part(*shape, rows=P):
            width = int(np.prod(shape))
            cut[0] += width
            assert cut[0] <= REGION
            return shaped(region[0:rows, cut[0] - width:cut[0]], *shape)

        def shaped(flat, *shape):
            return flat if len(shape) == 1 else flat.rearrange(
                "p (a b) -> p a b" if len(shape) == 2 else "p (a b c) -> p a b c", **dict(zip("abc", shape)))

        z = part(TB, C_MQ)
        turned = part(TB, 10 * HD)
        scratch = part(TB, 10 * HD)
        branchT = part(N_BRANCH * 4, S)
        bias_row = region[0:1, cut[0]:cut[0] + C_MQ]
        probs = part(8, S)
        mem_probs = part(MEM_HEADS, S)
        band_at = cut[0]
        qT = part(4, S)
        kT = part(4, S)
        mqT = part(MEM_HEADS, S)
        iqT = mem_probsT = part(4, S)
        ikT = part(S)
        mergedT = part(KC, S)
        mem_rows = shaped(region[:, TB * C_MQ + 4 * TB * 5 * HD:TB * C_MQ + 4 * TB * 5 * HD + TB * D], TB, D)
        memT = mergedT
        band = shaped(region[:, band_at:band_at + POOL_GROUPS * TB * S], POOL_GROUPS, TB, S)
        pool_w = shaped(region[:, band_at + POOL_GROUPS * TB * S:band_at + POOL_GROUPS * TB * S + BANK], POOL_GROUPS, P)
        norm_at = band_at + 8 * S
        norm_rows = shaped(region[:, norm_at:norm_at + 2 * D], 2, D)

        def z_probsT(h, n):
            return shaped(z[:, h // 4, C_Q + h % 4 * S:C_Q + (h % 4 + n) * S], n, S)

        cut[0] = 0
        sel = part(TB, N_EXPERTS, SLOTS)
        selT = [part(TB, P) for _ in range(2)]
        tokensT = [part(KC, 4 * SLOTS) for _ in range(2)]
        opened = [part(D_EXPERT) for _ in range(2)]
        hidden_rows = [part(D_EXPERT) for _ in range(2)]
        expertT = [part(4, P) for _ in range(2)]
        expert_out = [part(D) for _ in range(2)]
        late_w = [part(KC, P), part(KC, P), part(D)]
        late_gate = part(S)
        late_up = [part(S), part(S)]
        late_gatesT = part(S, rows=N_EXPERTS)
        late_rest = part(TB, N_EXPERTS)
        assert cut[0] <= norm_at

        cut[0] = 0
        z2 = part(TB, IN2)
        yT = part(KC, S)
        swa = dict(turned=part(TB, 10 * HD), probs=part(8, S), probsT=part(8, S), qT=part(4, S), kT=part(2, S))
        swa["scratch"] = shaped(swa["probsT"].rearrange("p h k -> p (h k)")[:, 0:TB * 10 * HD], TB, 10 * HD)
        fox = dict(turned=part(TB, 8 * HD), scratch=part(TB, 4 * HD), qT=part(2, S), kT=part(2, S),
                   probs=xT[0][:, 0:4, :], probsT=xT[0][:, 4:8, :])
        mls = dict(turned=part(TB, 4 * HD), scratch=part(TB, 8 * HD), qT=part(2, S), kT=part(2, S),
                   probs=xT[1][:, 0:4, :], probsT=xT[1][:, 4:8, :])
        squares = shaped(region[:, 0:TB * D], TB, D)
        hiddenT = [[shaped(region[:, (2 * i + k) * 4 * S + TB * D:(2 * i + k + 1) * 4 * S + TB * D], 4, S) for k in range(2)]
                   for i in range(2)]

        small = sb("small", SMALL)
        penalty = sb("penalty", TB, S)
        over = sb("over", 1, dt=I32)[0:1, :]
        bias_cols = sb("bias_cols", DEPTH, (D_IN - C_MQ) // P)
        pool_scale = sb("pool_scale", DEPTH, POOL_GROUPS)
        router_w = two_faced("router_w", KC, N_EXPERTS)
        router_parts = [two_faced("router_hi", KC, N_EXPERTS), router_w]
        router_b = sb("router_b", N_EXPERTS)
        rms_cols = sb("rms_cols", DEPTH, 2, KC)
        head_gain = sb("head_gain", DEPTH, 4, HD)
        mlstm_gain = sb("mlstm_gain", DEPTH, MLSTM_HEADS * HD)
        sinks = sb("sinks", DEPTH, SWA_HEADS)
        gate_bias = sb("gate_bias", DEPTH, 12)
        positions = sb("positions", TB, dt=I32)
        pos_cos = sb("pos_cos", TB, HALF)
        pos_sin = sb("pos_sin", TB, HALF)

        psum = ctx.enter_context(nc.psum_tensor("psum", [P, 8, BANK], F32))

        def const(name):
            at, width = CONST_AT[name]
            return consts[:, at:at + width]

        ident = const("ident")
        upto = const("upto").rearrange("p (b t) -> p b t", b=TB)
        reach_of = {n: const(n).rearrange("p (b t) -> p b t", b=TB) for n in ("dsa_reach", "swa_reach", "causal")}
        small_at = [0]

        def row_of(r, rows):
            return ident[0:rows, r:r + 1].to_broadcast([rows, P])

        def stat(*shape):
            width = int(np.prod(shape))
            if small_at[0] + width > SMALL:
                small_at[0] = 0
            small_at[0] += width
            return shaped(small[:, small_at[0] - width:small_at[0]], *shape)

        pe = Lane(nc.tensor, sem("pe_done"), False)
        vec = Lane(nc.vector, sem("vec_done"), True)
        act = Lane(nc.scalar, sem("act_done"), True)
        pool = Lane(nc.gpsimd, sem("pool_done"), True)
        sp = Lane(nc.sync, sem("sp_done"), False)
        const_loads = Loads(sem("consts_in"))
        param_loads = Loads(sem("params_in"))
        x_loads = Loads(sem("x_in"))
        router_loads = Loads(sem("router_in"))
        position_loads = Loads(sem("positions_in"))
        mem_loads = Loads(sem("mem_in"))
        bias_loads = Loads(sem("bias_row_in"))
        band_loads = Loads(sem("band_in"))
        norm_loads = Loads(sem("norm_rows_in"))
        stores = Loads(sem("out_stored"))

        for b in range(TB):
            x_in = x_loads.start(nc.sync, x[:, b, :], t["x"][0, b * P:(b + 1) * P, :])
        consts_in = const_loads.start(nc.scalar, consts[:, :], t["shape_consts"])
        banks = Banks([psum[:, 4 + i, :] for i in range(4)])
        held = psum[:, 0:4, :].rearrange("p (b h) n -> p b (h n)", b=TB)
        held_free = [None]
        weights = WeightRing(sp, act, vec, slots_of_ring, [sem(f"ring_in{i}") for i in range(RING)],
                             weight_plan(t, first_layers, second_layers), rounded)

        def param(dst, src):
            return param_loads.start(nc.gpsimd, dst, src)

        def load_layer_inputs(l, experts_done, norm_done):
            pool.after(experts_done)
            bias = bias_loads.start(nc.gpsimd, bias_row, t["b_in"][l:l + 1, 0:C_MQ])
            mem = mem_loads.start(nc.gpsimd, mem_rows, t["mem"][0].rearrange("(b p) n -> p b n", p=P))
            pool.after(norm_done)
            band_loads.start(nc.gpsimd, band, t["pool_band"])
            band_in = band_loads.start(nc.gpsimd, pool_w, t["pool_w"][l].rearrange("g c e -> c g e"))
            return bias, band_in, mem

        def load_params():
            param(router_b[:, :], t["router_bias"].partition_broadcast(P))
            for l in range(DEPTH):
                param(bias_cols[:, l, :], t["b_in"][l, C_MQ:D_IN].rearrange("(c p) -> p c", p=P))
                param(pool_scale[:, l, :], t["pool_scale"][l].rearrange("(c p) -> p c", p=P))
                for i, name in enumerate(("norm1_2", "norm2_2")):
                    param(rms_cols[:, l, i, :], t[name][l].rearrange("(c p) -> p c", p=P))
                for i, name in enumerate(("swa_q_norm_2", "swa_k_norm_2", "fox_q_norm_2", "fox_k_norm_2")):
                    param(head_gain[:, l, i, :], t[name][l].partition_broadcast(P))
                param(mlstm_gain[:, l, :], t["mlstm_out_norm_2"][l].rearrange("h d -> (h d)").partition_broadcast(P))
                param(sinks[:, l, :], t["swa_sinks_2"][l].partition_broadcast(P))
                for i, name in enumerate(("fox_f_bias_2", "mlstm_f_bias_2", "mlstm_i_bias_2")):
                    last = param(gate_bias[:, l, 4 * i:4 * i + 4], t[name][l].partition_broadcast(P))
            return last

        def load_norm_rows(gain, shift, *free):
            pool.after(*free)
            norm_loads.start(nc.gpsimd, norm_rows[:, 0, :], gain.partition_broadcast(P))
            return norm_loads.start(nc.gpsimd, norm_rows[:, 1, :], shift.partition_broadcast(P))

        def matmul(dst, lhsT, rhs, first, last):
            return pe.engine.matmul(dst, lhsT, rhs, start=first, stop=last, skip_group_check=True)

        def product3(dst, lhsT, rhs, first, last):
            if len(lhsT) == 2 and len(rhs) == 2:
                (a, da), (b, db) = ([rounded(p) for p in o] for o in (lhsT, rhs))
                matmul(dst, a, db, first, False)
                matmul(dst, da, b, False, False)
                return matmul(dst, a, b, False, last)
            lhsT, rhs = ([reread(p) for p in o] if len(o) == 2 else o for o in (lhsT, rhs))
            pairs = [(a, b) for a in lhsT for b in rhs]
            for n, (a, b) in enumerate(pairs):
                ins = matmul(dst, a, b, first and n == 0, last and n == len(pairs) - 1)
            return ins

        def act_copy(dst, src, *tokens):
            return act.done(act.beside(*tokens).activation(dst, src, ACT.Copy))

        def vec_copy(dst, src, *tokens):
            return vec.done((vec.beside if tokens else vec.after)(*tokens).tensor_copy(dst, src))

        def split(dst, c, src, ready):
            hi, lo = (p[:, c, :] for p in dst)
            hi_in = act.done(act.beside(ready).activation(rounded(hi), src, ACT.Copy))
            return vec.done(vec.beside(hi_in).tensor_tensor(rounded(lo), src, reread(hi), ALU.subtract))

        def turn(src, width, dst, ready, scale_col=None):
            for c in range(0, width // P, 2):
                n = min(2, width // P - c)
                i, bank, free = banks.take()
                pe.after(ready[c // 4] if isinstance(ready, list) else ready, free)
                for j in range(n):
                    for b in range(TB):
                        last = pe.engine.transpose(bank[:, j * S + b * P:j * S + (b + 1) * P],
                                                   src[:, b, (c + j) * P:(c + j + 1) * P], ident)
                turned_in = pe.done(last)
                if not isinstance(dst, list):
                    tok = act_copy(dst[:, c:c + n, :], bank[:, 0:n * S].rearrange("p (c t) -> p c t", c=n), turned_in)
                elif scale_col is None:
                    tok = split(dst, slice(c, c + n), bank[:, 0:n * S].rearrange("p (c t) -> p c t", c=n), turned_in)
                else:
                    for j in range(n):
                        hi_in = act.done(act.beside(turned_in).activation(
                            rounded(dst[0][:, c + j, :]), bank[:, j * S:(j + 1) * S], ACT.Copy,
                            scale=scale_col[:, c + j:c + j + 1]))
                    for j in range(n):
                        tok = vec.done(vec.beside(hi_in).scalar_tensor_tensor(
                            rounded(dst[1][:, c + j, :]), bank[:, j * S:(j + 1) * S], scale_col[:, c + j:c + j + 1],
                            reread(dst[0][:, c + j, :]), ALU.mult, ALU.subtract))
                banks.free[i] = tok
            return tok

        def turn_blocks(src, dst, ready):
            for b in range(TB):
                for c in range(0, KC, 4):
                    i, bank, free = banks.take()
                    pe.after(ready[b], free)
                    for j in range(4):
                        last = pe.engine.transpose(bank[:, j * P:(j + 1) * P], src[:, b, (c + j) * P:(c + j + 1) * P], ident)
                    hi, lo = (part_[:, c:c + 4, b * P:(b + 1) * P] for part_ in dst)
                    rows = bank.rearrange("p (c t) -> p c t", c=4)
                    hi_in = act.done(act.beside(pe.done(last)).activation(rounded(hi), rows, ACT.Copy))
                    banks.free[i] = tok = vec.done(vec.beside(hi_in).tensor_tensor(rounded(lo), rows, reread(hi), ALU.subtract))
            return tok

        def rows_product(lhs, n, emit, ready, bias=None):
            taken = [banks.take() for _ in range(TB)]
            for half in range(2):
                piece = weights.take()
                for b, (i, bank, free) in enumerate(taken):
                    pe.after(ready, free, *piece.ready)
                    for c in range(KC // 2):
                        k = half * KC // 2 + c
                        last = product3(bank[:, 0:n], [a[:, k, b * P:(b + 1) * P] for a in lhs],
                                        [w[:, c, :] for w in piece.parts], k == 0, k == KC - 1 and bias is None)
                    if half and bias is not None:
                        last = matmul(bank[:, 0:n], upto[0:1, 0, P:S], bias, False, True)
                    if b == TB - 1:
                        done = pe.done(last)
                        weights.release(piece, done)
                    elif half:
                        first_done = pe.done(last)
                if half:
                    tok = []
                    for b, (i, bank, free) in enumerate(taken):
                        banks.free[i] = emit(b, bank[:, 0:n], (first_done, done)[b])
                        tok.append(banks.free[i])
            return tok[-1]

        def cols_product(piece, cols, rhs, ready):
            i, bank, free = banks.take()
            pe.after(ready, free, *piece.ready)
            chunks = piece.raw.shape[1]
            for c in range(chunks):
                last = product3(bank[:, 0:S], [w[:, c, cols:cols + P] for w in piece.parts], [r[:, c, :] for r in rhs],
                                c == 0, c == chunks - 1)
            return i, bank[:, 0:S], pe.done(last)

        def held_product(lhs, ready):
            made = [[None] * TB for _ in range(2)]
            for half in range(2):
                for part_ in range(2):
                    piece = weights.take()
                    pe.after(held_free[0], *piece.ready)
                    for b in range(TB):
                        for c in range(KC // 2):
                            k = part_ * KC // 2 + c
                            pe.after(ready[k // 2])
                            last = product3(held[:, b, half * BANK:(half + 1) * BANK],
                                            [a[:, k, b * P:(b + 1) * P] for a in lhs], [w[:, c, :] for w in piece.parts],
                                            k == 0, k == KC - 1)
                        made[half][b] = pe.done(last)
                    weights.release(piece, made[half][TB - 1])
            return made

        def split_into_xT(src, *ready):
            act.beside(*ready)
            return [split(xT, slice(c, c + 2), src[:, c:c + 2, :], ready[0]) for c in range(0, KC, 2)]

        def softmax(scores, tops, heads, keys, sink, exp_scale):
            if sink is not None:
                vec.done(vec.after().tensor_tensor(tops, tops, sink, ALU.max))
            minus = stat(heads)
            sums = stat(heads)
            lowered = vec.done(vec.after().tensor_scalar(minus, tops, -exp_scale, None, ALU.mult))
            for h in range(heads):
                summed = act.done(act.beside(lowered).activation(
                    scores[:, h, 0:keys], scores[:, h, 0:keys], ACT.Exp, bias=minus[:, h:h + 1], scale=exp_scale,
                    accum_out=sums[:, h:h + 1]))
            if sink is not None:
                extra = stat(heads)
                more = vec.done(vec.after().tensor_tensor(extra, sink, minus, ALU.add))
                summed = act.done(act.beside(more).activation(extra, extra, ACT.Exp))
            yield
            if sink is not None:
                vec.done(vec.after(summed).tensor_tensor(sums, sums, extra, ALU.add))
            share = stat(heads)
            vec.done(vec.after(summed).reciprocal(share, sums))
            for h in range(heads):
                tok = vec.done((vec.beside if h else vec.after)().tensor_scalar(
                    scores[:, h, 0:keys], scores[:, h, 0:keys], share[:, h:h + 1], None, ALU.mult))
            return tok

        def turn_probs(scores, dst, heads, key_blocks, ready):
            pairs = [(h, kb) for h in range(heads) for kb in range(key_blocks)]
            for n in range(0, len(pairs), 4):
                i, bank, free = banks.take()
                pe.after(ready, free)
                for j, (h, kb) in enumerate(pairs[n:n + 4]):
                    last = pe.engine.transpose(bank[:, j * P:(j + 1) * P], scores[:, h, kb * P:(kb + 1) * P], ident)
                turned_in = pe.done(last)
                h0, count = pairs[n][0], 4 // key_blocks
                tok = act_copy(dst(h0, count)[:, :, 0:key_blocks * P],
                               bank[:, :].rearrange("p (h k) -> p h k", h=count), turned_in)
                banks.free[i] = tok
            return tok

        def head_values(pair, key_blocks, values, turned_probs, dst, ready):
            i, bank, free = banks.take()
            pe.after(ready, free)
            for j in range(2):
                h = 2 * pair + j
                for kb in range(key_blocks):
                    last = matmul(bank[j * HD:(j + 1) * HD, 0:P], values(h, kb), turned_probs(h, 1)[:, 0, kb * P:(kb + 1) * P],
                                  kb == 0, kb == key_blocks - 1)
            tok = act_copy(dst, bank[:, 0:P], pe.done(last))
            banks.free[i] = tok
            return tok

        def layer_norm(made, norm_in):
            stats, moments, root, minus = stat(TB, 2, 6), stat(TB, 2), stat(TB), stat(TB)
            for half in range(2):
                cols = slice(half * BANK, (half + 1) * BANK)
                for b in range(TB):
                    held_free[0] = vec.done(vec.beside(made[half][b]).scalar_tensor_tensor(
                        x[:, b, cols], x[:, b, cols], DN_ALPHA, held[:, b, cols], ALU.mult, ALU.add))
                    vec.done(vec.after().bn_stats(stats[:, b, half, :], x[:, b, cols]))
            for b in range(TB):
                tok = vec.done(vec.after().bn_aggr(moments[:, b, :], stats[:, b, :, :].rearrange("p k s -> p (k s)")))
            rooted = act.done(act.beside(tok).activation(root, moments[:, :, 1], ACT.Sqrt, bias=const("ln_eps")))
            vec.done(vec.after(rooted).reciprocal(root, root))
            tok = vec.done(vec.after().scalar_tensor_tensor(minus, moments[:, :, 0], -1.0, root, ALU.mult, ALU.mult))
            centred = [act.done(act.beside(tok).activation(x[:, b, :], x[:, b, :], ACT.Identity, bias=minus[:, b:b + 1],
                                                           scale=root[:, b:b + 1])) for b in range(TB)]
            normed = []
            for b in range(TB):
                vec.done(vec.beside(centred[b], norm_in).tensor_tensor(x[:, b, :], x[:, b, :], norm_rows[:, 0, :], ALU.mult))
                normed.append(vec.done(vec.after().tensor_tensor(x[:, b, :], x[:, b, :], norm_rows[:, 1, :], ALU.add)))
            return normed

        def rope(src, dst, cos, sin, heads, tmp):
            s, d = (a.rearrange("p (h d) -> p h d", d=HD) for a in (src, dst))
            m = tmp.rearrange("p (h d) -> p h d", d=HD)
            c = cos.unsqueeze(1).to_broadcast([P, heads, HALF])
            n = sin.unsqueeze(1).to_broadcast([P, heads, HALF])
            lo, hi = slice(0, HALF), slice(HALF, HD)
            vec.done(vec.after().tensor_tensor(d[:, :, lo], s[:, :, lo], c, ALU.mult))
            vec.done(vec.beside().tensor_tensor(m[:, :, lo], s[:, :, hi], n, ALU.mult))
            vec.done(vec.beside().tensor_tensor(d[:, :, hi], s[:, :, hi], c, ALU.mult))
            vec.done(vec.beside().tensor_tensor(m[:, :, hi], s[:, :, lo], n, ALU.mult))
            vec.done(vec.after().tensor_tensor(d[:, :, lo], d[:, :, lo], m[:, :, lo], ALU.subtract))
            return vec.done(vec.beside().tensor_tensor(d[:, :, hi], d[:, :, hi], m[:, :, hi], ALU.add))

        def position_angles():
            pos, inv = stat(TB), const("inv_freq")
            work = scratch[:, 0, :]
            vec.done(vec.after(positions_in, consts_in).tensor_copy(pos, positions[:, :]))
            two_pi = 2 * np.pi
            c1 = float(np.float32(6.28125))
            c2 = float(np.float32(np.float64(two_pi - c1) // 2.0 ** -21 * 2.0 ** -21))
            c3 = float(np.float32(two_pi - c1 - c2))
            magic = 1.5 * 2.0 ** 23
            for b in range(TB):
                ang, turns, k, r = (work[:, i * HALF:(i + 1) * HALF] for i in range(4))
                vec.done(vec.after().tensor_scalar(ang, inv, pos[:, b:b + 1], None, ALU.mult))
                for dst, quarter in ((pos_sin, 0.0), (pos_cos, 0.25)):
                    vec.done(vec.after().tensor_scalar(turns, ang, 1.0 / two_pi, quarter, ALU.mult, ALU.add))
                    vec.done(vec.after().tensor_scalar(k, turns, magic, None, ALU.add))
                    vec.done(vec.after().tensor_scalar(k, k, magic, None, ALU.subtract))
                    vec.done(vec.after().scalar_tensor_tensor(r, k, -c1, ang, ALU.mult, ALU.add))
                    vec.done(vec.after().scalar_tensor_tensor(r, k, -c2, r, ALU.mult, ALU.add))
                    vec.done(vec.after().scalar_tensor_tensor(r, k, -c3, r, ALU.mult, ALU.add))
                    if quarter:
                        vec.done(vec.after().tensor_scalar(r, r, float(np.pi / 2), None, ALU.add))
                    tok = vec.done(vec.after().tensor_scalar(r, r, 3.1415925, -3.1415925, ALU.min, ALU.max))
                    tok = act.done(act.after(tok).activation(dst[:, b, :], r, ACT.Sin))
                    vec.after(tok)
            return tok

        def dsa_branch(result):
            vec.after((yield from until("index", result)), result.get("angles"))
            for b in range(TB):
                tok = rope(z[:, b, C_IQ:C_IK], turned[:, b, 0:512], pos_cos[:, b, :], pos_sin[:, b, :], 8, scratch[:, b, 0:512])
            yield
            vec.after(turn(turned, 512, iqT, tok))
            for b in range(TB):
                rope(z[:, b, C_IK:C_IK + HD], turned[:, b, 0:HD], pos_cos[:, b, :], pos_sin[:, b, :], 1, scratch[:, b, 0:HD])
                tok = vec.done(vec.after().tensor_copy(turned[:, b, HD:2 * HD], turned[:, b, 0:HD]))
            yield
            heads_ready = turn(turned, 2 * HD, ikT.unsqueeze(1), tok)
            vec.after(heads_ready)
            iw = stat(TB, DSA_HEADS)
            vec.done(vec.after().tensor_scalar(iw, z[:, :, C_IW:C_IW + DSA_HEADS], DSA_HEADS ** -0.5, None, ALU.mult))
            for b in range(TB):
                keys = (b + 1) * P
                now, other = scratch[:, 0, 0:keys], scratch[:, 1, 0:keys]
                reach = reach_of["dsa_reach"][:, b, 0:keys]
                related = []
                for h in range(DSA_HEADS):
                    i, bank, free = banks.take()
                    at = HD * (h % 2)
                    pe.after(heads_ready, free)
                    product = pe.done(matmul(bank[:, 0:keys], iqT[at:at + HD, h // 2, b * P:(b + 1) * P],
                                             ikT[at:at + HD, 0:keys], True, True))
                    slot = turned[:, h % 4 // 2, h % 2 * keys:(h % 2 + 1) * keys]
                    read = related[h - 4] if h >= 4 else (vec.sem, vec.count)
                    banks.free[i] = tok = act.done(act.beside(product, read).activation(slot, bank[:, 0:keys], ACT.Relu,
                                                                                        scale=HD ** -0.5))
                    related.append(vec.done(vec.after(tok).scalar_tensor_tensor(
                        now, slot, iw[:, b, h:h + 1], reach if h == 0 else now, ALU.mult, ALU.add)))
                    if h % 4 == 3:
                        yield
                top8 = stat(8)
                for n in range(DSA_TOPK // 8):
                    vec.done(vec.after().max(top8, now))
                    vec.done(vec.after().match_replace(other, top8, now, TAKEN))
                    now, other = other, now
                    if n % 4 == 3:
                        yield
                vec.done(vec.after().tensor_scalar(penalty[:, b, 0:keys], now, TAKEN / 2, OUT_OF_REACH, ALU.is_gt, ALU.mult))
            vec.after((yield from until("heads", result)))
            for src, dst in ((C_Q, qT), (C_K, kT)):
                for b in range(TB):
                    tok = rope(z[:, b, src:src + 512], turned[:, b, 0:512], pos_cos[:, b, :], pos_sin[:, b, :], 8,
                               scratch[:, b, 0:512])
                yield
                heads_ready = turn(turned, 512, dst, tok)
                vec.after(heads_ready)
            done = None
            for b in range(TB):
                keys = (b + 1) * P
                tops = stat(DSA_HEADS)
                vec.after(done)
                for h in range(DSA_HEADS):
                    i, bank, free = banks.take()
                    at = HD * (h % 2)
                    pe.after(heads_ready, free)
                    product = pe.done(matmul(bank[:, 0:keys], qT[at:at + HD, h // 2, b * P:(b + 1) * P],
                                             kT[at:at + HD, h // 2, 0:keys], True, True))
                    banks.free[i] = vec.done((vec.beside if h else vec.after)(product).tensor_tensor_reduce(
                        out=probs[:, h, 0:keys], in0=bank[:, 0:keys], in1=penalty[:, b, 0:keys], scale=1.0, scalar=TAKEN,
                        op0=ALU.add, op1=ALU.max, accum_out=tops[:, h:h + 1]))
                    if h % 4 == 3:
                        yield
                ready = yield from softmax(probs, tops, DSA_HEADS, keys, None, HD ** -0.5)
                yield
                ready = turn_probs(probs, z_probsT, DSA_HEADS, b + 1, ready)
                yield
                for pair in range(DSA_HEADS // 2):
                    done = head_values(pair, b + 1, lambda h, kb: z[:, kb, C_V + h * HD:C_V + (h + 1) * HD], z_probsT,
                                       branchT[:, 4 + pair, b * P:(b + 1) * P], ready)
                yield
            result["dsa"] = done

        def pool_branch(l, ready, band_in):
            mixed = [None, None]
            for g in range(POOL_GROUPS):
                i, bank, free = banks.take()
                pe.after(ready, band_in, free)
                for b in range(TB):
                    last = matmul(bank[:, 0:S], z[:, b, g * P:(g + 1) * P], band[:, g, b, :], b == 0, b == TB - 1)
                differ = upT[g % 2][:, :]
                banks.free[i] = tok = vec_copy(differ, bank[:, 0:S], pe.done(last), mixed[g % 2])
                i, bank, free = banks.take()
                pe.after(tok, free)
                mixed[g % 2] = pe.done(matmul(bank[:, 0:S], pool_w[:, g, :], differ, True, True))
                banks.free[i] = tok = act.done(act.after(mixed[g % 2], params_in).activation(
                    branchT[:, g, :], bank[:, 0:S], ACT.Copy, scale=pool_scale[:, l, g:g + 1]))
                yield
            return tok, mixed

        def weights_work(l, x_ready, bias_in, band_in, mem_in, result):
            for name, cuts in FIRST_CUTS:
                for a, b_ in cuts:
                    pe.after(bias_in)
                    tok = rows_product(xT, b_ - a, lambda b, bank, product: act_copy(z[:, b, a:b_], bank, product),
                                       x_ready, bias_row[:, a:b_])
                    if l == 0 and "angles" not in result:
                        result["angles"] = position_angles()
                        router_ready.append(split(router_parts, slice(0, KC), router_w[:, :, :], router_in))
                    yield
                result[name] = tok
                if name == "pool":
                    mem_ready = turn(mem_rows, D, memT, mem_in)
                    yield
                    result["pooled"], result["upT"] = yield from pool_branch(l, tok, band_in)
            yield from memory_branch(l, mem_ready, x_ready, result)

        def memory_branch(l, mem_ready, x_ready, result):
            for n in range(2):
                piece = weights.take()
                for j in range(2):
                    h = 2 * n + j
                    i, bank, product = cols_product(piece, j * P, [memT], mem_ready)
                    banks.free[i] = act_copy(mkT[:, h, :], bank, product)
                weights.release(piece, product)
                yield
            kv_ready = rows_product([memT], BRANCH, lambda b, bank, product: act_copy(mv[:, b, :], bank, product), mem_ready)
            vec.after(kv_ready)
            yield
            yield from merge(l, 0, result["pooled"], True, result)
            for n in range(2):
                piece = weights.take()
                for j in range(2):
                    h = 2 * n + j
                    i, bank, product = cols_product(piece, j * P, xT, x_ready)
                    mq_ready = act.done(act.beside(product).activation(mqT[:, h, :], bank, ACT.Identity,
                                                                     bias=bias_cols[:, l, h:h + 1]))
                    banks.free[i] = mq_ready
                weights.release(piece, product)
                yield
            done = None
            for b in range(TB):
                tops = stat(MEM_HEADS)
                vec.after(done)
                for h in range(MEM_HEADS):
                    i, bank, free = banks.take()
                    pe.after(mq_ready, kv_ready, free)
                    product = pe.done(matmul(bank[:, 0:N_MEM], mqT[:, h, b * P:(b + 1) * P], mkT[:, h, :], True, True))
                    vec.done(vec.after(product).reduce_max(tops[:, h:h + 1], bank[:, 0:N_MEM], AX.X))
                    banks.free[i] = vec_copy(mem_probs[:, h, :], bank[:, 0:N_MEM])
                yield
                tok = yield from softmax(mem_probs, tops, MEM_HEADS, N_MEM, None, P ** -0.5)
                yield
                tok = turn_probs(mem_probs, lambda h, n: mem_probsT[:, h:h + n, :], MEM_HEADS, TB, tok)
                yield
                for h in range(MEM_HEADS):
                    i, bank, free = banks.take()
                    pe.after(tok, free)
                    for kb in range(TB):
                        last = matmul(bank[:, 0:P], mv[:, kb, h * P:(h + 1) * P], mem_probsT[:, h, kb * P:(kb + 1) * P],
                                      kb == 0, kb == 1)
                    done = act_copy(branchT[:, 8 + h, b * P:(b + 1) * P], bank[:, 0:P], pe.done(last))
                    banks.free[i] = done
                yield
            result["remembered"] = done
            yield from merge(l, 2, done, False, result)

        def merge(l, n, branch_ready, first, result):
            for half in range(2):
                gates = [weights.take() for _ in range(2)]
                projection = weights.take()
                for c in range(4):
                    dc = half * 4 + c
                    ig, gate_bank, gate_product = cols_product(gates[c // 2], c % 2 * P, xT, result["xT"])
                    if c % 2:
                        weights.release(gates[c // 2], gate_product)
                    ib, bank, product = cols_product(projection, c * P, [branchT[:, 4 * n:4 * n + 4, :]], branch_ready)
                    gate = upT[dc % 2]
                    opened_in = act.done(act.beside(gate_product, result["upT"][dc % 2]).activation(
                        gate[:, :], gate_bank, ACT.Sigmoid, bias=bias_cols[:, l, 4 + n * KC + dc:5 + n * KC + dc]))
                    banks.free[ig] = opened_in
                    target = mergedT[:, dc, :] if first else gate[:, :]
                    banks.free[ib] = merged = vec.done(vec.beside(opened_in, product).tensor_tensor(
                        target, gate[:, :], bank, ALU.mult))
                    if not first:
                        merged = vec.done(vec.after().tensor_tensor(mergedT[:, dc, :], mergedT[:, dc, :], target, ALU.add))
                    result["upT"][dc % 2] = merged
                    if c < 3:
                        yield
                weights.release(projection, product)
                yield
            result["merged"] = merged

        def route(gates_w, slots, ready):
            E = N_EXPERTS
            scores, biased, mask, ordered, first = (stat(TB, E) for _ in range(5))
            i, bank, free = banks.take()
            pe.after(ready, free, *router_ready)
            for c in range(KC):
                last = product3(bank[0:E, 0:S], [w[:, c, :] for w in router_parts], [a[:, c, :] for a in xT],
                                c == 0, c == KC - 1)
            banks.free[i] = tok = act.done(act.beside(pe.done(last)).activation(late_gatesT, bank[0:E, 0:S], ACT.Sigmoid))
            i, bank, free = banks.take()
            pe.after(tok, free)
            for b in range(TB):
                last = pe.engine.transpose(bank[:, b * E:(b + 1) * E], late_gatesT[:, b * P:(b + 1) * P], ident[0:E, 0:E])
            banks.free[i] = tok = vec_copy(scores.rearrange("p b e -> p (b e)"), bank[:, 0:TB * E], pe.done(last))
            bc = [P, TB, E]
            vec.done(vec.after().tensor_tensor(biased, scores, router_b[:, :].unsqueeze(1).to_broadcast(bc), ALU.add))
            pairs = stat(TB * N_GROUPS, 6)
            grouped = biased.rearrange("p b (g k) -> p (b g) k", k=PER_GROUP)
            vec.done(vec.after().tensor_tensor(pairs[:, :, 0:3], grouped[:, :, 0:3], grouped[:, :, 1:4], ALU.add))
            vec.done(vec.after().tensor_tensor(pairs[:, :, 3:5], grouped[:, :, 0:2], grouped[:, :, 2:4], ALU.add))
            vec.done(vec.after().tensor_tensor(pairs[:, :, 5:6], grouped[:, :, 0:1], grouped[:, :, 3:4], ALU.add))
            best = stat(TB, N_GROUPS)
            top, top_g = stat(TB), stat(TB)
            vec.done(vec.after().reduce_max(best.rearrange("p b g -> p (b g)"), pairs, AX.X))

            def first_of(values, width, hot):
                row = [P, TB, width]
                steps = const("descend")[:, E - width:E].unsqueeze(1).to_broadcast(row)
                vec.done(vec.after().reduce_max(top, values, AX.X))
                vec.done(vec.after().tensor_tensor(hot, values, top.unsqueeze(2).to_broadcast(row), ALU.is_equal))
                vec.done(vec.after().tensor_tensor(hot, hot, steps, ALU.mult))
                vec.done(vec.after().reduce_max(top_g, hot, AX.X))
                vec.done(vec.after().tensor_tensor(hot, steps, top_g.unsqueeze(2).to_broadcast(row), ALU.is_equal))

            chosen = stat(TB, N_GROUPS)
            first_of(best, N_GROUPS, chosen)
            vec.done(vec.after().tensor_scalar(chosen, chosen, 1.0, -OUT_OF_REACH, ALU.subtract, ALU.mult))
            vec.done(vec.after().tensor_tensor(
                grouped, grouped, chosen.rearrange("p b g -> p (b g)").unsqueeze(2).to_broadcast([P, TB * N_GROUPS, PER_GROUP]),
                ALU.add))
            first_of(biased, E, first)
            vec.done(vec.after().scalar_tensor_tensor(biased, first, TAKEN, biased, ALU.mult, ALU.add))
            first_of(biased, E, mask)
            tok = vec.done(vec.after().tensor_tensor(mask, mask, first, ALU.add))
            i, bank, free = banks.take()
            pe.after(tok, free)
            for b in range(TB):
                for sb_ in range(b + 1):
                    last = matmul(bank[:, b * E:(b + 1) * E], upto[:, sb_, b * P:(b + 1) * P], mask[:, sb_, :], sb_ == 0, sb_ == b)
            counted = pe.done(last)
            vec.done(vec.after().tensor_tensor(ordered, scores, mask, ALU.mult))
            vec.done(vec.after().reduce_sum(top, ordered, AX.X))
            vec.done(vec.after().reciprocal(top, top))
            vec.done(vec.after().tensor_tensor(gates_w, ordered, top.unsqueeze(2).to_broadcast(bc), ALU.mult))
            banks.free[i] = vec.done(vec.after(counted).tensor_tensor(
                slots, bank[:, 0:TB * E].rearrange("p (b e) -> p b e", b=TB), mask, ALU.mult))
            return vec.done(vec.after().tensor_scalar(slots, slots, -1.0, None, ALU.add))

        def expert_layer(l, ready):
            E = N_EXPERTS
            gates_w, slots = routed[:, 0, :, :], routed[:, 1, :, :]
            tok = route(gates_w, slots, ready)
            for b in range(TB):
                tok = vec.done(vec.after(tok).tensor_tensor(
                    sel[:, b, :, :], const("slot").unsqueeze(1).to_broadcast([P, E, SLOTS]),
                    slots[:, b, :].unsqueeze(2).to_broadcast([P, E, SLOTS]), ALU.is_equal))
            selected = tok
            flat = sel.rearrange("p b e s -> p b (e s)")

            def dispatch(quarter):
                dst = tokensT[quarter % 2]
                for c in range(0, KC, 2):
                    i, bank, free = banks.take()
                    pe.after(ready, selected, free)
                    for j in range(2):
                        for b in range(TB):
                            last = matmul(bank[:, j * S:(j + 1) * S], x[:, b, (c + j) * P:(c + j + 1) * P],
                                          flat[:, b, quarter * S:(quarter + 1) * S], b == 0, b == TB - 1)
                    banks.free[i] = tok = act_copy(dst[:, c:c + 2, :], bank[:, :].rearrange("p (c t) -> p c t", c=2),
                                                   pe.done(last))
                return tok

            def up(pair, src, src_in):
                projected = []
                for _ in ("w1", "w3"):
                    i, bank, free = banks.take()
                    for half in range(2):
                        taken = [weights.take() for _ in range(2)]
                        pe.after(free, src_in, *taken[0].ready, *taken[1].ready)
                        for c in range(KC // 2):
                            for j in range(2):
                                at, k = (2 * (pair % 2) + j) * SLOTS, half * KC // 2 + c
                                last = matmul(bank[j * SLOTS:(j + 1) * SLOTS, :], src[:, k, at:at + SLOTS],
                                              taken[j].raw[:, c, :], k == 0, k == KC - 1)
                        product = pe.done(last)
                        for piece in taken:
                            weights.release(piece, product)
                    projected.append((i, bank, product))
                (ia, a, a_in), (ib, g, g_in) = projected
                sig, rows = opened[pair % 2], hidden_rows[pair % 2]
                tok = act.done(act.after(a_in, read_sig[pair % 2]).activation(sig, a, ACT.Sigmoid))
                banks.free[ia] = read_sig[pair % 2] = vec.done(vec.after(tok).tensor_tensor(rows, sig, a, ALU.mult))
                banks.free[ib] = tok = vec.done(vec.after(g_in).tensor_tensor(rows, rows, g, ALU.mult))
                return tok

            def down(pair, rows_in):
                rows, rowsT, sT, y = hidden_rows[pair % 2], expertT[pair % 2], selT[pair % 2], expert_out[pair % 2]
                i, bank, free = banks.take()
                pe.after(selected, free)
                for b in range(TB):
                    last = pe.engine.transpose(bank[:, b * P:(b + 1) * P], flat[:, b, pair * P:(pair + 1) * P], ident)
                banks.free[i] = spread = act_copy(sT.rearrange("p b t -> p (b t)"), bank[:, 0:S], pe.done(last))
                i, bank, free = banks.take()
                pe.after(rows_in, free)
                for f in range(4):
                    last = pe.engine.transpose(bank[:, f * P:(f + 1) * P], rows[:, f * P:(f + 1) * P], ident)
                banks.free[i] = tok = act_copy(rowsT.rearrange("p f s -> p (f s)"), bank, pe.done(last))
                for half in range(2):
                    taken = [weights.take() for _ in range(2)]
                    i, bank, free = banks.take()
                    pe.after(tok, free, *taken[0].ready, *taken[1].ready)
                    for f in range(4):
                        for j in range(2):
                            last = matmul(bank[j * SLOTS:(j + 1) * SLOTS, :], rowsT[:, f, j * SLOTS:(j + 1) * SLOTS],
                                          taken[j].raw[:, f, :], f == 0, f == 3)
                    product = pe.done(last)
                    for piece in taken:
                        weights.release(piece, product)
                    banks.free[i] = gated = vec.done(vec.after(product).tensor_scalar(
                        y[:, half * BANK:(half + 1) * BANK], bank, slot_gate[:, pair:pair + 1], None, ALU.mult))
                return spread, gated

            def gather(pair, spread, gated):
                sT, y = selT[pair % 2], expert_out[pair % 2]
                pe.after(gated, spread, held_free[0])
                return [[pe.done(matmul(held[:, b, half * BANK:(half + 1) * BANK], sT[:, b, :],
                                        y[:, half * BANK:(half + 1) * BANK], pair == 0, pair == PAIRS - 1))
                         for b in range(TB)] for half in range(2)]

            read_sig = [None, None]
            rows_in = {}
            src_in = dispatch(0)
            for pair in range(PAIRS + 1):
                if pair < PAIRS:
                    rows_in[pair] = up(pair, tokensT[pair // 2 % 2], src_in)
                if pair == 0:
                    i, bank, free = banks.take()
                    pe.after(selected, free)
                    for n in range(PAIRS):
                        for b in range(TB):
                            last = matmul(bank[:, n * E:(n + 1) * E], flat[:, b, n * P:(n + 1) * P], gates_w[:, b, :],
                                          b == 0, b == TB - 1)
                    gate = pe.done(last)
                    for j in range(2):
                        tok = vec_copy(slot_gate[j * SLOTS:(j + 1) * SLOTS, :], bank[j * SLOTS:(j + 1) * SLOTS, j:PAIRS * E:E + 2], gate)
                    banks.free[i] = tok
                    flag = most_slots(slots, selected)
                if pair:
                    made = down(pair - 1, rows_in[pair - 1])
                    if pair % 2 == 1 and pair < PAIRS - 1:
                        src_in = dispatch((pair + 1) // 2)
                    summed = gather(pair - 1, *made)
            late_tokens(l, gates_w, slots, flag)
            return summed

        def most_slots(slots, ready):
            most = stat(1)
            tok = vec.done(vec.after().reduce_max(most, slots.rearrange("p b e -> p (b e)"), AX.X))
            i, bank, free = banks.take()
            pe.after(tok, free)
            tok = pe.done(pe.engine.transpose(bank[0:1, 0:P], most, ident))
            top = stat(1)[0:1, :]
            banks.free[i] = vec.done(vec.after(tok).reduce_max(top, bank[0:1, 0:P], AX.X))
            return vec.done(vec.after().tensor_scalar(over, top, SLOTS - 0.5, None, ALU.is_gt))

        def late_tokens(l, gates_w, slots, flag):
            entered = [(lane.sem, lane.count) for lane in (pe, vec, act)]
            for lane in (pe, vec, act, pool, sp):
                lane.after(flag)
            more = nc.values_load(over, min_val=0, max_val=1)
            with nc.If(more > 0):
                names = ("pe", "vec", "act", "sp")
                lanes = [Lane(lane.engine, sem(f"late_{name}{l}"), name in ("vec", "act"))
                         for name, lane in zip(names, (pe, vec, act, sp))]
                lpe, lvec, lact, lsp = lanes
                loads = [Loads(sem(f"late_in{l}_{i}")) for i in range(3)]
                for lane in lanes:
                    lane.after(*entered)
                rest = late_rest
                lvec.done(lvec.after().tensor_scalar(rest, slots, SLOTS - 0.5, None, ALU.is_gt))
                tok = lvec.done(lvec.after().tensor_tensor(rest, rest, gates_w, ALU.mult))
                bank = [psum[:, 4 + i, :] for i in range(4)]
                lpe.after(tok)
                for b in range(TB):
                    last = lpe.engine.transpose(bank[0][0:N_EXPERTS, b * P:(b + 1) * P], rest[:, b, :], ident)
                gates_in = lvec.done(lvec.after(lpe.done(last)).tensor_copy(late_gatesT, bank[0][0:N_EXPERTS, 0:S]))
                used = gates_in
                for e in range(N_EXPERTS):
                    lpe.after(gates_in)
                    tok = lpe.done(lpe.engine.matmul(bank[0][:, 0:S], row_of(e, N_EXPERTS), late_gatesT, start=True, stop=True))
                    weight_in = lvec.done(lvec.after(tok).tensor_copy(late_gate, bank[0][:, 0:S]))
                    for f in range(4):
                        cols = slice(f * P, (f + 1) * P)
                        lsp.after(used)
                        w_in = [loads[0].start(nc.sync, late_w[0], by_rows(t["w1"][l, e])[:, :, cols]),
                                loads[1].start(nc.sync, late_w[1], by_rows(t["w3"][l, e])[:, :, cols]),
                                loads[2].start(nc.sync, late_w[2], t["w2"][l, e, cols, :])]
                        for i in range(2):
                            lpe.after(w_in[i], weight_in)
                            for c in range(KC):
                                for k in range(2):
                                    last = lpe.engine.matmul(bank[1 + i][:, 0:S], late_w[i][:, c, :], reread(xT[k][:, c, :]),
                                                             start=(c + k == 0), stop=(c + k == KC))
                            tok = lpe.done(last)
                        tok = lact.done(lact.after(tok, used).activation(late_up[0], bank[1][:, 0:S], ACT.Sigmoid))
                        lvec.done(lvec.after(tok).tensor_tensor(late_up[1], late_up[0], bank[1][:, 0:S], ALU.mult))
                        lvec.done(lvec.after().tensor_tensor(late_up[1], late_up[1], bank[2][:, 0:S], ALU.mult))
                        tok = lvec.done(lvec.after().tensor_tensor(late_up[1], late_up[1], late_gate, ALU.mult))
                        lpe.after(tok, w_in[2])
                        for b in range(TB):
                            for half in range(2):
                                last = lpe.engine.matmul(held[:, b, half * BANK:(half + 1) * BANK],
                                                         late_up[1][:, b * P:(b + 1) * P],
                                                         late_w[2][:, half * BANK:(half + 1) * BANK],
                                                         start=False, stop=False, skip_group_check=True)
                        used = lpe.done(last)
                for engine in (nc.tensor, nc.vector, nc.scalar, nc.gpsimd, nc.sync):
                    engine.wait_ge(used[0], used[1])

        def first_block(l, x_ready, bias_in, band_in, mem_in):
            ready = turn_blocks(x, xT, x_ready)
            result = {"xT": ready}
            together(weights_work(l, ready, bias_in, band_in, mem_in, result), dsa_branch(result))
            norm_in = load_norm_rows(t["ln1_g"][l], t["ln1_b"][l], result["dsa"], result["remembered"])
            together(merge(l, 1, result["dsa"], False, result))
            mixed = held_product(xT, split_into_xT(mergedT, result["merged"], (pe.sem, pe.count)))
            normed = layer_norm(mixed, norm_in)
            norm_in = load_norm_rows(t["ln2_g"][l], t["ln2_b"][l], normed[-1])
            ready = turn_blocks(x, xT, normed)
            summed = expert_layer(l, ready)
            normed = layer_norm(summed, norm_in)
            return normed, load_layer_inputs(l + 1, summed[1][TB - 1], normed[-1]) if l + 1 < first_layers else ()

        def rms_turned(gain, ready):
            sums, share = stat(TB), stat(TB)
            turned_in = turn(x, D, xT, ready, scale_col=gain)
            for b in range(TB):
                tok = act.done(act.beside(*ready).activation(squares[:, b, :], x[:, b, :], ACT.Square,
                                                             accum_out=sums[:, b:b + 1]))
            tok = act.done(act.after().activation(share, sums, ACT.Sqrt, bias=const("rms_eps"), scale=1.0 / D))
            return turned_in, share, vec.done(vec.after(tok).reciprocal(share, share))

        def head_norm(src, dst, heads, gain, scale, sq):
            s, d, m = (a.rearrange("p (h d) -> p h d", d=HD) for a in (src, dst, sq))
            sums, root = stat(heads), stat(heads)
            vec.done(vec.after().tensor_tensor(m, s, s, ALU.mult))
            tok = vec.done(vec.after().reduce_sum(sums, m, AX.X))
            tok = act.done(act.after(tok).activation(root, sums, ACT.Sqrt, bias=const("rms_eps"), scale=1.0 / HD))
            yield
            vec.done(vec.after(tok).reciprocal(root, root))
            vec.done(vec.after().tensor_tensor(d, s, root.unsqueeze(2).to_broadcast([P, heads, HD]), ALU.mult))
            g = gain if len(gain.shape) == 3 else gain.unsqueeze(1).to_broadcast([P, heads, HD])
            return vec.done(vec.after().scalar_tensor_tensor(d, d, scale, g, ALU.mult, ALU.mult))

        def swa_branch(l, result):
            probs, qT, kT, scratch, turned = (swa[n] for n in ("probs", "qT", "kT", "scratch", "turned"))
            vec.after((yield from until("swa", result)))
            cos = const("rope_cos").rearrange("p (b d) -> p b d", b=TB)
            sin = const("rope_sin").rearrange("p (b d) -> p b d", b=TB)
            for b in range(TB):
                zb = z2[:, b, :]
                yield from head_norm(zb[:, C2_AQ:C2_AK], zb[:, C2_AQ:C2_AK], SWA_HEADS, head_gain[:, l, 0, :], HD ** -0.5,
                                     scratch[:, b, 0:512])
                yield from head_norm(zb[:, C2_AK:C2_AV], zb[:, C2_AK:C2_AV], SWA_KV, head_gain[:, l, 1, :], 1.0,
                                     scratch[:, b, 512:640])
                rope(zb[:, 0:C2_AV], turned[:, b, :], cos[:, b, :], sin[:, b, :], SWA_HEADS + SWA_KV, scratch[:, b, :])
                for kv in range(SWA_KV):
                    for j in range(2):
                        at = kv * P + j * HD
                        tok = vec.done(vec.after().tensor_copy(zb[:, C2_AQ + at:C2_AQ + at + HD],
                                                               turned[:, b, 512 + kv * HD:512 + (kv + 1) * HD]))
            yield
            turn(turned, 512, qT, tok)
            heads_ready = turn(z2[:, :, C2_AQ:C2_AQ + 2 * P], 2 * P, kT, tok)
            yield
            done = None
            for b in range(TB):
                keys = (b + 1) * P
                tops = stat(SWA_HEADS)
                vec.after(done)
                for h in range(SWA_HEADS):
                    i, bank, free = banks.take()
                    at = HD * (h % 2)
                    pe.after(heads_ready, free)
                    product = pe.done(matmul(bank[:, 0:keys], qT[at:at + HD, h // 2, b * P:(b + 1) * P],
                                             kT[at:at + HD, h // 4, 0:keys], True, True))
                    banks.free[i] = vec.done((vec.beside if h else vec.after)(product).tensor_tensor_reduce(
                        out=probs[:, h, 0:keys], in0=bank[:, 0:keys], in1=reach_of["swa_reach"][:, b, 0:keys], scale=1.0,
                        scalar=TAKEN, op0=ALU.add, op1=ALU.max, accum_out=tops[:, h:h + 1]))
                    if h % 4 == 3:
                        yield
                ready = yield from softmax(probs, tops, SWA_HEADS, keys, sinks[:, l, :], 1.0)
                yield
                room = lambda h, n: swa["probsT"][:, h:h + n, :]
                ready = turn_probs(probs, room, SWA_HEADS, b + 1, ready)
                yield
                for pair in range(SWA_HEADS // 2):
                    done = head_values(pair, b + 1,
                                       lambda h, kb: z2[:, kb, C2_AV + (h // 4) * HD:C2_AV + (h // 4 + 1) * HD], room,
                                       yT[:, pair, b * P:(b + 1) * P], ready)
                yield

        def decays(l, z_ready):
            pre, low, logs, keys_add = (stat(TB, 8) for _ in range(4))
            sums = decay_sums
            inp = stat(TB, 4)
            vec.after(z_ready)

            def biased(dst, at, i):
                return vec.done(vec.after().tensor_tensor(
                    dst, z2[:, :, at:at + 4], gate_bias[:, l, 4 * i:4 * i + 4].unsqueeze(1).to_broadcast([P, TB, 4]), ALU.add))

            biased(pre[:, :, 0:4], C2_BF, 0)
            biased(pre[:, :, 4:8], C2_CF, 1)
            biased(inp, C2_CI, 2)
            tok = vec.done(vec.after().scalar_tensor_tensor(low, pre, -1.0, pre, ALU.mult, ALU.max))
            act.done(act.after(tok).activation(low, low, ACT.Exp, scale=-1.0))
            tok = act.done(act.after().activation(low, low, ACT.Ln, bias=const("one")))
            tok = vec.done(vec.after(tok).scalar_tensor_tensor(logs, pre, 0.0, low, ALU.min, ALU.subtract))
            i, bank, free = banks.take()
            pe.after(tok, free)
            for b in range(TB):
                for sb_ in range(b + 1):
                    last = matmul(bank[:, b * 8:b * 8 + 8], upto[:, sb_, b * P:(b + 1) * P], logs[:, sb_, :], sb_ == 0, sb_ == b)
            banks.free[i] = vec_copy(sums.rearrange("p b h -> p (b h)"), bank[:, 0:TB * 8], pe.done(last))
            vec.done(vec.after().tensor_scalar(keys_add[:, :, 0:4], sums[:, :, 0:4], -1.0, None, ALU.mult))
            tok = vec.done(vec.after().tensor_tensor(keys_add[:, :, 4:8], inp, sums[:, :, 4:8], ALU.subtract))
            key_rows = upT[0][0:8, :]
            i, bank, free = banks.take()
            pe.after(tok, free)
            for b in range(TB):
                last = pe.engine.transpose(bank[0:8, b * P:(b + 1) * P], keys_add[:, b, :], ident)
            banks.free[i] = tok = vec_copy(key_rows, bank[0:8, 0:S], pe.done(last))
            return sums, key_rows, tok

        def fox_branch(l, result):
            sums, key_rows, rows_ready = yield from until("decays", result)
            probs, qT, kT, scratch, turned = (fox[n] for n in ("probs", "qT", "kT", "scratch", "turned"))
            for b in range(TB):
                zb = z2[:, b, :]
                yield from head_norm(zb[:, C2_BQ:C2_BK], turned[:, b, 0:256], FOX_HEADS, head_gain[:, l, 2, :], HD ** -0.5,
                                     scratch[:, b, 0:256])
                tok = yield from head_norm(zb[:, C2_BK:C2_BV], turned[:, b, 256:512], FOX_HEADS, head_gain[:, l, 3, :], 1.0,
                                           scratch[:, b, 0:256])
            yield
            turn(turned, 256, qT, tok)
            heads_ready = turn(turned[:, :, 256:512], 256, kT, tok)
            yield
            done = None
            for b in range(TB):
                keys = (b + 1) * P
                tops = stat(FOX_HEADS)
                vec.after(done)
                for h in range(FOX_HEADS):
                    i, bank, free = banks.take()
                    at = HD * (h % 2)
                    pe.after(heads_ready, rows_ready, free)
                    matmul(bank[:, 0:keys], qT[at:at + HD, h // 2, b * P:(b + 1) * P], kT[at:at + HD, h // 2, 0:keys],
                           True, False)
                    product = pe.done(matmul(bank[:, 0:keys], row_of(h, 8), key_rows[:, 0:keys], False, True))
                    banks.free[i] = vec.done((vec.beside if h else vec.after)(product).scalar_tensor_tensor(
                        probs[:, h, 0:keys], bank[:, 0:keys], sums[:, b, h:h + 1], reach_of["causal"][:, b, 0:keys],
                        ALU.add, ALU.add))
                yield
                vec.done(vec.after().reduce_max(tops, probs[:, 0:FOX_HEADS, 0:keys], AX.X))
                ready = yield from softmax(probs, tops, FOX_HEADS, keys, None, 1.0)
                yield
                room = lambda h, n: fox["probsT"][:, h:h + n, :]
                ready = turn_probs(probs, room, FOX_HEADS, b + 1, ready)
                yield
                for pair in range(FOX_HEADS // 2):
                    done = head_values(pair, b + 1, lambda h, kb: z2[:, kb, C2_BV + h * HD:C2_BV + (h + 1) * HD], room,
                                       yT[:, 4 + pair, b * P:(b + 1) * P], ready)
                yield

        def mlstm_branch(l, result):
            z_ready = yield from until("rest", result)
            probs, qT, kT, scratch, turned = (mls[n] for n in ("probs", "qT", "kT", "scratch", "turned"))
            turn(z2[:, :, C2_CQ:C2_CK], 256, qT, z_ready)
            heads_ready = turn(z2[:, :, C2_CK:C2_CV], 256, kT, z_ready)
            sums, key_rows, rows_ready = yield from until("decays", result)
            H = MLSTM_HEADS
            for b in range(TB):
                open_in = act.done(act.after(z_ready).activation(scratch[:, b, 256:512], z2[:, b, C2_CO:C2_CO + 256], ACT.Sigmoid))
            yield
            for b in range(TB):
                keys = (b + 1) * P
                tops, minus, dens, floor = stat(H), stat(H), stat(H), stat(H)
                own = sums[:, b, 4:8]
                for h in range(H):
                    i, bank, free = banks.take()
                    pe.after(rows_ready, free)
                    product = pe.done(matmul(bank[:, 0:keys], row_of(4 + h, 8), key_rows[:, 0:keys], True, True))
                    banks.free[i] = vec.done((vec.beside if h else vec.after)(product).scalar_tensor_tensor(
                        probs[:, h, 0:keys], bank[:, 0:keys], own[:, h:h + 1], reach_of["causal"][:, b, 0:keys],
                        ALU.add, ALU.add))
                yield
                vec.done(vec.after().reduce_max(tops, probs[:, 0:H, 0:keys], AX.X))
                vec.done(vec.after().tensor_tensor(tops, tops, own, ALU.max))
                lowered = vec.done(vec.after().tensor_scalar(minus, tops, -1.0, None, ALU.mult))
                for h in range(H):
                    weighed = act.done(act.beside(lowered).activation(probs[:, h, 0:keys], probs[:, h, 0:keys], ACT.Exp,
                                                                     bias=minus[:, h:h + 1]))
                floored = act.done(act.after().activation(floor, minus, ACT.Exp))
                yield
                for h in range(H):
                    i, bank, free = banks.take()
                    at = HD * (h % 2)
                    pe.after(heads_ready, free)
                    product = pe.done(matmul(bank[:, 0:keys], qT[at:at + HD, h // 2, b * P:(b + 1) * P],
                                             kT[at:at + HD, h // 2, 0:keys], True, True))
                    banks.free[i] = tok = vec.done(vec.beside(product, weighed).tensor_tensor_reduce(
                        out=probs[:, h, 0:keys], in0=bank[:, 0:keys], in1=probs[:, h, 0:keys], scale=HD ** -0.5, scalar=0.0,
                        op0=ALU.mult, op1=ALU.add, accum_out=dens[:, h:h + 1]))
                yield
                ready = turn_probs(probs, lambda h, n: mls["probsT"][:, h:h + n, :], H, b + 1, tok)
                vec.done(vec.after().scalar_tensor_tensor(dens, dens, -1.0, dens, ALU.mult, ALU.max))
                vec.done(vec.after(floored).tensor_tensor(dens, dens, floor, ALU.max))
                vec.done(vec.after().reciprocal(dens, dens))
                yield
                i, bank, free = banks.take()
                pe.after(ready, free)
                for h in range(H):
                    for kb in range(b + 1):
                        last = matmul(bank[:, h * HD:(h + 1) * HD], mls["probsT"][:, h, kb * P:(kb + 1) * P],
                                      z2[:, kb, C2_CV + h * HD:C2_CV + (h + 1) * HD], kb == 0, kb == b)
                hc = turned[:, b, 0:256]
                banks.free[i] = vec.done(vec.after(pe.done(last)).tensor_tensor(
                    hc.rearrange("p (h d) -> p h d", d=HD), bank[:, 0:256].rearrange("p (h d) -> p h d", d=HD),
                    dens.unsqueeze(2).to_broadcast([P, H, HD]), ALU.mult))
                yield from head_norm(hc, hc, H, mlstm_gain[:, l, :].rearrange("p (h d) -> p h d", d=HD), 1.0,
                                     scratch[:, b, 0:256])
                tok = vec.done(vec.after(open_in).tensor_tensor(hc, hc, scratch[:, b, 256:512], ALU.mult))
            yield
            turn(turned, 256, yT[:, 6:8, :], tok)

        def second_block(l, x_ready):
            ready, share, shared = rms_turned(rms_cols[:, l, 0, :], x_ready)
            result = {}

            def project():
                for name, cuts in SECOND_CUTS:
                    for a, b_ in cuts:
                        tok = rows_product(xT, b_ - a, lambda b, bank, product: act.done(act.beside(product, shared).activation(
                            z2[:, b, a:b_], bank, ACT.Copy, scale=share[:, b:b + 1])), ready)
                        yield
                    result[name] = tok
                result["decays"] = decays(l, tok)

            together(project(), swa_branch(l, result), fox_branch(l, result), mlstm_branch(l, result))
            made = held_product([yT], [(act.sem, act.count)] * 4)
            added = []
            for half in range(2):
                cols = slice(half * BANK, (half + 1) * BANK)
                for b in range(TB):
                    tok = vec.done(vec.beside(made[half][b]).tensor_tensor(x[:, b, cols], x[:, b, cols], held[:, b, cols], ALU.add))
                added.append(tok)
            held_free[0] = tok
            ready, share, shared = rms_turned(rms_cols[:, l, 1, :], added)
            vec.done(vec.after().tensor_tensor(share, share, share, ALU.mult))
            steps = D_FF // BANK

            def up(j):
                hidden = hiddenT[j % 2]
                for half in range(2):
                    piece = weights.take()
                    for f in (2 * half, 2 * half + 1):
                        i, bank, product = cols_product(piece, f % 2 * P, xT, ready)
                        kept = upT[f % 2]
                        banks.free[i] = tok = act.done(act.beside(product, kept_free[f % 2]).activation(kept[:, :], bank, ACT.Relu))
                        squared = vec.done(vec.beside(tok, down_done[j % 2]).tensor_tensor(kept[:, :], kept[:, :], kept[:, :], ALU.mult))
                        kept_free[f % 2] = made = split(hidden, f, kept[:, :], squared)
                    weights.release(piece, product)
                return made

            def down(j, made):
                hidden = hiddenT[j % 2]
                for half in range(2):
                    piece = weights.take()
                    pe.after(made, held_free[0], *piece.ready)
                    for b in range(TB):
                        for f in range(4):
                            last = product3(held[:, b, half * BANK:(half + 1) * BANK],
                                            [h[:, f, b * P:(b + 1) * P] for h in hidden], [w[:, f, :] for w in piece.parts],
                                            j == 0 and f == 0, j == steps - 1 and f == 3)
                    done = pe.done(last)
                    weights.release(piece, done)
                return done

            down_done, kept_free, made = [None, None], [None, None], {}
            for j in range(steps + 1):
                if j < steps:
                    made[j] = up(j)
                if j:
                    down_done[(j - 1) % 2] = down(j - 1, made[j - 1])
            added = []
            for half in range(2):
                cols = slice(half * BANK, (half + 1) * BANK)
                for b in range(TB):
                    tok = vec.done(vec.beside(down_done[(steps - 1) % 2]).scalar_tensor_tensor(
                        x[:, b, cols], held[:, b, cols], share[:, b:b + 1], x[:, b, cols], ALU.mult, ALU.add))
                added.append(tok)
            held_free[0] = tok
            return added

        routed = sb("routed", 2, TB, N_EXPERTS)
        slot_gate = sb("slot_gate", PAIRS)
        decay_sums = sb("decay_sums", TB, 8)
        positions_in = position_loads.start(nc.gpsimd, positions[:, :], t["positions"][0].rearrange("(b p) -> p b", p=P))
        inputs_in = load_layer_inputs(0, None, None)
        router_in = router_loads.start(nc.gpsimd, router_w[:, :, :], by_rows(t["w_router"]))
        params_in = load_params()
        router_ready = []
        pe.after(consts_in)
        x_ready = [x_in] * TB
        for l in range(first_layers):
            x_ready, inputs_in = first_block(l, x_ready, *inputs_in)
        x_ready = [x_ready[-1]] * 2
        for l in range(second_layers):
            x_ready = second_block(l, x_ready)
        sp.after(*x_ready)
        for b in range(TB):
            stored = stores.start(nc.sync, out[0, b * P:(b + 1) * P, :], x[:, b, :])
        sp.after(stored)


_INPUTS = ("x", "mem", "positions", "w_in", "b_in", "pool_w", "pool_scale", "w_mem_kv", "w_br", "w_out", "ln1_g", "ln1_b",
           "w_router", "router_bias", "w1", "w3", "w2", "ln2_g", "ln2_b", "norm1_2", "w_in_2", "swa_q_norm_2",
           "swa_k_norm_2", "swa_sinks_2", "fox_q_norm_2", "fox_k_norm_2", "fox_f_bias_2", "mlstm_i_bias_2",
           "mlstm_f_bias_2", "mlstm_out_norm_2", "w_out_2", "norm2_2", "w_ff1_2", "w_ff2_2")


def kernel(**inputs):
    import concourse.bacc as bacc
    from concourse.bass_utils import run_bass_kernel_spmd

    nc = bacc.Bacc("TRN2", target_bir_lowering=False, num_devices=1)
    arrays = {f"in_{n}": np.ascontiguousarray(inputs[n]) for n in _INPUTS}
    arrays["in_shape_consts"] = shape_constants()
    arrays["in_pool_band"] = pool_band()
    t = {n[3:]: nc.dram_tensor(n, a.shape, mybir.dt.from_np(a.dtype), kind="ExternalInput").ap() for n, a in arrays.items()}
    out = nc.dram_tensor("out_0", (1, S, D), F32, kind="ExternalOutput").ap()
    build_program(nc, t, out)
    return run_bass_kernel_spmd(nc, [arrays], core_ids=[0]).results[0]["out_0"]
```
